# Optimizing a Trainium2 kernel written in Bass

```python
import math
import jax, jax.numpy as jnp
from jax import lax
import numpy as np

D_MODEL = 1024
BATCH = 1
SEQ = 512
DEPTH = 2
DEC_BATCH = 8
DEC_SEQ = 1
PAST_LEN = 256
PAGE_SIZE = 128

N_A = DEPTH // 2
N_B = DEPTH - N_A
HEAD_DIM = 64
N_HEADS = D_MODEL // (2 * HEAD_DIM)
QK_DIM = N_HEADS * 2 * HEAD_DIM
V_DIM = N_HEADS * 2 * HEAD_DIM
D_FF = ((8 * D_MODEL // 3 + 255) // 256) * 256
CONV_WIDTH = 31
ROPE_THETA = 10000.0
Q_BLOCK = 128
EPS = 1e-6
LAMBDA_STD = 0.1

kernel_name = "yoco_conformer_diffattn_step"

def rms_norm(x, g):
    xf = x.astype(jnp.float32)
    y = xf * lax.rsqrt(jnp.mean(xf * xf, axis=-1, keepdims=True) + EPS)
    return (y * g.astype(jnp.float32)).astype(x.dtype)

def layer_norm(x, g, b):
    xf = x.astype(jnp.float32)
    mu = jnp.mean(xf, axis=-1, keepdims=True)
    xc = xf - mu
    y = xc * lax.rsqrt(jnp.mean(xc * xc, axis=-1, keepdims=True) + EPS)
    return (y * g.astype(jnp.float32) + b.astype(jnp.float32)).astype(x.dtype)

def swiglu_ffn(x, w_in, w_out):
    gate, up = jnp.split(x @ w_in, 2, axis=-1)
    return (jax.nn.silu(gate) * up) @ w_out

def rope(x, pos):
    half = HEAD_DIM // 2
    freqs = ROPE_THETA ** (-jnp.arange(half, dtype=jnp.float32) * 2.0 / HEAD_DIM)
    ang = pos.astype(jnp.float32)[:, None] * freqs[None, :]
    cos = jnp.cos(ang)[None, :, None, None, :]
    sin = jnp.sin(ang)[None, :, None, None, :]
    xf = x.astype(jnp.float32)
    x1, x2 = xf[..., :half], xf[..., half:]
    out = jnp.concatenate([x1 * cos - x2 * sin, x2 * cos + x1 * sin], axis=-1)
    return out.astype(x.dtype)

def conv_module(x_n, prev, w_in, b_in, dw, dw_b, ln_g, ln_b, w_out, b_out):
    a, g = jnp.split(x_n @ w_in + b_in, 2, axis=-1)
    u = a * jax.nn.sigmoid(g)
    full = jnp.concatenate([prev.astype(u.dtype), u], axis=1)
    c = lax.conv_general_dilated(
        full, dw[:, None, :].astype(u.dtype), window_strides=(1,), padding='VALID',
        dimension_numbers=('NWC', 'WIO', 'NWC'), feature_group_count=D_MODEL)
    c = layer_norm(c + dw_b, ln_g, ln_b)
    out = jax.nn.silu(c) @ w_out + b_out
    return out, full[:, -(CONV_WIDTH - 1):]

def diff_attention(q, q_pos, k, v, k_pos, lam):
    b, nq = q.shape[0], q.shape[1]
    blk = Q_BLOCK if nq % Q_BLOCK == 0 else nq
    nb = nq // blk
    qb = q.reshape(b, nb, blk, N_HEADS, 2, HEAD_DIM).transpose(1, 0, 2, 3, 4, 5)
    pb = q_pos.reshape(nb, blk)
    scale = HEAD_DIM ** -0.5

    def one_block(args):
        qi, pi = args
        s = jnp.einsum('bqhcd,bkhcd->bhcqk', qi, k).astype(jnp.float32) * scale
        mask = k_pos[None, :] <= pi[:, None]
        s = jnp.where(mask, s, -jnp.inf)
        p = jax.nn.softmax(s, axis=-1)
        a = p[:, :, 0] - lam * p[:, :, 1]
        return jnp.einsum('bhqk,bkhe->bqhe', a.astype(v.dtype), v)

    o = lax.map(one_block, (qb, pb))
    return o.transpose(1, 0, 2, 3, 4).reshape(b, nq, N_HEADS, 2 * HEAD_DIM)

def setup_inputs(seed: int = 0) -> dict:
    key = jax.random.key(seed)
    ks = jax.random.split(key, 32)
    n_pages = PAST_LEN // PAGE_SIZE
    n_pool = (DEC_BATCH * n_pages * 5) // 4
    f32 = jnp.float32
    nrm = lambda k, shape, s: jax.random.normal(k, shape, f32) * s
    gain = lambda k, shape: 1.0 + 0.02 * jax.random.normal(k, shape, f32)
    page_table = jax.random.permutation(ks[5], n_pool)[:DEC_BATCH * n_pages]
    page_table = page_table.reshape(DEC_BATCH, n_pages).astype(jnp.int32)
    return {
        "x_prompt": nrm(ks[0], (BATCH, SEQ, D_MODEL), 1.0),
        "x_sample": nrm(ks[1], (DEC_BATCH, DEC_SEQ, D_MODEL), 1.0),
        "state_conv": nrm(ks[2], (N_A, DEC_BATCH, CONV_WIDTH - 1, D_MODEL), 0.5),
        "cache_k": nrm(ks[3], (n_pool, PAGE_SIZE, N_HEADS, 2 * HEAD_DIM), 1.0),
        "cache_v": nrm(ks[4], (n_pool, PAGE_SIZE, N_HEADS, 2 * HEAD_DIM), 1.0),
        "page_table": page_table,
        "norm_ffn": gain(ks[6], (DEPTH, 2, D_MODEL)),
        "ffn_w_in": nrm(ks[7], (DEPTH, 2, D_MODEL, 2 * D_FF), D_MODEL ** -0.5),
        "ffn_w_out": nrm(ks[8], (DEPTH, 2, D_FF, D_MODEL), D_FF ** -0.5),
        "norm_mix": gain(ks[9], (DEPTH, D_MODEL)),
        "conv_w_in": nrm(ks[10], (N_A, D_MODEL, 2 * D_MODEL), D_MODEL ** -0.5),
        "conv_b_in": nrm(ks[11], (N_A, 2 * D_MODEL), 0.02),
        "conv_dw": nrm(ks[12], (N_A, CONV_WIDTH, D_MODEL), CONV_WIDTH ** -0.5),
        "conv_dw_b": nrm(ks[13], (N_A, D_MODEL), 0.02),
        "conv_ln_g": gain(ks[14], (N_A, D_MODEL)),
        "conv_ln_b": nrm(ks[15], (N_A, D_MODEL), 0.02),
        "conv_w_out": nrm(ks[16], (N_A, D_MODEL, D_MODEL), D_MODEL ** -0.5),
        "conv_b_out": nrm(ks[17], (N_A, D_MODEL), 0.02),
        "kv_norm": gain(ks[18], (D_MODEL,)),
        "w_kv": nrm(ks[19], (D_MODEL, QK_DIM + V_DIM), D_MODEL ** -0.5),
        "w_q": nrm(ks[20], (N_B, D_MODEL, QK_DIM), D_MODEL ** -0.5),
        "lambda_q1": nrm(ks[21], (N_B, HEAD_DIM), LAMBDA_STD),
        "lambda_k1": nrm(ks[22], (N_B, HEAD_DIM), LAMBDA_STD),
        "lambda_q2": nrm(ks[23], (N_B, HEAD_DIM), LAMBDA_STD),
        "lambda_k2": nrm(ks[24], (N_B, HEAD_DIM), LAMBDA_STD),
        "subln_g": gain(ks[25], (N_B, 2 * HEAD_DIM)),
        "w_o": nrm(ks[26], (N_B, V_DIM, D_MODEL), V_DIM ** -0.5),
        "norm_final": gain(ks[27], (D_MODEL,)),
    }

def reference(x_prompt, x_sample, state_conv, cache_k, cache_v, page_table,
              norm_ffn, ffn_w_in, ffn_w_out, norm_mix,
              conv_w_in, conv_b_in, conv_dw, conv_dw_b, conv_ln_g, conv_ln_b,
              conv_w_out, conv_b_out, kv_norm, w_kv, w_q,
              lambda_q1, lambda_k1, lambda_q2, lambda_k2, subln_g, w_o, norm_final):

    def run(x, pos, conv_prev, past_k, past_v):
        b, s = x.shape[0], x.shape[1]
        conv_states = []
        k_new = v_new = k_all = v_all = k_pos = None
        for l in range(DEPTH):
            if l == N_A:
                kv = rms_norm(x, kv_norm) @ w_kv
                k_new = rope(kv[..., :QK_DIM].reshape(b, s, N_HEADS, 2, HEAD_DIM), pos)
                k_new = k_new.reshape(b, s, N_HEADS, 2 * HEAD_DIM)
                v_new = kv[..., QK_DIM:].reshape(b, s, N_HEADS, 2 * HEAD_DIM)
                if past_k is None:
                    k_all, v_all, k_pos = k_new, v_new, pos
                else:
                    k_all = jnp.concatenate([past_k.astype(k_new.dtype), k_new], axis=1)
                    v_all = jnp.concatenate([past_v.astype(v_new.dtype), v_new], axis=1)
                    k_pos = jnp.arange(k_all.shape[1], dtype=jnp.int32)
                k_all = k_all.reshape(b, -1, N_HEADS, 2, HEAD_DIM)
            x = x + 0.5 * swiglu_ffn(rms_norm(x, norm_ffn[l, 0]), ffn_w_in[l, 0], ffn_w_out[l, 0])
            h = rms_norm(x, norm_mix[l])
            if l < N_A:
                mix, st = conv_module(h, conv_prev[l], conv_w_in[l], conv_b_in[l],
                                      conv_dw[l], conv_dw_b[l], conv_ln_g[l], conv_ln_b[l],
                                      conv_w_out[l], conv_b_out[l])
                conv_states.append(st)
            else:
                j = l - N_A
                lam_init = 0.8 - 0.6 * math.exp(-0.3 * l)
                lam = (jnp.exp(jnp.sum(lambda_q1[j].astype(jnp.float32) * lambda_k1[j].astype(jnp.float32)))
                       - jnp.exp(jnp.sum(lambda_q2[j].astype(jnp.float32) * lambda_k2[j].astype(jnp.float32)))
                       + lam_init)
                q = rope((h @ w_q[j]).reshape(b, s, N_HEADS, 2, HEAD_DIM), pos)
                o = diff_attention(q, pos, k_all, v_all, k_pos, lam)
                o = rms_norm(o, subln_g[j]) * (1.0 - lam_init)
                mix = o.reshape(b, s, V_DIM) @ w_o[j]
            x = x + mix
            x = x + 0.5 * swiglu_ffn(rms_norm(x, norm_ffn[l, 1]), ffn_w_in[l, 1], ffn_w_out[l, 1])
        return rms_norm(x, norm_final), jnp.stack(conv_states, axis=0), k_new, v_new

    pos_p = jnp.arange(x_prompt.shape[1], dtype=jnp.int32)
    prev_p = jnp.zeros((N_A, x_prompt.shape[0], CONV_WIDTH - 1, D_MODEL), x_prompt.dtype)
    y_prompt, conv_p, k_p, v_p = run(x_prompt, pos_p, prev_p, None, None)

    n_dec, past_len = page_table.shape[0], page_table.shape[1] * PAGE_SIZE
    past_k = cache_k[page_table].reshape(n_dec, past_len, N_HEADS, 2 * HEAD_DIM)
    past_v = cache_v[page_table].reshape(n_dec, past_len, N_HEADS, 2 * HEAD_DIM)
    pos_s = past_len + jnp.arange(x_sample.shape[1], dtype=jnp.int32)
    y_sample, conv_s, k_s, v_s = run(x_sample, pos_s, state_conv, past_k, past_v)

    return (y_prompt, y_sample, conv_p, k_p, v_p, conv_s, k_s, v_s)


_drawn_inputs = setup_inputs


def setup_inputs(seed=0):
    import zlib

    import numpy as np

    out = dict(_drawn_inputs(seed))
    spreads = {}
    factors = {'norm_ffn': 3.76,
     'norm_mix': 2.667,
     'conv_b_in': 2.754,
     'conv_ln_g': 3.259,
     'conv_ln_b': 2.867,
     'kv_norm': 2.906,
     'lambda_q1': 4.077,
     'lambda_k1': 6.874,
     'subln_g': 41.346,
     'norm_final': 9.702,
     'conv_b_out': 5.392}
    for name, (base, spread) in spreads.items():
        noise = np.random.default_rng([zlib.crc32(name.encode()), seed]).standard_normal(out[name].shape)
        drawn = base * np.exp(spread * noise) if base else spread * noise
        out[name] = __import__('jax').numpy.asarray(drawn.astype(out[name].dtype))
    for name, factor in factors.items():
        out[name] = (out[name] * factor).astype(out[name].dtype)
    return out
```

```python
import math
from contextlib import ExitStack

import numpy as np

import concourse.bass as bass
from concourse import mybir
from concourse.alu_op_type import AluOpType as ALU

F32 = mybir.dt.float32
F32R = mybir.dt.float32r
BF16 = mybir.dt.bfloat16
I32 = mybir.dt.int32
ACT = mybir.ActivationFunctionType
AX = mybir.AxisListType

P = 128
D = 1024
KD = D // P
SEQ = 512
NS = 8
T = SEQ + NS
HALF = T // 2
FF = 2816
KF = FF // P
HEADS = 8
HD = 64
CW = 31
PAST = 256
PAGE = 128
NPG = PAST // PAGE
NPOOL = NS * NPG * 5 // 4
EPS = 1e-6
SCALE = HD ** -0.5
LAM_INIT = 0.8 - 0.6 * math.exp(-0.3 * 1)
KW = KF // 2
MIX = KF - KD
NEG = -1.0e30

VEC = {}
_at = 0
for _name, _n in (("ffn", 4 * KD), ("mix", 2 * KD), ("kv", KD), ("final", KD), ("b_in", 2 * KD),
                  ("dw", CW * KD), ("dw_b", KD), ("ln_g", KD), ("ln_b", KD), ("b_out", KD), ("sub", 1)):
    VEC[_name] = _at
    _at += _n
NVEC = _at
C_ID, C_ROT, C_MASK, C_PAIR, C_EVEN, C_ODD = 0, P, 2 * P, 3 * P, 3 * P + HD, 3 * P + HD + 1
NCST = C_ODD + 1

DVE_TAPS = 19


class Phase:

    def __init__(self, kind, tiles, chunks, per, weights, j=0):
        self.kind, self.tiles, self.chunks, self.per, self.weights, self.j = kind, tiles, chunks, per, weights, j
        self.groups = chunks // 4
        self.chunk0 = self.unit0 = self.pair0 = self.h0 = self.set = self.next = None


def plan(w_in, w_out, c_in, c_out, w_kv, w_q, w_o):
    def pair(w, half):
        v = w.rearrange("(k p) (a m c) -> a p m k c", p=P, a=2, c=P)
        return lambda g, c: v[(c % 2) ^ half, :, 2 * g + c // 2, :, :]

    def down(w):
        v = w.rearrange("(f k p) (m c) -> f p m k c", f=2, p=P, c=P)
        return lambda g, c: v[c % 2, :, 2 * g + c // 2, :, :]

    def square(w):
        v = w.rearrange("(k p) (m c) -> p m k c", p=P, c=P)
        return lambda g, c: v[:, 4 * g + c, :, :]

    def ffn(j):
        return [Phase("up", KD, 2 * KF, 1, pair(w_in[j // 2, j % 2], 0), j),
                Phase("down", KW, 2 * KD, 2, down(w_out[j // 2, j % 2]), j)]

    phases = (ffn(0) + [Phase("conv_in", KD, 2 * KD, 1, pair(c_in[0], 1)), Phase("conv_out", KD, KD, 1, square(c_out[0]))]
              + ffn(1) + [Phase("k", KD, KD, 1, square(w_kv[:, 0:D])), Phase("v", KD, KD, 1, square(w_kv[:, D:2 * D]))]
              + ffn(2) + [Phase("q", KD, KD, 1, square(w_q[0])), Phase("o", KD, KD, 1, square(w_o[0]))] + ffn(3))
    chunk = unit = pairs = h = sets = 0
    for ph in phases:
        ph.chunk0, ph.unit0, ph.pair0, ph.h0 = chunk, unit, pairs, h
        chunk += ph.chunks
        unit += ph.chunks // ph.per
        pairs += ph.chunks // 2 if ph.kind in ("up", "conv_in") else 0
        h += {"up": KF, "conv_in": KD}.get(ph.kind, 0)
        if ph.kind in ("up", "conv_in", "k", "q"):
            ph.set = sets
            sets += 1
        elif ph.kind == "v":
            ph.set = sets - 1
    for a, b in zip(phases, phases[1:]):
        a.next = b
    return phases


def trunk(nc, xT, vec_d, cst_d, rope_d, lam_d, stateT, state, cache_k, cache_v, pages, w_in, w_out, c_in, c_out,
          w_kv, w_q, w_o, y_d, conv_d, new_state_d, k_d, v_d, vs_d):
    phases = plan(w_in, w_out, c_in, c_out, w_kv, w_q, w_o)
    KIND = {}
    for ph in phases:
        KIND.setdefault(ph.kind, []).append(ph)
    last_phase = phases[-1]

    with ExitStack() as ctx:
        def sb(name, shape, dt=F32):
            return ctx.enter_context(nc.sbuf_tensor(name, shape, dt))

        def sem(name):
            return ctx.enter_context(nc.semaphore(name))

        cursor = [-(-nc.sbuf_base // 32) * 32]
        top = cursor[0]

        def place(name, shape, dt=F32, at=None):
            size = int(np.prod(shape[1:])) * (2 if dt == BF16 else 4)
            if at is None:
                at = cursor[0]
                cursor[0] += -(-size // 32) * 32
            where[name] = (at, at + -(-size // 32) * 32)
            return nc.alloc_sbuf_tensor_at(name, shape, dt, offset=at)

        where = {}
        xg_hi = place("xg_hi", [P, KD, T], F32R)
        xg_lo = place("xg_lo", [P, KD, T], F32R)
        h_hi = place("h_hi", [P, KF, T], F32R)
        h_lo = place("h_lo", [P, KF, T], F32R)
        x = place("x", [P, KD, T])
        raw = place("raw", [P, 4, KW * P])
        w_hi = place("w_hi", [P, 2, KW * P], F32R)
        w_lo = place("w_lo", [P, 2, KW * P], F32R)
        rstd = place("rstd", [P, T])
        acc = place("acc", [P, T])
        sq = place("sq", [P, 2, T])
        t_gate = place("t_gate", [P, 2, T])
        t_act = place("t_act", [P, 2, T])
        t_out = place("t_out", [P, 2, T])
        vec = place("vec", [P, NVEC])
        cst = place("cst", [P, NCST])
        ones_d = place("ones_d", [P, P])
        ident_b = place("ident_b", [P, P], BF16)
        mask_b = place("mask_b", [P, P], BF16)
        v_s = place("v_s", [P, HEADS, NS])
        neglam = place("neglam", [P, 1])
        pairco = place("pairco", [P, 1])
        sub_g = place("sub_g", [P, 1])
        lam_s = place("lam_s", [1, 8])
        pages_s = place("pages_s", [1, NS * NPG], I32)
        mx = place("mx", [P, 2, 2])
        nmx = place("nmx", [P, 2, 2])
        lsum = place("lsum", [P, 2, 2])
        rl = place("rl", [P, 2, 2])
        rl2 = place("rl2", [P, 2])
        mx_s = place("mx_s", [P, 4])
        var = place("var", [P, 6])
        inv = place("inv", [P, 6])
        minus_half = place("minus_half", [P, 6])
        assert cursor[0] <= nc.sbuf_usable_end, cursor[0]
        sb("fence", [P, (cursor[0] - top) // 4])

        XG, HH, HL = where["xg_hi"][0], where["h_hi"][0], where["h_lo"][0]
        room = MIX * T * 4

        def over(base, size, items):
            made, at = [], base
            for name, shape in items:
                made.append(place(name, shape, at=at))
                at = where[name][1]
            assert at <= base + size, (items, at - base - size)
            return made

        lam_row, lam_prod = over(HH, room, [("lam_row", [1, 4, HD]), ("lam_prod", [1, 2, HD])])
        conv, window, conv_p = over(HL, room, [("conv", [P, KD, T]), ("window", [P, KD, NS, CW]), ("conv_p", [P, 2, SEQ])])
        glu, tap, conv_b, swin, tail = over(HH, room, [
            ("glu", [P, 2, CW - 1 + T]), ("tap", [P, 3, SEQ]), ("conv_b", [P, SEQ]), ("swin", [P, NS, CW]),
            ("tail", [P, KD, CW - 1 + NS])])
        k_new, = over(HL, room, [("k_new", [P, KD, T])])
        cs_k, v_tok = over(HH, room, [("cs_k", [P, 2, T]), ("v_tok", [P, KD, SEQ])])
        qT, cs_q, pr = over(HL, room, [("qT", [P, KD, T]), ("cs_q", [P, 2, T]), ("pr", [P, 2, 2, SEQ])])
        kT, at_n, aT, s_dec, p_dec, at_dec, an_dec = over(HH, room, [
            ("kT", [P, KD, T]), ("at_n", [P, 2, SEQ]), ("aT", [P, 2, SEQ]), ("s_dec", [P, NPG, NS, 2 * HEADS]),
            ("p_dec", [P, PAST + 1]), ("at_dec", [P, NPG, NS, HEADS]), ("an_dec", [P, NS, HEADS])])
        vT, page = over(XG, 2 * KD * T * 4, [("vT", [P, SEQ // P, D]), ("page", [P, 4, D])])
        tg0 = where["t_gate"][0]
        qb, kprod = over(tg0, 6 * T * 4, [("qb", [P, 2, D]), ("kprod", [P, D])])
        z_dec, = over(where["sq"][0], 4160, [("z_dec", [P, NS, HEADS, 2])])

        ps_all = ctx.enter_context(nc.psum_tensor("ps_all", [P, 8, 512], F32))
        unit = [ps_all[:, 2 * s:2 * s + 2, 0:HALF] for s in range(2)]
        ps_stat = ps_all[:, 4:6, 0:HALF]
        ps_var = ps_all[:, 4, 0:6]
        ps_rot = ps_all[:, 6:8, 0:HALF]

        def halves(ap):
            return ap.rearrange("p (a b) -> p a b", a=2)

        raw_full = [sem(f"raw_full{s}") for s in range(4)]
        hi_made = sem("hi_made")
        weights_ready = sem("weights_ready")
        chunk_used = sem("chunk_used")
        drained = sem("drained")
        act_done = sem("act_done")
        act_scaled = sem("act_scaled")
        h_hi_made = sem("h_hi_made")
        h_ready = sem("h_ready")
        xg_hi_made = sem("xg_hi_made")
        xg_ready = sem("xg_ready")
        squared = sem("squared")
        summed = sem("summed")
        mean_done = sem("mean_done")
        var_done = sem("var_done")
        var_read = sem("var_read")
        inv_made = sem("inv_made")
        spread_done = sem("spread_done")
        rstd_made = sem("rstd_made")
        inputs = sem("inputs")
        in_state = sem("in_state")
        in_rope = [sem("in_rope_k"), sem("in_rope_q")]
        const_done = sem("const_done")
        lam_step = sem("lam_step")
        rot_done = sem("rot_done")
        cos_done = sem("cos_done")
        sin_done = sem("sin_done")
        rope_done = sem("rope_done")
        v_turned = sem("v_turned")
        v_copied = sem("v_copied")
        vs_copied = sem("vs_copied")
        kv_out = sem("kv_out")
        out_done = sem("out_done")
        glu_done = sem("glu_done")
        tap_made = sem("tap_made")
        tap_added = sem("tap_added")
        tapped = sem("tapped")
        conv_done = sem("conv_done")
        centred = sem("centred")
        ln_scaled = sem("ln_scaled")
        ln_done = sem("ln_done")
        dve_self = sem("dve_self")
        in_kt, in_vt = sem("in_kt"), sem("in_vt")
        page_full = [sem(f"page_full{s}") for s in range(4)]
        v_page_used = sem("v_page_used")
        table_in = sem("table_in")
        scores_done = sem("scores_done")
        max_done = sem("max_done")
        exp_done = sem("exp_done")
        a_done = sem("a_done")
        aT_done = sem("aT_done")
        aT_copied = sem("aT_copied")
        o_done = sem("o_done")
        o_copied = sem("o_copied")
        o_squared = sem("o_squared")
        o_stat, o_var, o_inv, o_spread = sem("o_stat"), sem("o_var"), sem("o_inv"), sem("o_spread")
        o_normed = sem("o_normed")
        o_hi_made = sem("o_hi_made")
        o_lo_made = sem("o_lo_made")
        qb_made = sem("qb_made")
        qb_copied = sem("qb_copied")
        kprod_done = sem("kprod_done")
        kred_done = sem("kred_done")
        d_new, d_scores, d_max, d_exp, d_weights = (sem(n) for n in ("d_new", "d_scores", "d_max", "d_exp", "d_weights"))
        d_turned, d_turned_read, d_out, d_squared, d_stat, d_normed = (
            sem(n) for n in ("d_turned", "d_turned_read", "d_out", "d_squared", "d_stat", "d_normed"))
        d_inv, d_spread = sem("d_inv"), sem("d_spread")
        glu_pad = sem("glu_pad")
        win_done = sem("win_done")
        final_done = sem("final_done")

        N_IN = 16 * (KD + 3)
        N_KV_OUT = 16 * (2 * KD + 1)
        N_OUT = 16 * (KD + 2)
        block = ctx.enter_context(nc.Block())

        def groups(engine, ph, body, first=False, last=False):
            a, b = int(first), ph.groups - int(last)
            if ph.groups <= 2:
                a = b = ph.groups
                for g in range(a):
                    body(g)
                return
            if first:
                body(0)
            with engine.Fori(a, b) as g:
                body(g)
            if last:
                body(ph.groups - 1)

        def wait_then_address(engine, semaphore, value):
            engine.wait_ge(semaphore, value)
            if not isinstance(value, int):
                engine.wait_ge(inputs, N_IN)

        def coming(ph, g, c):
            if c < 2:
                return ph, g, c + 2
            if isinstance(g, int) and g == ph.groups - 1:
                return (ph.next, 0, c - 2) if ph.next else None
            return ph, g + 1, c - 2

        def col(name, i):
            at = VEC[name] + i
            return vec[:, at:at + 1] if isinstance(at, int) else vec[:, bass.ds(at, 1)]

        def at(tensor, m):
            return tensor[:, m, :] if isinstance(m, int) else tensor[:, bass.ds(m, 1), :].rearrange("p a t -> p (a t)")

        def gain(s, k):
            name, i = (("ffn", 0), ("mix", 0), ("ffn", 1), ("kv", 0), ("ffn", 2), ("mix", 1), ("ffn", 3))[s]
            return col(name, KD * i + k)

        SET_AFTER = {("down", 0): 1, ("conv_out", 0): 2, ("down", 1): 3, ("down", 2): 5, ("o", 0): 6, ("down", 3): None}
        SUMS_BEFORE = {("down", 0): KD, ("conv_out", 0): 4 * KD, ("down", 1): 5 * KD, ("down", 2): 6 * KD,
                       ("o", 0): 7 * KD, ("down", 3): 8 * KD}
        SQUARES_BEFORE = {("down", 0): KD, ("conv_out", 0): 3 * KD, ("down", 1): 4 * KD, ("down", 2): 5 * KD,
                          ("o", 0): 6 * KD, ("down", 3): 7 * KD}
        POOL_TAPS = CW - DVE_TAPS
        Q0 = KIND["q"][0].unit0
        K0 = KIND["k"][0].unit0
        V0 = KIND["v"][0].unit0
        STEPS = HEADS * (SEQ // P)

        BLOCKS = tuple(s * HALF + at for s in range(2) for at in (0, P, HALF - P))

        def fresh(ph):
            return ph.kind in ("up", "conv_in", "k", "q") and not (ph.kind == "up" and ph.j == 2)

        @block.sync
        def _(sp):
            for k in range(KD):
                sp.dma_start(x[:, k, :], xT[:, k, :]).then_inc(inputs, 16)
            sp.dma_start(vec[:, :], vec_d).then_inc(inputs, 16)
            sp.dma_start(cst[:, :], cst_d).then_inc(inputs, 16)
            sp.dma_start(lam_row[0:1, :, :], lam_d).then_inc(inputs, 16)

            def load_chunk(ph, g, c):
                n = ph.chunk0 + 4 * g + c
                if not (isinstance(n, int) and n < 4):
                    wait_then_address(sp, weights_ready, n - 3)
                dst = raw[:, c, 0:ph.tiles * P].rearrange("p (k c) -> p k c", c=P)
                sp.dma_start(dst, ph.weights(g, c)).then_inc(raw_full[c], 16)

            def load_page(i, cache):
                if i >= 4:
                    if i < 4 + NS * NPG:
                        sp.wait_ge(kprod_done, i - 3)
                    else:
                        sp.wait_ge(v_page_used, i - 3 - NS * NPG)
                e = i % (NS * NPG)
                pg = sp.value_load(pages_s[0:1, e:e + 1], min_val=0, max_val=NPOOL - 1)
                sp.dma_start(page[:, i % 4, :], cache[bass.ds(pg, 1), :, :].rearrange("a t f -> (a t) f")
                             ).then_inc(page_full[i % 4], 16)

            for ph in phases:
                if ph.kind == "conv_in":
                    sp.wait_ge(chunk_used, ph.chunk0)
                    sp.dma_start(window[:, :, :, 0:CW - 1], stateT).then_inc(in_state, 16)
                if ph.kind == "k":
                    sp.wait_ge(chunk_used, ph.chunk0)
                    sp.dma_start(cs_k[:, :, :], rope_d).then_inc(in_rope[0], 16)
                if ph.kind == "q":
                    for c in range(4):
                        load_chunk(ph, 0, c)
                    sp.wait_ge(chunk_used, ph.chunk0)
                    sp.dma_start(cs_q[:, :, :], rope_d).then_inc(in_rope[1], 16)
                    sp.wait_ge(kv_out, N_KV_OUT)
                    sp.dma_start(kT[:, :, :], k_d).then_inc(in_kt, 16)
                    for c in range(4):
                        load_chunk(ph, 1, c)
                elif ph.kind == "o":
                    for c in range(4):
                        load_chunk(ph, 0, c)
                    sp.wait_ge(chunk_used, ph.chunk0)
                    sp.dma_start(vT[:, :, :], v_d.rearrange("(t p) f -> p t f", p=P)).then_inc(in_vt, 16)
                    sp.dma_start(pages_s[0:1, :], pages).then_inc(table_in, 16)
                    sp.wait_ge(table_in, 16)
                    for i in range(2 * NS * NPG):
                        load_page(i, cache_k if i < NS * NPG else cache_v)
                    for c in range(4):
                        load_chunk(ph, 1, c)
                elif ph.kind == "conv_in":
                    for g in range(ph.groups):
                        for c in range(4):
                            load_chunk(ph, g, c)
                else:
                    groups(sp, ph, lambda g: [load_chunk(ph, g, c) for c in range(4)], first=ph is phases[0])
            sp.wait_ge(kv_out, N_KV_OUT)
            sp.wait_ge(out_done, N_OUT)

        @block.tensor
        def _(pe):
            def chunk(ph, g, c, made=None):
                n = ph.chunk0 + 4 * g + c
                u = ph.unit0 + (4 * g + c if ph.per == 1 else 2 * g + c // 2)
                part = c % ph.per
                slot = c % 2 if ph.per == 1 else c // 2
                pe.wait_ge(weights_ready, n + 1)
                if part == 0 and not (isinstance(u, int) and u < 2):
                    pe.wait_ge(drained, u - 1)
                opening = isinstance(g, int) and g == 0 and c < ph.per and ph.kind != "v"
                for k in range(ph.tiles):
                    if made and k == 2:
                        spread(made)
                    kk = part * ph.tiles + k
                    if ph.kind == "down":
                        hi, lo, need = h_hi[:, kk], h_lo[:, kk], (h_ready, ph.h0 - KF + kk + 1)
                    elif ph.kind == "conv_out":
                        hi, lo, need = h_hi[:, MIX + kk], h_lo[:, MIX + kk], (h_ready, ph.h0 - KD + kk + 1)
                    elif ph.kind == "o":
                        hi, lo, need = h_hi[:, MIX + kk], h_lo[:, MIX + kk], (o_lo_made, HEADS + 1)
                    else:
                        hi, lo, need = xg_hi[:, kk], xg_lo[:, kk], (xg_ready, KD * ph.set + kk + 1)
                    if opening:
                        pe.wait_ge(*need)
                    for i, (w, m) in enumerate(((w_hi, hi), (w_hi, lo), (w_lo, hi))):
                        for s in range(2):
                            mm = nc.tensor.matmul(unit[slot][:, s, :], w[:, c % 2, k * P:(k + 1) * P],
                                                  m[:, s * HALF:(s + 1) * HALF], start=kk == 0 and i == 0,
                                                  stop=kk == ph.per * ph.tiles - 1 and i == 2)
                mm.then_inc(chunk_used, 1)

            def mean(sums, made):
                pe.wait_ge(summed, sums)
                pe.wait_ge(rstd_made, made)
                for s in range(2):
                    mm = nc.tensor.matmul(ps_stat[:, s, :], ones_d[:, :], acc[:, s * HALF:(s + 1) * HALF],
                                          start=True, stop=True)
                mm.then_inc(mean_done, 1)

            def variance(sums, free):
                pe.wait_ge(summed, sums)
                if free:
                    pe.wait_ge(*free)
                for i, b in enumerate(BLOCKS):
                    mm = nc.tensor.matmul(ps_var[:, i:i + 1], acc[:, b:b + P], ones_d[:, 0:1], start=True, stop=True)
                mm.then_inc(var_done, 1)

            def spread(made):
                pe.wait_ge(inv_made, made)
                for i, b in enumerate(BLOCKS):
                    half, at_b = divmod(b, HALF)
                    mm = nc.tensor.matmul(ps_stat[:, half, at_b:at_b + P], inv[:, i:i + 1].broadcast_to([P, P]),
                                          cst[:, C_ID:C_ID + P], start=True, stop=True)
                mm.then_inc(spread_done, 1)

            def rotate(r, u):
                pe.wait_ge(drained, u + 1)
                if r >= 1:
                    pe.wait_ge(sin_done, r)
                for s in range(2):
                    mm = nc.tensor.matmul(ps_rot[:, s, :], cst[:, C_ROT:C_ROT + P],
                                          t_gate[:, r % 2, s * HALF:(s + 1) * HALF], start=True, stop=True)
                mm.then_inc(rot_done, 1)

            def turn_v(m):
                pe.wait_ge(drained, V0 + m + 1)
                if m == 0:
                    pe.wait_ge(sin_done, KD)
                else:
                    pe.wait_ge(v_copied, m)
                for t in range(SEQ // P):
                    mm = nc.tensor.transpose(ps_all[:, 6, t * P:(t + 1) * P], t_gate[:, m % 2, t * P:(t + 1) * P],
                                             cst[:, C_ID:C_ID + P])
                mm.then_inc(v_turned, 1)

            def scores(s):
                h, t = divmod(s, SEQ // P)
                keys = (t + 1) * P
                if s >= 2:
                    pe.wait_ge(exp_done, s - 1)
                for c in range(2):
                    rows = slice(c * HD, (c + 1) * HD)
                    nc.tensor.matmul(ps_all[:, 2 * (s % 2) + c, 0:keys], qT[rows, h, t * P:(t + 1) * P],
                                     kT[rows, h, 0:keys], start=True, stop=False)
                for c in range(2):
                    mm = nc.tensor.matmul(ps_all[:, 2 * (s % 2) + c, keys - P:keys], ident_b[:, :], mask_b[:, :],
                                          start=False, stop=True)
                mm.then_inc(scores_done, 1)

            def turn_a(s):
                pe.wait_ge(a_done, s + 1)
                if s >= 2:
                    pe.wait_ge(aT_copied, s - 1)
                for k in range(s % (SEQ // P) + 1):
                    mm = nc.tensor.transpose(ps_all[:, 4 + s % 2, k * P:(k + 1) * P],
                                             at_n[:, s % 2, k * P:(k + 1) * P], cst[:, C_ID:C_ID + P])
                mm.then_inc(aT_done, 1)

            def values(s):
                h, t = divmod(s, SEQ // P)
                pe.wait_ge(aT_copied, s + 1)
                if t == 0 and h:
                    pe.wait_ge(o_copied, h)
                for k in range(t + 1):
                    mm = nc.tensor.matmul(ps_all[:, 6, t * P:(t + 1) * P], vT[:, k, h * P:(h + 1) * P],
                                          aT[:, s % 2, k * P:(k + 1) * P], start=k == 0, stop=k == t)
                if t == SEQ // P - 1:
                    mm.then_inc(o_done, 1)

            def head_stat(h):
                pe.wait_ge(o_squared, h + 1)
                if h:
                    pe.wait_ge(qb_copied, 2 * h)
                for t in range(SEQ // P):
                    mm = nc.tensor.matmul(ps_all[:, 7, t:t + 1], sq[:, 0, t * P:(t + 1) * P], ones_d[:, 0:1], start=True, stop=True)
                mm.then_inc(o_stat, 1)

            def head_spread(h):
                pe.wait_ge(o_inv, h + 1)
                for t in range(SEQ // P):
                    mm = nc.tensor.matmul(ps_all[:, 7, t * P:(t + 1) * P], inv[:, t:t + 1].broadcast_to([P, P]),
                                          cst[:, C_ID:C_ID + P], start=True, stop=True)
                mm.then_inc(o_spread, 1)

            def spread_q(b, half):
                if half == 0:
                    pe.wait_ge(o_normed, b + 1)
                else:
                    pe.wait_ge(qb_copied, 2 * b + 1)
                for i in range(HEADS // 2):
                    h = HEADS // 2 * half + i
                    mm = nc.tensor.matmul(ps_all[:, 7, i * P:(i + 1) * P],
                                          qT[:, h, SEQ + b:SEQ + b + 1].broadcast_to([P, P]),
                                          cst[:, C_ID:C_ID + P], start=True, stop=True)
                mm.then_inc(qb_made, 1)

            def attention():
                pe.wait_ge(rope_done, 2 * KD)
                pe.wait_ge(drained, Q0 + KD)
                pe.wait_ge(in_kt, 16)
                scores(0)
                for s in range(STEPS + 5):
                    if s + 1 < STEPS:
                        scores(s + 1)
                    if s < STEPS:
                        turn_a(s)
                    if 1 <= s <= STEPS:
                        if s == 1:
                            pe.wait_ge(in_vt, 16)
                        values(s - 1)
                    h, t = divmod(s - 5, 4)
                    if t == 0 and 0 <= h < HEADS:
                        head_stat(h)
                    if t == 1 and 0 <= h < HEADS:
                        head_spread(h)
                    if t == 2 and 0 <= h < HEADS:
                        spread_q(h, 0)
                    if t == 3 and 0 <= h < HEADS:
                        spread_q(h, 1)
                pe.wait_ge(kred_done, NS * NPG)
                pe.wait_ge(d_new, 3)
                for g in range(NPG):
                    nc.tensor.transpose(ps_all[:, 0, g * P:(g + 1) * P], s_dec[:, g].rearrange("p b j -> p (b j)"),
                                        cst[:, C_ID:C_ID + P])
                nc.tensor.matmul(ps_all[:, 0, PAST:PAST + 1], z_dec[:, :, :, :].rearrange("p b h c -> p (b h c)"),
                                 ones_d[:, 0:1], start=True, stop=True).then_inc(d_scores, 1)
                pe.wait_ge(d_weights, 1)
                for g in range(NPG):
                    nc.tensor.matmul(ps_all[:, 1, g * HD:(g + 1) * HD], p_dec[:, g * P:(g + 1) * P],
                                     cst[:, C_PAIR:C_PAIR + HD], start=True, stop=True)
                nc.tensor.matmul(ps_all[:, 1, 2 * HD:3 * HD], p_dec[:, PAST:PAST + 1].broadcast_to([P, P]),
                                 cst[:, C_PAIR:C_PAIR + HD], start=True, stop=True).then_inc(d_turned, 1)
                pe.wait_ge(d_turned_read, 1)
                for b in range(NS):
                    for g in range(NPG):
                        i = NS * NPG + NPG * b + g
                        pe.wait_ge(page_full[i % 4], 16 * (i // 4 + 1))
                    for h in range(HEADS):
                        for g in range(NPG):
                            mm = nc.tensor.matmul(ps_all[:, 2, h * NS + b:h * NS + b + 1],
                                                  page[:, (NPG * b + g) % 4, h * P:(h + 1) * P],
                                                  at_dec[:, g, b, h:h + 1], start=g == 0, stop=g == NPG - 1)
                    mm.then_inc(v_page_used, NPG)
                pe.wait_ge(d_squared, 1)
                nc.tensor.matmul(ps_all[0:HD, 3, 0:1], kprod[:, 2 * HD:3 * HD], ones_d[:, 0:1], start=True, stop=True
                                 ).then_inc(d_stat, 1)
                pe.wait_ge(d_inv, 2)
                nc.tensor.matmul(ps_all[:, 3, 0:HD], inv[0:HD, 0:1].broadcast_to([HD, P]), cst[0:HD, C_ID:C_ID + HD],
                                 start=True, stop=True).then_inc(d_spread, 1)

            pe.wait_ge(inputs, N_IN)
            pe.wait_ge(const_done, 4)
            pe.wait_ge(lam_step, 4)
            nc.tensor.matmul(ps_all[:, 6, 0:1], ones_d[0:1, :], lam_s[0:1, 4:5], start=True, stop=True).then_inc(lam_step, 1)
            sums = 0
            made = 0
            for ph in phases:
                if fresh(ph):
                    sums += KD

                def body(g):
                    for c in range(4):
                        opening = isinstance(g, int) and g == 0
                        chunk(ph, g, c, made + 1 if opening and c == 1 and fresh(ph) else None)
                        r = 4 * g + c - 1
                        if opening and c == 0:
                            if fresh(ph):
                                variance(sums, (rstd_made, made) if made else None)
                        elif ph.kind == "k":
                            rotate(r, K0 + r)
                        elif ph.kind == "q":
                            rotate(KD + r, Q0 + r)
                        elif ph.kind == "v" and r >= 0:
                            turn_v(r)
                groups(pe, ph, body, first=True)
                made += fresh(ph)
                if ph.kind == "k":
                    rotate(KD - 1, K0 + KD - 1)
                elif ph.kind == "v":
                    turn_v(KD - 1)
                elif ph.kind == "q":
                    rotate(2 * KD - 1, Q0 + KD - 1)
                    attention()
                elif ph.kind == "conv_in":
                    mean(sums + KD, made)
                    variance(sums + 2 * KD, (centred, KD))
                    spread(made + 1)
                    sums += 2 * KD
                    made += 1
            variance(sums + KD, (rstd_made, made))
            spread(made + 1)

        @block.scalar
        def _(act):
            squares = [0]

            def round_hi(ph, g, c):
                n = ph.chunk0 + 4 * g + c
                act.wait_ge(raw_full[c], 16 * (ph.chunk0 // 4 + g + 1))
                if not (isinstance(n, int) and n < 2):
                    act.wait_ge(chunk_used, n - 1)
                w = ph.tiles * P
                nc.scalar.activation(w_hi[:, c % 2, 0:w], raw[:, c, 0:w], ACT.Copy).then_inc(hi_made, 1)

            def ahead(ph, g, c):
                to = coming(ph, g, c)
                if to:
                    round_hi(*to)

            def x_hi(s, m):
                nc.scalar.activation(xg_hi[:, m, :], x[:, m, :], ACT.Copy, scale=gain(s, m)).then_inc(xg_hi_made, 1)

            def square(sums, m, src):
                if not (isinstance(sums + m, int) and sums + m < 2):
                    act.wait_ge(summed, sums + m - 1)
                nc.scalar.activation(sq[:, m % 2, :] if isinstance(m, int) else sq_of(m), src, ACT.Square
                                     ).then_inc(squared, 1)

            act.wait_ge(inputs, N_IN)
            nc.scalar.activation(ident_b[:, :], cst[:, C_ID:C_ID + P], ACT.Copy).then_inc(const_done, 1)
            nc.scalar.activation(mask_b[:, :], cst[:, C_MASK:C_MASK + P], ACT.Copy).then_inc(const_done, 1)
            act.wait_ge(lam_step, 2)
            nc.scalar.activation(lam_s[0:1, 2:4], lam_s[0:1, 0:2], ACT.Exp).then_inc(lam_step, 1)
            for m in range(KD):
                x_hi(0, m)
                square(0, m, x[:, m, :])
            round_hi(phases[0], 0, 0)
            round_hi(phases[0], 0, 1)
            act.dma_start(new_state_d, state[:, 1:CW - 1, :]).then_inc(out_done, 16)

            def up(ph):
                def body(g):
                    for q in range(2):
                        u, p = ph.unit0 + 4 * g + 2 * q, ph.pair0 + 2 * g + q
                        ahead(ph, g, 2 * q)
                        act.wait_ge(drained, u + 1)
                        nc.scalar.activation(t_act[:, q, :], t_gate[:, q, :], ACT.Silu).then_inc(act_done, 1)
                        ahead(ph, g, 2 * q + 1)
                        wait_then_address(act, drained, u + 2)
                        if isinstance(g, int) and g == 0 and q == 0 and ph.j in (1, 2):
                            if ph.j == 1:
                                act.wait_ge(out_done, 16 * 2)
                            else:
                                act.wait_ge(kv_out, N_KV_OUT)
                        nc.scalar.activation(at(h_hi, 2 * g + q), t_out[:, q, :], ACT.Copy).then_inc(h_hi_made, 1)
                groups(act, ph, body, first=ph.j in (1, 2), last=True)

            def residual(ph):
                key = (ph.kind, ph.j)
                sums = SUMS_BEFORE[key]

                def body(g):
                    for c in range(4):
                        ahead(ph, g, c)
                        if c % ph.per == ph.per - 1:
                            m = (4 * g + c) if ph.per == 1 else 2 * g + c // 2
                            act.wait_ge(summed, sums + m - 1)
                            wait_then_address(act, drained, ph.unit0 + m + 1)
                            if SET_AFTER[key] is not None:
                                nc.scalar.activation(at(xg_hi, m), at(x, m), ACT.Copy, scale=gain(SET_AFTER[key], m)
                                                     ).then_inc(xg_hi_made, 1)
                            slot = (c if ph.per == 1 else c // 2) % 2
                            nc.scalar.activation(sq[:, slot, :], at(x, m), ACT.Square).then_inc(squared, 1)
                groups(act, ph, body, last=True)

            def conv_in(ph):
                def body(g):
                    for q in range(2):
                        m, u = 2 * g + q, ph.unit0 + 4 * g + 2 * q
                        ahead(ph, g, 2 * q)
                        wait_then_address(act, drained, u + 1)
                        nc.scalar.activation(t_act[:, q, :], t_gate[:, q, :], ACT.Sigmoid, bias=col("b_in", KD + m)
                                             ).then_inc(act_done, 1)
                        ahead(ph, g, 2 * q + 1)
                        act.wait_ge(glu_done, m + 1)
                        for i in range(POOL_TAPS):
                            j = DVE_TAPS + i
                            if i >= 3:
                                wait_then_address(act, tap_added, (POOL_TAPS - 1) * m + max(i - 3, 1))
                            elif not (isinstance(m, int) and m == 0):
                                wait_then_address(act, tap_added, (POOL_TAPS - 1) * (m - 1) + max(POOL_TAPS + i - 3, 1))
                            nc.scalar.activation(tap[:, i % 3, :], glu[:, q, j:j + SEQ], ACT.Copy,
                                                 scale=col("dw", KD * j + m)).then_inc(tap_made, 1)
                groups(act, ph, body, first=True, last=True)
                for m in range(KD):
                    act.wait_ge(centred, m + 1)
                    act.wait_ge(summed, 3 * KD + m - 1)
                    nc.scalar.activation(sq[:, m % 2, :], conv[:, m, :], ACT.Square).then_inc(squared, 1)
                act.dma_start(conv_d, tail[:, :, :]).then_inc(out_done, 16)
                for m in range(KD):
                    act.wait_ge(ln_scaled, m + 1)
                    nc.scalar.activation(t_act[:, m % 2, :], t_gate[:, m % 2, :], ACT.Silu, scale=col("ln_g", m),
                                         bias=col("ln_b", m)).then_inc(ln_done, 1)
                    act.wait_ge(ln_done, m + 1)
                    nc.scalar.activation(h_hi[:, MIX + m, :], t_act[:, m % 2, :], ACT.Copy).then_inc(h_hi_made, 1)

            def rotary(ph):
                for g in range(ph.groups):
                    for c in range(4):
                        ahead(ph, g, c)
                        m = 4 * g + c - 1
                        if ph.kind == "k" and m >= 1:
                            act.wait_ge(rope_done, m)
                            act.dma_start(k_d[:, m - 1, :], k_new[:, m - 1, :]).then_inc(kv_out, 16)
                if ph.kind == "k":
                    for m in (KD - 2, KD - 1):
                        act.wait_ge(rope_done, m + 1)
                        act.dma_start(k_d[:, m, :], k_new[:, m, :]).then_inc(kv_out, 16)

            def store_v(m):
                act.wait_ge(v_turned, m + 1)
                nc.scalar.activation(v_tok[:, m, :], ps_all[:, 6, :], ACT.Copy).then_inc(v_copied, 1)
                act.wait_ge(v_copied, m + 1)
                act.dma_start(v_d[:, m * P:(m + 1) * P].rearrange("(t p) c -> p t c", p=P),
                              v_tok[:, m, :].rearrange("p (t c) -> p t c", c=P)).then_inc(kv_out, 16)

            def v(ph):
                for g in range(ph.groups):
                    for c in range(4):
                        ahead(ph, g, c)
                        if 4 * g + c >= 1:
                            store_v(4 * g + c - 1)
                act.wait_ge(chunk_used, ph.chunk0 + ph.chunks)
                for m in range(KD):
                    x_hi(4, m)
                store_v(KD - 1)
                act.wait_ge(vs_copied, KD)
                act.dma_start(vs_d, v_s[:, :, :]).then_inc(kv_out, 16)

            def attention():
                for s in range(STEPS + 6):
                    if s < STEPS:
                        keys = (s % 4 + 1) * P
                        act.wait_ge(max_done, s + 1)
                        for c in range(2):
                            e = nc.scalar.activation(pr[:, s % 2, c, 0:keys], ps_all[:, 2 * (s % 2) + c, 0:keys], ACT.Exp,
                                                     scale=SCALE, bias=nmx[:, s % 2, c:c + 1],
                                                     accum_out=lsum[:, s % 2, c:c + 1])
                        e.then_inc(exp_done, 1)
                    if 1 <= s <= STEPS:
                        keys = ((s - 1) % 4 + 1) * P
                        act.wait_ge(aT_done, s)
                        nc.scalar.activation(aT[:, (s - 1) % 2, 0:keys], ps_all[:, 4 + (s - 1) % 2, 0:keys], ACT.Copy
                                             ).then_inc(aT_copied, 1)
                    h, t = divmod(s - 5, 4)
                    if t == 0 and 0 <= h < HEADS:
                        act.wait_ge(o_done, h + 1)
                        nc.scalar.activation(sq[:, 0, 0:SEQ], ps_all[:, 6, :], ACT.Square).then_inc(o_squared, 1)
                        nc.scalar.activation(acc[:, 0:SEQ], ps_all[:, 6, :], ACT.Copy).then_inc(o_copied, 1)
                    if t == 2 and 0 <= h < HEADS:
                        act.wait_ge(o_normed, h + 1)
                        nc.scalar.activation(h_hi[:, MIX + h, 0:SEQ], sq[:, 1, 0:SEQ], ACT.Copy, scale=sub_g[:, 0:1]
                                             ).then_inc(o_hi_made, 1)
                    for half in range(2):
                        b, r = divmod(s - 8 - half, 4)
                        if r == 0 and 0 <= b < NS:
                            act.wait_ge(qb_made, 2 * b + half + 1)
                            if half == 0 and b >= 2:
                                act.wait_ge(kprod_done, NPG * (b - 1))
                            nc.scalar.activation(qb[:, b % 2, half * SEQ:(half + 1) * SEQ], ps_all[:, 7, :], ACT.Copy
                                                 ).then_inc(qb_copied, 1)
                act.wait_ge(d_max, 2)
                nc.scalar.activation(p_dec[:, :], ps_all[:, 0, 0:PAST + 1], ACT.Exp, scale=SCALE, bias=mx_s[:, 1:2],
                                     accum_out=mx_s[:, 2:3]).then_inc(d_exp, 1)
                act.wait_ge(d_out, 2)
                nc.scalar.activation(kprod[:, 2 * HD:3 * HD], kprod[:, HD:2 * HD], ACT.Square).then_inc(d_squared, 1)
                act.wait_ge(d_normed, 1)
                nc.scalar.activation(h_hi[:, MIX:KF, SEQ:T], kprod[:, 4 * HD:5 * HD].rearrange("p (h b) -> p h b", h=HEADS),
                                     ACT.Copy, scale=sub_g[:, 0:1]).then_inc(o_hi_made, 1)

            for ph in phases:
                if ph.kind == "up":
                    up(ph)
                elif ph.kind == "conv_in":
                    conv_in(ph)
                elif ph.kind in ("k", "q"):
                    rotary(ph)
                    if ph.kind == "q":
                        attention()
                elif ph.kind == "v":
                    v(ph)
                else:
                    residual(ph)
            for m in range(KD):
                act.wait_ge(final_done, m + 1)
                act.dma_start(y_d[:, m, :], x[:, m, :]).then_inc(out_done, 16)

        @block.vector
        def _(dve):
            own = [0]

            def link(instruction):
                own[0] += 1
                instruction.then_inc(dve_self, 1)
                dve.wait_ge(dve_self, own[0])

            made = [0]

            def split_lo(ph, g, c):
                n = ph.chunk0 + 4 * g + c
                dve.wait_ge(hi_made, n + 1)
                w = ph.tiles * P
                nc.vector.tensor_tensor(w_lo[:, c % 2, 0:w], raw[:, c, 0:w], w_hi[:, c % 2, 0:w], ALU.subtract
                                        ).then_inc(weights_ready, 1)

            def ahead(ph, g, c):
                to = coming(ph, g, c)
                if to:
                    split_lo(*to)

            def x_lo(s, m):
                dve.wait_ge(xg_hi_made, KD * s + m + 1)
                nc.vector.scalar_tensor_tensor(at(xg_lo, m), at(x, m), gain(s, m), at(xg_hi, m), ALU.mult, ALU.subtract
                                               ).then_inc(xg_ready, 1)

            def rms():
                made[0] += 1
                dve.wait_ge(var_done, made[0])
                nc.vector.tensor_scalar(var[:, :], ps_var, EPS, None, ALU.add).then_inc(var_read, 1)
                dve.wait_ge(spread_done, made[0])
                nc.vector.tensor_copy(halves(rstd[:, :]), ps_stat).then_inc(rstd_made, 1)
                dve.wait_ge(rstd_made, made[0])

            def scaled(out, slot):
                return nc.vector.tensor_tensor(halves(out), unit[slot], halves(rstd[:, :]), ALU.mult)

            dve.wait_ge(inputs, N_IN)
            nc.vector.tensor_tensor(lam_prod[0:1, :, :], lam_row[0:1, 0:4:2, :], lam_row[0:1, 1:4:2, :], ALU.mult
                                    ).then_inc(lam_step, 1)
            dve.wait_ge(lam_step, 1)
            nc.vector.tensor_reduce(lam_s[0:1, 0:2], lam_prod[0:1, :, :], AX.X, ALU.add).then_inc(lam_step, 1)
            dve.wait_ge(lam_step, 3)
            nc.vector.tensor_scalar(lam_s[0:1, 4:5], lam_s[0:1, 3:4], lam_s[0:1, 2:3], LAM_INIT, ALU.subtract, ALU.subtract
                                    ).then_inc(lam_step, 1)
            for m in range(KD):
                x_lo(0, m)
            split_lo(phases[0], 0, 0)
            split_lo(phases[0], 0, 1)
            dve.wait_ge(lam_step, 5)
            link(nc.vector.tensor_scalar(neglam[:, :], ps_all[:, 6, 0:1], float(D), None, ALU.mult))
            nc.vector.scalar_tensor_tensor(pairco[:, :], cst[:, C_ODD:C_ODD + 1], neglam[:, :], cst[:, C_EVEN:C_EVEN + 1],
                                           ALU.mult, ALU.add)
            nc.vector.tensor_scalar(sub_g[:, :], col("sub", 0), 1.0 - LAM_INIT, None, ALU.mult)

            def up(ph):
                def body(g):
                    for q in range(2):
                        n, p = ph.chunk0 + 4 * g + 2 * q, ph.pair0 + 2 * g + q
                        dve.wait_ge(chunk_used, n + 1)
                        scaled(t_gate[:, q, :], 0).then_inc(drained, 1)
                        ahead(ph, g, 2 * q)
                        dve.wait_ge(chunk_used, n + 2)
                        dve.wait_ge(act_scaled, p + 1 - KD * (ph.j > 0))
                        nc.vector.tensor_tensor(halves(t_out[:, q, :]), unit[1], halves(t_gate[:, q, :]), ALU.mult
                                                ).then_inc(drained, 1)
                        ahead(ph, g, 2 * q + 1)
                groups(dve, ph, body, last=True)

            def residual(ph):
                s = SET_AFTER[ph.kind, ph.j]

                def body(g):
                    for c in range(4):
                        last = c % ph.per == ph.per - 1
                        m = (4 * g + c) if ph.per == 1 else 2 * g + c // 2
                        slot = (c if ph.per == 1 else c // 2) % 2
                        dve.wait_ge(chunk_used, ph.chunk0 + 4 * g + c + 1)
                        if last:
                            op, by = {"down": (ALU.mult, 0.5), "o": (ALU.mult, 1.0)}.get(ph.kind) or (ALU.add, col("b_out", m))
                            xm = halves(at(x, m))
                            nc.vector.scalar_tensor_tensor(xm, unit[slot], by, xm, op, ALU.add).then_inc(drained, 1)
                        ahead(ph, g, c)
                        if last and s is not None:
                            x_lo(s, m)
                groups(dve, ph, body, last=True)

            def taps(m, q):
                chains = (conv[:, m, 0:SEQ] if isinstance(m, int) else conv[:, bass.ds(m, 1), 0:SEQ].rearrange("p a t -> p (a t)"),
                          conv_b[:, :])
                for j in range(DVE_TAPS):
                    src = glu[:, q, j:j + SEQ]
                    w = col("dw", KD * j + m)
                    out = chains[j % 2]
                    if j == 0:
                        i = nc.vector.tensor_scalar(out, src, w, col("dw_b", m), ALU.mult, ALU.add)
                    elif j == 1:
                        i = nc.vector.tensor_scalar(out, src, w, None, ALU.mult)
                    else:
                        dve.wait_ge(tapped, DVE_TAPS * m + j - 1)
                        i = nc.vector.scalar_tensor_tensor(out, src, w, out, ALU.mult, ALU.add)
                    i.then_inc(tapped, 1)
                return chains

            def conv_in(ph):
                nc.vector.memset(glu[:, :, 0:CW - 1], 0.0).then_inc(glu_pad, 1)
                dve.wait_ge(glu_pad, 1)

                def body(g):
                    for q in range(2):
                        n, m, p = ph.chunk0 + 4 * g + 2 * q, 2 * g + q, ph.pair0 + 2 * g + q
                        dve.wait_ge(chunk_used, n + 1)
                        scaled(t_gate[:, q, :], 0).then_inc(drained, 1)
                        ahead(ph, g, 2 * q)
                        dve.wait_ge(chunk_used, n + 2)
                        scaled(t_out[:, q, :], 1).then_inc(drained, 1)
                        dve.wait_ge(drained, ph.unit0 + 4 * g + 2 * q + 2)
                        dve.wait_ge(act_done, p + 1)
                        nc.vector.scalar_tensor_tensor(glu[:, q, CW - 1:CW - 1 + T], t_out[:, q, :], col("b_in", m), t_act[:, q, :],
                                                       ALU.add, ALU.mult).then_inc(glu_done, 1)
                        ahead(ph, g, 2 * q + 1)
                        dve.wait_ge(glu_done, m + 1)
                        a, b = taps(m, q)
                        nc.vector.tensor_copy(at(tail, m), glu[:, q, SEQ:CW - 1 + T])
                        win = window[:, m] if isinstance(m, int) else window[:, bass.ds(m, 1)].rearrange("p a b j -> p (a b) j")
                        nc.vector.tensor_copy(win[:, :, CW - 1], glu[:, q, CW - 1 + SEQ:CW - 1 + T]).then_inc(win_done, 2)
                        dve.wait_ge(win_done, 4 * m + 2)
                        w = vec[:, VEC["dw"] + m:VEC["dw"] + m + KD * (CW - 1) + 1:KD] if isinstance(m, int) else \
                            vec[:, bass.ds(VEC["dw"] + m, CW, KD)]
                        nc.vector.tensor_tensor(swin[:, :, :], win, w.unsqueeze(1).broadcast_to([P, NS, CW]), ALU.mult
                                                ).then_inc(win_done, 1)
                        dve.wait_ge(tapped, DVE_TAPS * (m + 1))
                        dve.wait_ge(win_done, 4 * m + 3)
                        nc.vector.tensor_tensor(a, a, b, ALU.add)
                        cs = conv[:, m, SEQ:T] if isinstance(m, int) else conv[:, bass.ds(m, 1), SEQ:T].rearrange("p a t -> p (a t)")
                        nc.vector.tensor_reduce(cs, swin[:, :, :], AX.X, ALU.add).then_inc(win_done, 1)
                        dve.wait_ge(win_done, 4 * m + 4)
                        dve.wait_ge(tap_added, (POOL_TAPS - 1) * (m + 1))
                        nc.vector.tensor_scalar(cs, cs, col("dw_b", m), None, ALU.add)
                        nc.vector.tensor_tensor(a, a, conv_p[:, q, :], ALU.add).then_inc(conv_done, 1)
                dve.wait_ge(in_state, 16)
                groups(dve, ph, body, last=True)
                dve.wait_ge(mean_done, 1)
                for m in range(KD):
                    cm = halves(conv[:, m, :])
                    nc.vector.tensor_tensor(cm, cm, ps_stat, ALU.subtract).then_inc(centred, 1)
                rms()

                def lo(m):
                    dve.wait_ge(h_hi_made, ph.h0 + m + 1)
                    nc.vector.tensor_tensor(h_lo[:, MIX + m, :], t_act[:, m % 2, :], h_hi[:, MIX + m, :], ALU.subtract
                                            ).then_inc(h_ready, 1)
                for m in range(KD):
                    nc.vector.tensor_tensor(t_gate[:, m % 2, :], conv[:, m, :], rstd[:, :], ALU.mult).then_inc(ln_scaled, 1)
                    if m:
                        lo(m - 1)
                lo(KD - 1)

            def rotary(ph):
                r0 = 0 if ph.kind == "k" else KD
                cs = cs_k if ph.kind == "k" else cs_q

                def sine(r):
                    dve.wait_ge(rot_done, r + 1)
                    nc.vector.tensor_tensor(halves(t_out[:, r % 2, :]), ps_rot, halves(cs[:, 1, :]), ALU.mult
                                            ).then_inc(sin_done, 1)
                dve.wait_ge(in_rope[ph.kind == "q"], 16)
                for g in range(ph.groups):
                    for c in range(4):
                        r = r0 + 4 * g + c
                        dve.wait_ge(chunk_used, ph.chunk0 + 4 * g + c + 1)
                        if r >= 2:
                            dve.wait_ge(rope_done, r - 1)
                        scaled(t_gate[:, r % 2, :], c % 2).then_inc(drained, 1)
                        ahead(ph, g, c)
                        if r > r0:
                            sine(r - 1)
                sine(r0 + KD - 1)

            def v(ph):
                for g in range(ph.groups):
                    for c in range(4):
                        m = 4 * g + c
                        dve.wait_ge(chunk_used, ph.chunk0 + m + 1)
                        if m < 2:
                            dve.wait_ge(rope_done, KD - 1 + m)
                        else:
                            dve.wait_ge(v_turned, m - 1)
                            dve.wait_ge(vs_copied, m - 1)
                        scaled(t_gate[:, m % 2, :], m % 2).then_inc(drained, 1)
                        ahead(ph, g, c)
                for m in range(KD):
                    x_lo(4, m)
                dve.wait_ge(v_turned, KD)
                dve.wait_ge(vs_copied, KD)

            def attention():
                for s in range(STEPS + 8):
                    if s < STEPS:
                        keys = (s % 4 + 1) * P
                        dve.wait_ge(scores_done, s + 1)
                        link(nc.vector.tensor_reduce(mx[:, s % 2, :], ps_all[:, 2 * (s % 2):2 * (s % 2) + 2, 0:keys], AX.X, ALU.max))
                        nc.vector.tensor_scalar(nmx[:, s % 2, :], mx[:, s % 2, :], -SCALE, None, ALU.mult).then_inc(max_done, 1)
                    if 1 <= s <= STEPS:
                        e, keys = (s - 1) % 2, ((s - 1) % 4 + 1) * P
                        dve.wait_ge(exp_done, s)
                        link(nc.vector.reciprocal(rl[:, e, :], lsum[:, e, :]))
                        link(nc.vector.tensor_tensor(rl2[:, e:e + 1], rl[:, e, 1:2], neglam[:, :], ALU.mult))
                        link(nc.vector.tensor_scalar(pr[:, e, 1, 0:keys], pr[:, e, 1, 0:keys], rl2[:, e:e + 1], None, ALU.mult))
                        nc.vector.scalar_tensor_tensor(at_n[:, e, 0:keys], pr[:, e, 0, 0:keys], rl[:, e, 0:1], pr[:, e, 1, 0:keys],
                                                       ALU.mult, ALU.add).then_inc(a_done, 1)
                    h, t = divmod(s - 6, 4)
                    if t == 0 and 0 <= h < HEADS:
                        dve.wait_ge(o_stat, h + 1)
                        nc.vector.tensor_scalar(var[:, 0:SEQ // P], ps_all[:, 7, 0:SEQ // P], D / P, EPS, ALU.mult, ALU.add).then_inc(o_var, 1)
                    if t == 1 and 0 <= h < HEADS:
                        dve.wait_ge(o_spread, h + 1)
                        nc.vector.tensor_tensor(sq[:, 1, 0:SEQ], ps_all[:, 7, :], acc[:, 0:SEQ], ALU.mult).then_inc(o_normed, 1)
                    if t == 2 and 0 <= h < HEADS:
                        dve.wait_ge(o_hi_made, h + 1)
                        nc.vector.scalar_tensor_tensor(h_lo[:, MIX + h, 0:SEQ], sq[:, 1, 0:SEQ], sub_g[:, 0:1], h_hi[:, MIX + h, 0:SEQ],
                                                       ALU.mult, ALU.subtract).then_inc(o_lo_made, 1)
                    for g in range(NPG):
                        b, r = divmod(s - 10 - g, 4)
                        if r == 0 and 0 <= b < NS:
                            dve.wait_ge(kprod_done, NPG * b + g + 1)
                            nc.vector.tensor_reduce(s_dec[:, g, b, :], kprod[:, :].rearrange("p (j d) -> p j d", d=HD), AX.X,
                                                    ALU.add).then_inc(kred_done, 1)
                nc.vector.memset(z_dec[:, :, :, :], 0.0).then_inc(d_new, 1)
                dve.wait_ge(d_new, 1)
                for c in range(2):
                    rows = slice(c * HD, (c + 1) * HD)
                    nc.vector.scalar_tensor_tensor(z_dec[rows, :, :, c].rearrange("p b h -> p h b"), qT[rows, :, SEQ:T], float(D),
                                                   kT[rows, :, SEQ:T], ALU.mult, ALU.mult).then_inc(d_new, 1)
                dve.wait_ge(d_scores, 1)
                nc.vector.tensor_reduce(mx_s[:, 0:1], ps_all[:, 0, 0:PAST + 1], AX.X, ALU.max).then_inc(d_max, 1)
                dve.wait_ge(d_max, 1)
                nc.vector.tensor_scalar(mx_s[:, 1:2], mx_s[:, 0:1], -SCALE, None, ALU.mult).then_inc(d_max, 1)
                dve.wait_ge(d_exp, 1)
                link(nc.vector.reciprocal(rl2[:, 0:1], mx_s[:, 2:3]))
                link(nc.vector.tensor_tensor(rl2[:, 1:2], rl2[:, 0:1], pairco[:, :], ALU.mult))
                nc.vector.tensor_scalar(p_dec[:, :], p_dec[:, :], rl2[:, 1:2], None, ALU.mult).then_inc(d_weights, 1)
                dve.wait_ge(d_turned, 1)
                link(nc.vector.tensor_copy(an_dec[:, :, :], ps_all[:, 1, 2 * HD:3 * HD].rearrange("p (b h) -> p b h", b=NS)))
                nc.vector.tensor_copy(at_dec[:, :, :, :].rearrange("p g b h -> p (g b h)"), ps_all[:, 1, 0:2 * HD]).then_inc(d_turned_read, 1)
                nc.vector.tensor_tensor(kprod[:, 0:HD].rearrange("p (h b) -> p h b", h=HEADS), an_dec[:, :, :].rearrange("p b h -> p h b"),
                                        v_s[:, :, :], ALU.mult).then_inc(d_out, 1)
                dve.wait_ge(v_page_used, NS * NPG)
                dve.wait_ge(d_out, 1)
                nc.vector.tensor_tensor(kprod[:, HD:2 * HD], ps_all[:, 2, 0:HD], kprod[:, 0:HD], ALU.add).then_inc(d_out, 1)
                dve.wait_ge(d_stat, 1)
                nc.vector.tensor_scalar(var[0:HD, 0:1], ps_all[0:HD, 3, 0:1], D / P, EPS, ALU.mult, ALU.add).then_inc(d_inv, 1)
                dve.wait_ge(d_spread, 1)
                nc.vector.tensor_tensor(kprod[:, 4 * HD:5 * HD], ps_all[:, 3, 0:HD], kprod[:, HD:2 * HD], ALU.mult).then_inc(d_normed, 1)
                dve.wait_ge(o_hi_made, HEADS + 1)
                nc.vector.scalar_tensor_tensor(h_lo[:, MIX:KF, SEQ:T], kprod[:, 4 * HD:5 * HD].rearrange("p (h b) -> p h b", h=HEADS),
                                               sub_g[:, 0:1], h_hi[:, MIX:KF, SEQ:T], ALU.mult, ALU.subtract).then_inc(o_lo_made, 1)

            for ph in phases:
                if fresh(ph):
                    rms()
                if ph.kind == "up":
                    up(ph)
                elif ph.kind == "conv_in":
                    conv_in(ph)
                elif ph.kind in ("k", "q"):
                    rotary(ph)
                    if ph.kind == "q":
                        attention()
                elif ph.kind == "v":
                    v(ph)
                else:
                    residual(ph)
            rms()
            for m in range(KD):
                nc.vector.scalar_tensor_tensor(x[:, m, :], x[:, m, :], col("final", m), rstd[:, :], ALU.mult, ALU.mult
                                               ).then_inc(final_done, 1)

        @block.gpsimd
        def _(pool):
            nc.gpsimd.memset(ones_d[:, :], 1.0 / D).then_inc(const_done, 1)
            nc.gpsimd.memset(minus_half[:, :], -0.5).then_inc(const_done, 1)
            sums, squares = [0], [0]

            def add_tile(m, src):
                if m == 0:
                    i = nc.gpsimd.tensor_copy(acc[:, :], src)
                else:
                    pool.wait_ge(summed, sums[0])
                    i = nc.gpsimd.tensor_tensor(acc[:, :], acc[:, :], src, ALU.add)
                i.then_inc(summed, 1)
                sums[0] += 1

            def add_squares():
                for m in range(KD):
                    squares[0] += 1
                    pool.wait_ge(squared, squares[0])
                    add_tile(m, sq[:, m % 2, :])

            def up(ph):
                def body(g):
                    for q in range(2):
                        p = ph.pair0 + 2 * g + q
                        pool.wait_ge(act_done, p + 1)
                        nc.gpsimd.tensor_tensor(t_gate[:, q, :], t_act[:, q, :], rstd[:, :], ALU.mult).then_inc(act_scaled, 1)
                        pool.wait_ge(h_hi_made, ph.h0 + 2 * g + q + 1)
                        nc.gpsimd.tensor_tensor(at(h_lo, 2 * g + q), t_out[:, q, :], at(h_hi, 2 * g + q), ALU.subtract
                                                ).then_inc(h_ready, 1)
                groups(pool, ph, body)

            def conv_in(ph):
                for m in range(KD):
                    for i in range(1, POOL_TAPS):
                        pool.wait_ge(tap_made, POOL_TAPS * m + i + 1)
                        if i == 1:
                            s = nc.gpsimd.tensor_tensor(conv_p[:, m % 2, :], tap[:, 0, :], tap[:, 1, :], ALU.add)
                        else:
                            pool.wait_ge(tap_added, (POOL_TAPS - 1) * m + i - 1)
                            s = nc.gpsimd.tensor_tensor(conv_p[:, m % 2, :], conv_p[:, m % 2, :], tap[:, i % 3, :], ALU.add)
                        s.then_inc(tap_added, 1)
                    pool.wait_ge(conv_done, m + 1)
                    add_tile(m, conv[:, m, :])
                add_squares()
                rms()

            def rotary(ph):
                r0, u0 = (0, K0) if ph.kind == "k" else (KD, Q0)
                cs, out = (cs_k, k_new) if ph.kind == "k" else (cs_q, qT)

                def both(r):
                    pool.wait_ge(sin_done, r + 1)
                    pool.wait_ge(cos_done, r + 1)
                    nc.gpsimd.tensor_tensor(out[:, r - r0, :], t_act[:, r % 2, :], t_out[:, r % 2, :], ALU.add
                                            ).then_inc(rope_done, 1)
                pool.wait_ge(in_rope[ph.kind == "q"], 16)
                for r in range(r0, r0 + KD):
                    pool.wait_ge(drained, u0 + r - r0 + 1)
                    nc.gpsimd.tensor_tensor(t_act[:, r % 2, :], t_gate[:, r % 2, :], cs[:, 0, :], ALU.mult).then_inc(cos_done, 1)
                    if r > r0:
                        both(r - 1)
                both(r0 + KD - 1)

            def attention():
                for b in range(NS):
                    pool.wait_ge(o_var, b + 1)
                    power(SEQ // P).then_inc(o_inv, 1)
                    pool.wait_ge(qb_copied, 2 * b + 2)
                    for g in range(NPG):
                        i = NPG * b + g
                        pool.wait_ge(page_full[i % 4], 16 * (i // 4 + 1))
                        if i:
                            pool.wait_ge(kred_done, i)
                        nc.gpsimd.tensor_tensor(kprod[:, :], page[:, i % 4, :], qb[:, b % 2, :], ALU.mult).then_inc(kprod_done, 1)
                pool.wait_ge(d_inv, 1)
                power(1, HD).then_inc(d_inv, 1)

            def power(n, rows=P):
                return nc.gpsimd.tensor_tensor(inv[0:rows, 0:n], var[0:rows, 0:n], minus_half[0:rows, 0:n], ALU.pow)

            made = [0]

            def rms():
                made[0] += 1
                pool.wait_ge(var_read, made[0])
                power(len(BLOCKS)).then_inc(inv_made, 1)

            add_squares()
            for ph in phases:
                if fresh(ph):
                    rms()
                if ph.kind == "up":
                    up(ph)
                elif ph.kind == "conv_in":
                    conv_in(ph)
                elif ph.kind in ("k", "q"):
                    rotary(ph)
                    if ph.kind == "q":
                        attention()
                elif ph.kind == "v":
                    for m in range(KD):
                        pool.wait_ge(drained, V0 + m + 1)
                        nc.gpsimd.tensor_copy(v_s[:, m, :], t_gate[:, m % 2, SEQ:T]).then_inc(vs_copied, 1)
                else:
                    add_squares()
            rms()


def kernel(**inputs):
    import concourse.bacc as bacc
    from concourse.bass_utils import run_bass_kernel_spmd

    a = {k: np.ascontiguousarray(v) for k, v in inputs.items()}

    def features(t):
        return np.ascontiguousarray(t.reshape(-1, KD, P).transpose(2, 1, 0))

    f32 = np.float32
    rows = np.concatenate([a[n].reshape(-1, P) for n in (
        "norm_ffn", "norm_mix", "kv_norm", "norm_final", "conv_b_in", "conv_dw", "conv_dw_b", "conv_ln_g", "conv_ln_b",
        "conv_b_out", "subln_g")])
    i = np.arange(P)
    rot = (i[:, None] == (i ^ (HD // 2))[None, :]).astype(f32)
    cst = np.concatenate([np.eye(P, dtype=f32), rot, np.where(i[None, :] > i[:, None], NEG, 0.0).astype(f32),
                          (i[:, None] // 2 == np.arange(HD)[None, :]).astype(f32),
                          (i[:, None] % 2 == 0).astype(f32), (i[:, None] % 2 == 1).astype(f32)], axis=1)
    pos = np.concatenate([np.arange(SEQ), np.full(NS, PAST)]).astype(f32)
    freqs = (f32(10000.0) ** (-np.arange(HD // 2, dtype=f32) * f32(2.0) / f32(HD))).astype(f32)
    ang = freqs[i % (HD // 2)][:, None] * pos[None, :]
    sign = np.where(i % HD < HD // 2, -1.0, 1.0).astype(f32)[:, None]
    rope = np.stack([np.cos(ang), sign * np.sin(ang)], axis=1).astype(f32)

    ins = {
        "xT": features(np.concatenate([a["x_prompt"].reshape(SEQ, D), a["x_sample"].reshape(NS, D)])),
        "vec": np.ascontiguousarray(rows.T),
        "cst": np.ascontiguousarray(cst),
        "rope": np.ascontiguousarray(rope),
        "lam": np.concatenate([a[n] for n in ("lambda_q1", "lambda_k1", "lambda_q2", "lambda_k2")]).reshape(1, 4, HD),
        "stateT": np.ascontiguousarray(a["state_conv"][0].reshape(NS, CW - 1, KD, P).transpose(3, 2, 0, 1)),
        "state": a["state_conv"][0],
        "cache_k": a["cache_k"].reshape(NPOOL, PAGE, D),
        "cache_v": a["cache_v"].reshape(NPOOL, PAGE, D),
        "pages": a["page_table"].reshape(1, NS * NPG),
        "w_in": a["ffn_w_in"], "w_out": a["ffn_w_out"], "c_in": a["conv_w_in"], "c_out": a["conv_w_out"],
        "w_kv": a["w_kv"], "w_q": a["w_q"], "w_o": a["w_o"],
    }
    outs = {"y": (P, KD, T), "conv_tail": (P, KD, CW - 1 + NS), "new_state": (NS, CW - 2, D), "k_new_out": (P, KD, T),
            "v_new_out": (SEQ, D), "v_new_s": (P, KD, NS)}
    nc = bacc.Bacc("TRN2", target_bir_lowering=False, num_devices=1)
    args = [nc.dram_tensor(n, v.shape, mybir.dt.from_np(v.dtype), kind="ExternalInput").ap() for n, v in ins.items()]
    args += [nc.dram_tensor(n, s, F32, kind="ExternalOutput").ap() for n, s in outs.items()]
    trunk(nc, *args)
    r = run_bass_kernel_spmd(nc, [ins], core_ids=[0]).results[0]

    def tokens(t):
        return np.ascontiguousarray(t.transpose(2, 1, 0)).reshape(t.shape[2], -1)

    y, k, v_s, tail = tokens(r["y"]), tokens(r["k_new_out"]), tokens(r["v_new_s"]), tokens(r["conv_tail"])
    heads = (HEADS, 2 * HD)
    new_s = np.concatenate([r["new_state"], tail[CW - 1:].reshape(NS, 1, D)], axis=1)
    return (y[:SEQ].reshape(1, SEQ, D), y[SEQ:].reshape(NS, 1, D), tail[:CW - 1].reshape(1, 1, CW - 1, D),
            k[:SEQ].reshape(1, SEQ, *heads), r["v_new_out"].reshape(1, SEQ, *heads), new_s.reshape(1, NS, CW - 1, D),
            k[SEQ:].reshape(NS, 1, *heads), v_s.reshape(NS, 1, *heads))
```

```python
import math
from contextlib import ExitStack

import numpy as np

import concourse.bass as bass
from concourse import mybir
from concourse.alu_op_type import AluOpType as ALU

F32 = mybir.dt.float32
F32R = mybir.dt.float32r
BF16 = mybir.dt.bfloat16
I32 = mybir.dt.int32
ACT = mybir.ActivationFunctionType
AX = mybir.AxisListType

P = 128
D = 1024
KD = D // P
SEQ = 512
NS = 8
T = SEQ + NS
HALF = T // 2
FF = 2816
KF = FF // P
HEADS = 8
HD = 64
CW = 31
PAST = 256
PAGE = 128
NPG = PAST // PAGE
NPOOL = NS * NPG * 5 // 4
EPS = 1e-6
SCALE = HD ** -0.5
LAM_INIT = 0.8 - 0.6 * math.exp(-0.3 * 1)
KW = KF // 2
MIX = KF - KD
NEG = -1.0e30

VEC = {}
_at = 0
for _name, _n in (("ffn", 4 * KD), ("mix", 2 * KD), ("kv", KD), ("final", KD), ("b_in", 2 * KD),
                  ("dw", CW * KD), ("dw_b", KD), ("ln_g", KD), ("ln_b", KD), ("b_out", KD), ("sub", 1)):
    VEC[_name] = _at
    _at += _n
NVEC = _at
C_ID, C_ROT, C_MASK, C_PAIR, C_EVEN, C_ODD = 0, P, 2 * P, 3 * P, 3 * P + HD, 3 * P + HD + 1
NCST = C_ODD + 1

DVE_TAPS = 16


class Phase:

    def __init__(self, kind, tiles, chunks, per, weights, j=0):
        self.kind, self.tiles, self.chunks, self.per, self.weights, self.j = kind, tiles, chunks, per, weights, j
        self.groups = chunks // 4
        self.chunk0 = self.unit0 = self.pair0 = self.h0 = self.set = self.next = None


def plan(w_in, w_out, c_in, c_out, w_kv, w_q, w_o):
    def pair(w, half):
        v = w.rearrange("(k p) (a m c) -> a p m k c", p=P, a=2, c=P)
        return lambda g, c: v[(c % 2) ^ half, :, 2 * g + c // 2, :, :]

    def down(w):
        v = w.rearrange("(f k p) (m c) -> f p m k c", f=2, p=P, c=P)
        return lambda g, c: v[c % 2, :, 2 * g + c // 2, :, :]

    def square(w):
        v = w.rearrange("(k p) (m c) -> p m k c", p=P, c=P)
        return lambda g, c: v[:, 4 * g + c, :, :]

    def ffn(j):
        return [Phase("up", KD, 2 * KF, 1, pair(w_in[j // 2, j % 2], 0), j),
                Phase("down", KW, 2 * KD, 2, down(w_out[j // 2, j % 2]), j)]

    phases = (ffn(0) + [Phase("conv_in", KD, 2 * KD, 1, pair(c_in[0], 1)), Phase("conv_out", KD, KD, 1, square(c_out[0]))]
              + ffn(1) + [Phase("k", KD, KD, 1, square(w_kv[:, 0:D])), Phase("v", KD, KD, 1, square(w_kv[:, D:2 * D]))]
              + ffn(2) + [Phase("q", KD, KD, 1, square(w_q[0])), Phase("o", KD, KD, 1, square(w_o[0]))] + ffn(3))
    chunk = unit = pairs = h = sets = 0
    for ph in phases:
        ph.chunk0, ph.unit0, ph.pair0, ph.h0 = chunk, unit, pairs, h
        chunk += ph.chunks
        unit += ph.chunks // ph.per
        pairs += ph.chunks // 2 if ph.kind in ("up", "conv_in") else 0
        h += {"up": KF, "conv_in": KD}.get(ph.kind, 0)
        if ph.kind in ("up", "conv_in", "k", "q"):
            ph.set = sets
            sets += 1
        elif ph.kind == "v":
            ph.set = sets - 1
    for a, b in zip(phases, phases[1:]):
        a.next = b
    return phases


def trunk(nc, xT, vec_d, cst_d, rope_d, lam_d, stateT, state, cache_k, cache_v, pages, w_in, w_out, c_in, c_out,
          w_kv, w_q, w_o, y_d, conv_d, new_state_d, k_d, v_d, vs_d):
    q_dram = nc.dram_tensor("q_dram", (NS, D), F32, kind="Internal").ap()
    phases = plan(w_in, w_out, c_in, c_out, w_kv, w_q, w_o)
    KIND = {}
    for ph in phases:
        KIND.setdefault(ph.kind, []).append(ph)
    last_phase = phases[-1]

    with ExitStack() as ctx:
        def sb(name, shape, dt=F32):
            return ctx.enter_context(nc.sbuf_tensor(name, shape, dt))

        def sem(name):
            return ctx.enter_context(nc.semaphore(name))

        cursor = [-(-nc.sbuf_base // 32) * 32]
        top = cursor[0]

        def place(name, shape, dt=F32, at=None):
            size = int(np.prod(shape[1:])) * (2 if dt == BF16 else 4)
            if at is None:
                at = cursor[0]
                cursor[0] += -(-size // 32) * 32
            where[name] = (at, at + -(-size // 32) * 32)
            return nc.alloc_sbuf_tensor_at(name, shape, dt, offset=at)

        where = {}
        xg_hi = place("xg_hi", [P, KD, T], F32R)
        xg_lo = place("xg_lo", [P, KD, T], F32R)
        h_hi = place("h_hi", [P, KF, T], F32R)
        h_lo = place("h_lo", [P, KF, T], F32R)
        x = place("x", [P, KD, T])
        raw = place("raw", [P, 4, KW * P])
        w_hi = place("w_hi", [P, 2, KW * P], F32R)
        w_lo = place("w_lo", [P, 2, KW * P], F32R)
        rstd = place("rstd", [P, T])
        acc = place("acc", [P, T])
        sq = place("sq", [P, 2, T])
        t_gate = place("t_gate", [P, 2, T])
        t_act = place("t_act", [P, 2, T])
        t_out = place("t_out", [P, 2, T])
        vec = place("vec", [P, NVEC])
        cst = place("cst", [P, NCST])
        ones_d = place("ones_d", [P, P])
        ident_b = place("ident_b", [P, P], BF16)
        mask_b = place("mask_b", [P, P], BF16)
        v_s = place("v_s", [P, HEADS, NS])
        neglam = place("neglam", [P, 1])
        pairco = place("pairco", [P, 1])
        sub_g = place("sub_g", [P, 1])
        lam_s = place("lam_s", [1, 8])
        pages_s = place("pages_s", [1, NS * NPG], I32)
        mx = place("mx", [P, 2, 2])
        nmx = place("nmx", [P, 2, 2])
        lsum = place("lsum", [P, 2, 2])
        rl = place("rl", [P, 2, 2])
        rl2 = place("rl2", [P, 2])
        mx_s = place("mx_s", [P, 4])
        var = place("var", [P, 6])
        inv = place("inv", [P, 6])
        minus_half = place("minus_half", [P, 6])
        assert cursor[0] <= nc.sbuf_usable_end, cursor[0]
        sb("fence", [P, (cursor[0] - top) // 4])

        XG, HH, HL = where["xg_hi"][0], where["h_hi"][0], where["h_lo"][0]
        room = MIX * T * 4

        def over(base, size, items):
            made, at = [], base
            for name, shape in items:
                made.append(place(name, shape, at=at))
                at = where[name][1]
            assert at <= base + size, (items, at - base - size)
            return made

        lam_row, lam_prod = over(HH, room, [("lam_row", [1, 4, HD]), ("lam_prod", [1, 2, HD])])
        conv, window, conv_p = over(HL, room, [("conv", [P, KD, T]), ("window", [P, KD, CW, NS]), ("conv_p", [P, 2, SEQ])])
        glu, tap, conv_b, swin, tail = over(HH, room, [
            ("glu", [P, 2, CW - 1 + T]), ("tap", [P, 3, SEQ]), ("conv_b", [P, SEQ]), ("swin", [P, CW, NS]),
            ("tail", [P, KD, CW - 1 + NS])])
        k_new, = over(HL, room, [("k_new", [P, KD, T])])
        cs_k, v_tok = over(HH, room, [("cs_k", [P, 2, T]), ("v_tok", [P, KD, SEQ])])
        qT, cs_q, pr = over(HL, room, [("qT", [P, KD, T]), ("cs_q", [P, 2, T]), ("pr", [P, 2, 2, SEQ])])
        kT, at_n, aT, s_dec, p_dec, at_dec, an_dec = over(HH, room, [
            ("kT", [P, KD, T]), ("at_n", [P, 2, SEQ]), ("aT", [P, 2, SEQ]), ("s_dec", [P, NPG, NS, 2 * HEADS]),
            ("p_dec", [P, PAST + 1]), ("at_dec", [P, NPG, NS, HEADS]), ("an_dec", [P, NS, HEADS])])
        vT, page = over(XG, 2 * KD * T * 4, [("vT", [P, SEQ // P, D]), ("page", [P, 4, D])])
        page_4, = over(where["cs_q"][0], 2 * T * 4, [("page_4", [P, D])])
        tg0 = where["t_gate"][0]
        qb, kprod = over(tg0, 6 * T * 4, [("qb", [P, 2, D]), ("kprod", [P, D])])
        z_dec, = over(where["sq"][0], 4160, [("z_dec", [P, NS, HEADS, 2])])

        K_SLOTS = [page[:, i, :] for i in range(4)] + [page_4[:, :]]
        V_SLOTS = K_SLOTS + [qb[:, i, :] for i in range(2)]

        ps_all = ctx.enter_context(nc.psum_tensor("ps_all", [P, 8, 512], F32))
        unit = [ps_all[:, 2 * s:2 * s + 2, 0:HALF] for s in range(2)]
        ps_stat = ps_all[:, 4:6, 0:HALF]
        ps_var = ps_all[:, 4, 0:6]
        ps_rot = ps_all[:, 6:8, 0:HALF]

        def halves(ap):
            return ap.rearrange("p (a b) -> p a b", a=2)

        raw_full = [sem(f"raw_full{s}") for s in range(4)]
        hi_made = sem("hi_made")
        weights_ready = sem("weights_ready")
        chunk_used = sem("chunk_used")
        drained = sem("drained")
        act_done = sem("act_done")
        act_scaled = sem("act_scaled")
        h_hi_made = sem("h_hi_made")
        h_ready = sem("h_ready")
        xg_hi_made = sem("xg_hi_made")
        xg_ready = sem("xg_ready")
        squared = sem("squared")
        sq_used = sem("sq_used")
        acc_copied = sem("acc_copied")
        summed = sem("summed")
        mean_done = sem("mean_done")
        var_done = sem("var_done")
        var_read = sem("var_read")
        inv_made = sem("inv_made")
        spread_done = sem("spread_done")
        rstd_made = sem("rstd_made")
        inputs = sem("inputs")
        in_state = sem("in_state")
        in_rope = [sem("in_rope_k"), sem("in_rope_q")]
        const_done = sem("const_done")
        lam_step = sem("lam_step")
        rot_done = sem("rot_done")
        cos_done = sem("cos_done")
        sin_done = sem("sin_done")
        rope_done = sem("rope_done")
        v_turned = sem("v_turned")
        v_copied = sem("v_copied")
        vs_copied = sem("vs_copied")
        kv_out = sem("kv_out")
        out_done = sem("out_done")
        glu_done = sem("glu_done")
        tap_made = sem("tap_made")
        tap_added = sem("tap_added")
        tapped = sem("tapped")
        conv_done = sem("conv_done")
        centred = sem("centred")
        ln_scaled = sem("ln_scaled")
        ln_done = sem("ln_done")
        dve_self = sem("dve_self")
        in_kt, in_vt = sem("in_kt"), sem("in_vt")
        x_in = [sem(f"x_in{i}") for i in range(2)]
        k_page_full = [sem(f"k_page_full{s}") for s in range(5)]
        v_page_full = [sem(f"v_page_full{s}") for s in range(7)]
        q_turned, q_copied, q_stored = sem("q_turned"), sem("q_copied"), sem("q_stored")
        qb_full = [sem(f"qb_full{s}") for s in range(2)]
        v_page_used = sem("v_page_used")
        scores_done = sem("scores_done")
        max_done = sem("max_done")
        exp_done = sem("exp_done")
        a_done = sem("a_done")
        aT_done = sem("aT_done")
        aT_copied = sem("aT_copied")
        o_done = sem("o_done")
        o_squared = sem("o_squared")
        o_stat, o_var, o_inv, o_spread = sem("o_stat"), sem("o_var"), sem("o_inv"), sem("o_spread")
        o_normed = sem("o_normed")
        o_hi_made = sem("o_hi_made")
        o_lo_made = sem("o_lo_made")
        kprod_done = sem("kprod_done")
        kred_done = sem("kred_done")
        d_new, d_scores, d_max, d_exp, d_weights = (sem(n) for n in ("d_new", "d_scores", "d_max", "d_exp", "d_weights"))
        d_turned, d_turned_read, d_out, d_squared, d_stat, d_normed = (
            sem(n) for n in ("d_turned", "d_turned_read", "d_out", "d_squared", "d_stat", "d_normed"))
        d_inv, d_spread = sem("d_inv"), sem("d_spread")
        glu_pad = sem("glu_pad")
        win_done = sem("win_done")
        final_done = sem("final_done")

        N_IN = 16 * 4
        N_KV_OUT = 16 * (2 * KD + 1)
        N_OUT = 16 * (KD + 2)
        block = ctx.enter_context(nc.Block())

        def groups(engine, ph, body, first=False, last=False):
            a, b = int(first), ph.groups - int(last)
            if ph.groups <= 2:
                a = b = ph.groups
                for g in range(a):
                    body(g)
                return
            if first:
                body(0)
            with engine.Fori(a, b) as g:
                body(g)
            if last:
                body(ph.groups - 1)

        def wait_then_address(engine, semaphore, value):
            engine.wait_ge(semaphore, value)
            if not isinstance(value, int):
                engine.wait_ge(inputs, N_IN)

        def coming(ph, g, c):
            if c < 2:
                return ph, g, c + 2
            if isinstance(g, int) and g == ph.groups - 1:
                return (ph.next, 0, c - 2) if ph.next else None
            return ph, g + 1, c - 2

        def col(name, i):
            at = VEC[name] + i
            return vec[:, at:at + 1] if isinstance(at, int) else vec[:, bass.ds(at, 1)]

        def at(tensor, m):
            return tensor[:, m, :] if isinstance(m, int) else tensor[:, bass.ds(m, 1), :].rearrange("p a t -> p (a t)")

        def gain(s, k):
            name, i = (("ffn", 0), ("mix", 0), ("ffn", 1), ("kv", 0), ("ffn", 2), ("mix", 1), ("ffn", 3))[s]
            return col(name, KD * i + k)

        SET_AFTER = {("down", 0): 1, ("conv_out", 0): 2, ("down", 1): 3, ("down", 2): 5, ("o", 0): 6, ("down", 3): None}
        SUMS_BEFORE = {("down", 0): KD, ("conv_out", 0): 2 * KD, ("down", 1): 3 * KD, ("down", 2): 4 * KD,
                       ("o", 0): 5 * KD, ("down", 3): 6 * KD}
        POOL_TAPS = CW - DVE_TAPS
        Q0 = KIND["q"][0].unit0
        K0 = KIND["k"][0].unit0
        V0 = KIND["v"][0].unit0
        STEPS = HEADS * (SEQ // P)

        BLOCKS = tuple(s * HALF + at for s in range(2) for at in (0, P, HALF - P))

        def fresh(ph):
            return ph.kind in ("up", "conv_in", "k", "q") and not (ph.kind == "up" and ph.j == 2)

        @block.sync
        def _(sp):
            def load_chunk(ph, g, c):
                n = ph.chunk0 + 4 * g + c
                if not (isinstance(n, int) and n < 4):
                    wait_then_address(sp, weights_ready, n - 3)
                dst = raw[:, c, 0:ph.tiles * P].rearrange("p (k c) -> p k c", c=P)
                sp.dma_start(dst, ph.weights(g, c)).then_inc(raw_full[c], 16)

            def page_of(i, cache):
                pg = sp.value_load(pages_s[0:1, i:i + 1], min_val=0, max_val=NPOOL - 1)
                return cache[bass.ds(pg, 1), :, :].rearrange("a t f -> (a t) f")

            def load_page(i):
                if i >= len(K_SLOTS):
                    sp.wait_ge(kprod_done, i - len(K_SLOTS) + 1)
                s = i % len(K_SLOTS)
                sp.dma_start(K_SLOTS[s], page_of(i, cache_k)).then_inc(k_page_full[s], 16)

            def load_q(b):
                if b >= 2:
                    sp.wait_ge(kprod_done, NPG * (b - 1))
                sp.dma_start(qb[:, b % 2, :], q_dram[b:b + 1, :].broadcast_to([P, D])).then_inc(qb_full[b % 2], 16)

            def load_v_page(i):
                if i == 0:
                    sp.wait_ge(kprod_done, NS * NPG)
                if i >= len(V_SLOTS):
                    sp.wait_ge(v_page_used, i - len(V_SLOTS) + 1)
                s = i % len(V_SLOTS)
                sp.dma_start(V_SLOTS[s], page_of(i, cache_v)).then_inc(v_page_full[s], 16)

            first_chunk = phases[0]
            sp.dma_start(vec[:, :], vec_d).then_inc(inputs, 16)
            load_chunk(first_chunk, 0, 0)
            for i in range(2):
                k = slice(i * KD // 2, (i + 1) * KD // 2)
                sp.dma_start(x[:, k, :], xT[:, k, :]).then_inc(x_in[i], 16)
            load_chunk(first_chunk, 0, 1)
            sp.dma_start(cst[:, :], cst_d).then_inc(inputs, 16)
            sp.dma_start(lam_row[0:1, :, :], lam_d).then_inc(inputs, 16)
            sp.dma_start(pages_s[0:1, :], pages).then_inc(inputs, 16)
            load_chunk(first_chunk, 0, 2)
            load_chunk(first_chunk, 0, 3)
            for ph in phases:
                if ph.kind == "o":
                    for c in range(4):
                        load_chunk(ph, 0, c)
                    sp.wait_ge(chunk_used, ph.chunk0)
                    sp.wait_ge(rope_done, 2 * KD)
                    for i in range(NS * NPG):
                        load_page(i)
                        if i == 1:
                            sp.wait_ge(q_stored, 16)
                        if i % NPG == 1:
                            load_q(i // NPG)
                    for i in range(NS * NPG):
                        load_v_page(i)
                    for c in range(4):
                        load_chunk(ph, 1, c)
                elif ph.kind == "conv_in":
                    for g in range(ph.groups):
                        for c in range(4):
                            load_chunk(ph, g, c)
                else:
                    groups(sp, ph, lambda g: [load_chunk(ph, g, c) for c in range(4)
                                              if not (ph is first_chunk and isinstance(g, int))], first=ph is first_chunk)
            sp.wait_ge(kv_out, N_KV_OUT)
            sp.wait_ge(out_done, N_OUT)

        @block.tensor
        def _(pe):
            def chunk(ph, g, c, made=None):
                n = ph.chunk0 + 4 * g + c
                u = ph.unit0 + (4 * g + c if ph.per == 1 else 2 * g + c // 2)
                part = c % ph.per
                slot = c % 2 if ph.per == 1 else c // 2
                pe.wait_ge(weights_ready, n + 1)
                if part == 0 and not (isinstance(u, int) and u < 2):
                    pe.wait_ge(drained, u - 1)
                opening = isinstance(g, int) and g == 0 and c < ph.per and ph.kind != "v"
                for k in range(ph.tiles):
                    if made and k == 2:
                        spread(made)
                    kk = part * ph.tiles + k
                    if ph.kind == "down":
                        hi, lo, need = h_hi[:, kk], h_lo[:, kk], (h_ready, ph.h0 - KF + kk + 1)
                    elif ph.kind == "conv_out":
                        hi, lo, need = h_hi[:, MIX + kk], h_lo[:, MIX + kk], (h_ready, ph.h0 - KD + kk + 1)
                    elif ph.kind == "o":
                        hi, lo, need = h_hi[:, MIX + kk], h_lo[:, MIX + kk], (o_lo_made, HEADS + 1)
                    else:
                        hi, lo, need = xg_hi[:, kk], xg_lo[:, kk], (xg_ready, KD * ph.set + kk + 1)
                    if opening:
                        pe.wait_ge(*need)
                    for i, (w, m) in enumerate(((w_hi, hi), (w_hi, lo), (w_lo, hi))):
                        for s in range(2):
                            mm = nc.tensor.matmul(unit[slot][:, s, :], w[:, c % 2, k * P:(k + 1) * P],
                                                  m[:, s * HALF:(s + 1) * HALF], start=kk == 0 and i == 0,
                                                  stop=kk == ph.per * ph.tiles - 1 and i == 2)
                mm.then_inc(chunk_used, 1)

            def mean(m, src, out):
                for s in range(2):
                    mm = nc.tensor.matmul(out[:, s, :], ones_d[:, :], src[:, s * HALF:(s + 1) * HALF],
                                          start=m == 0, stop=m == KD - 1)
                return mm

            def conv_mean(m):
                pe.wait_ge(conv_done, m + 1)
                return mean(m, conv[:, m, :], ps_rot)

            def layer_norm(made):
                for m in range(KD - 2, KD):
                    mm = conv_mean(m)
                mm.then_inc(mean_done, 1)
                pe.wait_ge(rstd_made, made)
                for m in range(KD):
                    pe.wait_ge(squared, 2 * KD + m + 1)
                    mean(m, sq[:, m % 2, :], ps_stat).then_inc(sq_used, 1)
                pe.wait_ge(acc_copied, 1)
                for i, b in enumerate(BLOCKS):
                    mm = nc.tensor.matmul(ps_all[:, 6, i:i + 1], acc[:, b:b + P], cst[:, C_ID:C_ID + 1], start=True, stop=True)
                mm.then_inc(var_done, 1)
                spread(made + 1)

            def variance(sums, free):
                pe.wait_ge(summed, sums)
                if free:
                    pe.wait_ge(*free)
                for i, b in enumerate(BLOCKS):
                    mm = nc.tensor.matmul(ps_var[:, i:i + 1], acc[:, b:b + P], ones_d[:, 0:1], start=True, stop=True)
                mm.then_inc(var_done, 1)

            def spread(made):
                pe.wait_ge(inv_made, made)
                for i, b in enumerate(BLOCKS):
                    half, at_b = divmod(b, HALF)
                    mm = nc.tensor.matmul(ps_stat[:, half, at_b:at_b + P], inv[:, i:i + 1].broadcast_to([P, P]),
                                          cst[:, C_ID:C_ID + P], start=True, stop=True)
                mm.then_inc(spread_done, 1)

            def rotate(r, u):
                pe.wait_ge(drained, u + 1)
                if r >= 1:
                    pe.wait_ge(sin_done, r)
                for s in range(2):
                    mm = nc.tensor.matmul(ps_rot[:, s, :], cst[:, C_ROT:C_ROT + P],
                                          t_gate[:, r % 2, s * HALF:(s + 1) * HALF], start=True, stop=True)
                mm.then_inc(rot_done, 1)

            def turn_v(m):
                pe.wait_ge(drained, V0 + m + 1)
                if m == 0:
                    pe.wait_ge(sin_done, KD)
                else:
                    pe.wait_ge(v_copied, m)
                for t in range(SEQ // P):
                    mm = nc.tensor.transpose(ps_all[:, 6, t * P:(t + 1) * P], t_gate[:, m % 2, t * P:(t + 1) * P],
                                             cst[:, C_ID:C_ID + P])
                mm.then_inc(v_turned, 1)

            def scores(s):
                h, t = divmod(s, SEQ // P)
                keys = (t + 1) * P
                if s >= 2:
                    pe.wait_ge(exp_done, s - 1)
                for c in range(2):
                    rows = slice(c * HD, (c + 1) * HD)
                    nc.tensor.matmul(ps_all[:, 2 * (s % 2) + c, 0:keys], qT[rows, h, t * P:(t + 1) * P],
                                     kT[rows, h, 0:keys], start=True, stop=False)
                for c in range(2):
                    mm = nc.tensor.matmul(ps_all[:, 2 * (s % 2) + c, keys - P:keys], ident_b[:, :], mask_b[:, :],
                                          start=False, stop=True)
                mm.then_inc(scores_done, 1)

            def turn_a(s):
                pe.wait_ge(a_done, s + 1)
                if s >= 2:
                    pe.wait_ge(aT_copied, s - 1)
                for k in range(s % (SEQ // P) + 1):
                    mm = nc.tensor.transpose(ps_all[:, 4 + s % 2, k * P:(k + 1) * P],
                                             at_n[:, s % 2, k * P:(k + 1) * P], cst[:, C_ID:C_ID + P])
                mm.then_inc(aT_done, 1)

            def values(s):
                h, t = divmod(s, SEQ // P)
                pe.wait_ge(aT_copied, s + 1)
                if t == 0 and h:
                    pe.wait_ge(o_squared, h)
                for k in range(t + 1):
                    mm = nc.tensor.matmul(ps_all[:, 6, t * P:(t + 1) * P], vT[:, k, h * P:(h + 1) * P],
                                          aT[:, s % 2, k * P:(k + 1) * P], start=k == 0, stop=k == t)
                if t == SEQ // P - 1:
                    mm.then_inc(o_done, 1)

            def head_stat(h):
                pe.wait_ge(o_squared, h + 1)
                if h:
                    pe.wait_ge(o_normed, h)
                for t in range(SEQ // P):
                    mm = nc.tensor.matmul(ps_all[:, 7, t:t + 1], sq[:, 0, t * P:(t + 1) * P], ones_d[:, 0:1], start=True, stop=True)
                mm.then_inc(o_stat, 1)

            def head_spread(h):
                pe.wait_ge(o_inv, h + 1)
                for t in range(SEQ // P):
                    mm = nc.tensor.matmul(ps_all[:, 7, t * P:(t + 1) * P], inv[:, t:t + 1].broadcast_to([P, P]),
                                          cst[:, C_ID:C_ID + P], start=True, stop=True)
                mm.then_inc(o_spread, 1)

            def turn_q():
                for h in range(HEADS):
                    mm = nc.tensor.transpose(ps_all[0:NS, 4 + h // 4, h % 4 * P:(h % 4 + 1) * P], qT[:, h, SEQ:T],
                                             cst[:, C_ID:C_ID + P])
                mm.then_inc(q_turned, 1)

            def attention():
                pe.wait_ge(rope_done, 2 * KD)
                turn_q()
                pe.wait_ge(drained, Q0 + KD)
                pe.wait_ge(in_kt, 16)
                pe.wait_ge(const_done, 4)
                scores(0)
                scores(1)
                pe.wait_ge(q_copied, 1)
                for s in range(STEPS + 3):
                    if s + 2 < STEPS:
                        scores(s + 2)
                    if s < STEPS:
                        turn_a(s)
                    if 1 <= s <= STEPS:
                        if s == 1:
                            pe.wait_ge(in_vt, 16)
                        values(s - 1)
                    h, t = divmod(s - 5, 4)
                    if t == 0 and 0 <= h < HEADS:
                        head_stat(h)
                    if t == 1 and 0 <= h < HEADS:
                        head_spread(h)
                pe.wait_ge(kred_done, NS * NPG)
                pe.wait_ge(d_new, 3)
                for g in range(NPG):
                    nc.tensor.transpose(ps_all[:, 0, g * P:(g + 1) * P], s_dec[:, g].rearrange("p b j -> p (b j)"),
                                        cst[:, C_ID:C_ID + P])
                nc.tensor.matmul(ps_all[:, 0, PAST:PAST + 1], z_dec[:, :, :, :].rearrange("p b h c -> p (b h c)"),
                                 ones_d[:, 0:1], start=True, stop=True).then_inc(d_scores, 1)
                pe.wait_ge(d_weights, 1)
                for g in range(NPG):
                    nc.tensor.matmul(ps_all[:, 1, g * HD:(g + 1) * HD], p_dec[:, g * P:(g + 1) * P],
                                     cst[:, C_PAIR:C_PAIR + HD], start=True, stop=True)
                nc.tensor.matmul(ps_all[:, 1, 2 * HD:3 * HD], p_dec[:, PAST:PAST + 1].broadcast_to([P, P]),
                                 cst[:, C_PAIR:C_PAIR + HD], start=True, stop=True).then_inc(d_turned, 1)
                pe.wait_ge(d_turned_read, 1)
                for b in range(NS):
                    for g in range(NPG):
                        i = NPG * b + g
                        pe.wait_ge(v_page_full[i % len(V_SLOTS)], 16 * (i // len(V_SLOTS) + 1))
                    for h in range(HEADS):
                        for g in range(NPG):
                            mm = nc.tensor.matmul(ps_all[:, 2, h * NS + b:h * NS + b + 1],
                                                  V_SLOTS[(NPG * b + g) % len(V_SLOTS)][:, h * P:(h + 1) * P],
                                                  at_dec[:, g, b, h:h + 1], start=g == 0, stop=g == NPG - 1)
                    mm.then_inc(v_page_used, NPG)
                pe.wait_ge(d_squared, 1)
                nc.tensor.matmul(ps_all[0:HD, 3, 0:1], kprod[:, 2 * HD:3 * HD], ones_d[:, 0:1], start=True, stop=True
                                 ).then_inc(d_stat, 1)
                pe.wait_ge(d_inv, 2)
                nc.tensor.matmul(ps_all[:, 3, 0:HD], inv[0:HD, 0:1].broadcast_to([HD, P]), cst[0:HD, C_ID:C_ID + HD],
                                 start=True, stop=True).then_inc(d_spread, 1)

            pe.wait_ge(inputs, N_IN)
            sums = 0
            made = 0
            for ph in phases:
                if fresh(ph):
                    sums += KD

                def body(g):
                    for c in range(4):
                        opening = isinstance(g, int) and g == 0
                        chunk(ph, g, c, made + 1 if opening and c == 1 and fresh(ph) else None)
                        r = 4 * g + c - 1
                        if opening and c == 0:
                            if ph is phases[0]:
                                pe.wait_ge(const_done, 2)
                            if fresh(ph):
                                variance(sums, (rstd_made, made) if made else None)
                        elif ph.kind == "k":
                            rotate(r, K0 + r)
                        elif ph.kind == "q":
                            rotate(KD + r, Q0 + r)
                        elif ph.kind == "v" and r >= 0:
                            turn_v(r)
                        if ph.kind == "conv_in" and c % 2 and 2 * g + c // 2 >= 2:
                            conv_mean(2 * g + c // 2 - 2)
                if ph.kind == "conv_in":
                    for g in range(ph.groups):
                        body(g)
                else:
                    groups(pe, ph, body, first=True)
                made += fresh(ph)
                if ph is phases[0]:
                    pe.wait_ge(lam_step, 4)
                    nc.tensor.matmul(ps_all[:, 6, 0:1], ones_d[0:1, :], lam_s[0:1, 4:5], start=True, stop=True
                                     ).then_inc(lam_step, 1)
                if ph.kind == "k":
                    rotate(KD - 1, K0 + KD - 1)
                elif ph.kind == "v":
                    turn_v(KD - 1)
                elif ph.kind == "q":
                    rotate(2 * KD - 1, Q0 + KD - 1)
                    attention()
                elif ph.kind == "conv_in":
                    layer_norm(made)
                    made += 1
            variance(sums + KD, (rstd_made, made))
            spread(made + 1)

        @block.scalar
        def _(act):
            squares = [0]

            def round_hi(ph, g, c):
                n = ph.chunk0 + 4 * g + c
                act.wait_ge(raw_full[c], 16 * (ph.chunk0 // 4 + g + 1))
                if not (isinstance(n, int) and n < 2):
                    act.wait_ge(chunk_used, n - 1)
                w = ph.tiles * P
                nc.scalar.activation(w_hi[:, c % 2, 0:w], raw[:, c, 0:w], ACT.Copy).then_inc(hi_made, 1)

            def ahead(ph, g, c):
                to = coming(ph, g, c)
                if to:
                    round_hi(*to)

            def x_hi(s, m):
                nc.scalar.activation(xg_hi[:, m, :], x[:, m, :], ACT.Copy, scale=gain(s, m)).then_inc(xg_hi_made, 1)

            def square(sums, m, src):
                if not (isinstance(sums + m, int) and sums + m < 2):
                    act.wait_ge(summed, sums + m - 1)
                nc.scalar.activation(sq[:, m % 2, :], src, ACT.Square).then_inc(squared, 1)

            act.wait_ge(inputs, N_IN)
            round_hi(phases[0], 0, 0)
            for m in range(KD):
                if m % (KD // 2) == 0:
                    act.wait_ge(x_in[m // (KD // 2)], 16)
                x_hi(0, m)
            round_hi(phases[0], 0, 1)
            for m in range(KD):
                square(0, m, x[:, m, :])
            nc.scalar.activation(ident_b[:, :], cst[:, C_ID:C_ID + P], ACT.Copy).then_inc(const_done, 1)
            nc.scalar.activation(mask_b[:, :], cst[:, C_MASK:C_MASK + P], ACT.Copy).then_inc(const_done, 1)
            act.wait_ge(lam_step, 2)
            nc.scalar.activation(lam_s[0:1, 2:4], lam_s[0:1, 0:2], ACT.Exp).then_inc(lam_step, 1)
            act.dma_start(new_state_d, state[:, 1:CW - 1, :]).then_inc(out_done, 16)

            def up(ph):
                def body(g):
                    for q in range(2):
                        u, p = ph.unit0 + 4 * g + 2 * q, ph.pair0 + 2 * g + q
                        ahead(ph, g, 2 * q)
                        act.wait_ge(drained, u + 1)
                        nc.scalar.activation(t_act[:, q, :], t_gate[:, q, :], ACT.Silu).then_inc(act_done, 1)
                        ahead(ph, g, 2 * q + 1)
                        wait_then_address(act, drained, u + 2)
                        if isinstance(g, int) and g == 0 and q == 0 and ph.j in (1, 2):
                            if ph.j == 1:
                                act.wait_ge(out_done, 16 * 2)
                            else:
                                act.wait_ge(kv_out, N_KV_OUT)
                        nc.scalar.activation(at(h_hi, 2 * g + q), t_out[:, q, :], ACT.Copy).then_inc(h_hi_made, 1)
                groups(act, ph, body, first=True, last=True)

            def residual(ph):
                key = (ph.kind, ph.j)
                sums = SUMS_BEFORE[key]

                def body(g):
                    for c in range(4):
                        ahead(ph, g, c)
                        if c % ph.per == ph.per - 1:
                            m = (4 * g + c) if ph.per == 1 else 2 * g + c // 2
                            act.wait_ge(summed, sums + m - 1)
                            wait_then_address(act, drained, ph.unit0 + m + 1)
                            if SET_AFTER[key] is not None:
                                nc.scalar.activation(at(xg_hi, m), at(x, m), ACT.Copy, scale=gain(SET_AFTER[key], m)
                                                     ).then_inc(xg_hi_made, 1)
                            slot = (c if ph.per == 1 else c // 2) % 2
                            nc.scalar.activation(sq[:, slot, :], at(x, m), ACT.Square).then_inc(squared, 1)
                groups(act, ph, body, last=True)

            def conv_in(ph):
                def body(g):
                    for q in range(2):
                        m, u = 2 * g + q, ph.unit0 + 4 * g + 2 * q
                        ahead(ph, g, 2 * q)
                        wait_then_address(act, drained, u + 1)
                        nc.scalar.activation(t_act[:, q, :], t_gate[:, q, :], ACT.Sigmoid, bias=col("b_in", KD + m)
                                             ).then_inc(act_done, 1)
                        ahead(ph, g, 2 * q + 1)
                        act.wait_ge(glu_done, m + 1)
                        for i in range(POOL_TAPS):
                            j = DVE_TAPS + i
                            if i >= 3:
                                wait_then_address(act, tap_added, (POOL_TAPS - 1) * m + max(i - 3, 1))
                            elif not (isinstance(m, int) and m == 0):
                                wait_then_address(act, tap_added, (POOL_TAPS - 1) * (m - 1) + max(POOL_TAPS + i - 3, 1))
                            nc.scalar.activation(tap[:, i % 3, :], glu[:, q, j:j + SEQ], ACT.Copy,
                                                 scale=col("dw", KD * j + m)).then_inc(tap_made, 1)
                groups(act, ph, body, first=True, last=True)
                act.wait_ge(summed, 2 * KD)
                for m in range(KD):
                    act.wait_ge(centred, m + 1)
                    if m >= 2:
                        act.wait_ge(sq_used, m - 1)
                    nc.scalar.activation(sq[:, m % 2, :], conv[:, m, :], ACT.Square).then_inc(squared, 1)
                act.dma_start(conv_d, tail[:, :, :]).then_inc(out_done, 16)
                for m in range(KD):
                    act.wait_ge(ln_scaled, m + 1)
                    nc.scalar.activation(t_act[:, m % 2, :], t_gate[:, m % 2, :], ACT.Silu, scale=col("ln_g", m),
                                         bias=col("ln_b", m)).then_inc(ln_done, 1)
                    act.wait_ge(ln_done, m + 1)
                    nc.scalar.activation(h_hi[:, MIX + m, :], t_act[:, m % 2, :], ACT.Copy).then_inc(h_hi_made, 1)

            def rotary(ph):
                for g in range(ph.groups):
                    for c in range(4):
                        ahead(ph, g, c)
                        m = 4 * g + c - 1
                        if ph.kind == "k" and m >= 1:
                            act.wait_ge(rope_done, m)
                            act.dma_start(k_d[:, m - 1, :], k_new[:, m - 1, :]).then_inc(kv_out, 16)
                if ph.kind == "k":
                    for m in (KD - 2, KD - 1):
                        act.wait_ge(rope_done, m + 1)
                        act.dma_start(k_d[:, m, :], k_new[:, m, :]).then_inc(kv_out, 16)

            def store_v(m):
                act.wait_ge(v_turned, m + 1)
                nc.scalar.activation(v_tok[:, m, :], ps_all[:, 6, :], ACT.Copy).then_inc(v_copied, 1)
                act.wait_ge(v_copied, m + 1)
                act.dma_start(v_d[:, m * P:(m + 1) * P].rearrange("(t p) c -> p t c", p=P),
                              v_tok[:, m, :].rearrange("p (t c) -> p t c", c=P)).then_inc(kv_out, 16)

            def v(ph):
                for g in range(ph.groups):
                    for c in range(4):
                        ahead(ph, g, c)
                        if 4 * g + c >= 1:
                            store_v(4 * g + c - 1)
                act.wait_ge(chunk_used, ph.chunk0 + ph.chunks)
                for m in range(KD):
                    x_hi(4, m)
                store_v(KD - 1)
                act.wait_ge(vs_copied, KD)
                act.dma_start(vs_d, v_s[:, :, :]).then_inc(kv_out, 16)

            def attention():
                def exps(s):
                    keys = (s % 4 + 1) * P
                    act.wait_ge(max_done, s + 1)
                    if s >= 2:
                        act.wait_ge(a_done, s - 1)
                    for c in range(2):
                        e = nc.scalar.activation(pr[:, s % 2, c, 0:keys], ps_all[:, 2 * (s % 2) + c, 0:keys], ACT.Exp,
                                                 scale=SCALE, bias=nmx[:, s % 2, c:c + 1],
                                                 accum_out=lsum[:, s % 2, c:c + 1])
                    e.then_inc(exp_done, 1)

                act.wait_ge(q_turned, 1)
                nc.scalar.activation(kprod[0:NS, :].rearrange("p (a c) -> p a c", a=2), ps_all[0:NS, 4:6, :], ACT.Copy
                                     ).then_inc(q_copied, 1)
                act.wait_ge(q_copied, 1)
                act.dma_start(q_dram, kprod[0:NS, :]).then_inc(q_stored, 16)
                exps(0)
                for s in range(STEPS + 5):
                    if s + 1 < STEPS:
                        exps(s + 1)
                    if s < STEPS:
                        keys = (s % 4 + 1) * P
                        act.wait_ge(aT_done, s + 1)
                        nc.scalar.activation(aT[:, s % 2, 0:keys], ps_all[:, 4 + s % 2, 0:keys], ACT.Copy
                                             ).then_inc(aT_copied, 1)
                    h, t = divmod(s - 8, 4)
                    if t == 0 and 0 <= h < HEADS:
                        act.wait_ge(o_normed, h + 1)
                        nc.scalar.activation(h_hi[:, MIX + h, 0:SEQ], sq[:, 1, 0:SEQ], ACT.Copy, scale=sub_g[:, 0:1]
                                             ).then_inc(o_hi_made, 1)
                    h, t = divmod(s - 4, 4)
                    if t == 0 and 0 <= h < HEADS:
                        act.wait_ge(o_done, h + 1)
                        nc.scalar.activation(acc[:, 0:SEQ], ps_all[:, 6, :], ACT.Copy)
                        nc.scalar.activation(sq[:, 0, 0:SEQ], ps_all[:, 6, :], ACT.Square).then_inc(o_squared, 1)
                act.wait_ge(d_max, 2)
                nc.scalar.activation(p_dec[:, :], ps_all[:, 0, 0:PAST + 1], ACT.Exp, scale=SCALE, bias=mx_s[:, 1:2],
                                     accum_out=mx_s[:, 2:3]).then_inc(d_exp, 1)
                act.wait_ge(d_out, 2)
                nc.scalar.activation(kprod[:, 2 * HD:3 * HD], kprod[:, HD:2 * HD], ACT.Square).then_inc(d_squared, 1)
                act.wait_ge(d_normed, 1)
                nc.scalar.activation(h_hi[:, MIX:KF, SEQ:T], kprod[:, 4 * HD:5 * HD].rearrange("p (h b) -> p h b", h=HEADS),
                                     ACT.Copy, scale=sub_g[:, 0:1]).then_inc(o_hi_made, 1)

            for ph in phases:
                if ph.kind == "up":
                    up(ph)
                elif ph.kind == "conv_in":
                    conv_in(ph)
                elif ph.kind in ("k", "q"):
                    rotary(ph)
                    if ph.kind == "q":
                        attention()
                elif ph.kind == "v":
                    v(ph)
                else:
                    residual(ph)
            for m in range(KD):
                act.wait_ge(final_done, m + 1)
                act.dma_start(y_d[:, m, :], x[:, m, :]).then_inc(out_done, 16)

        @block.vector
        def _(dve):
            own = [0]

            def link(instruction):
                own[0] += 1
                instruction.then_inc(dve_self, 1)
                dve.wait_ge(dve_self, own[0])

            made = [0]

            def split_lo(ph, g, c):
                n = ph.chunk0 + 4 * g + c
                dve.wait_ge(hi_made, n + 1)
                w = ph.tiles * P
                nc.vector.tensor_tensor(w_lo[:, c % 2, 0:w], raw[:, c, 0:w], w_hi[:, c % 2, 0:w], ALU.subtract
                                        ).then_inc(weights_ready, 1)

            def ahead(ph, g, c):
                to = coming(ph, g, c)
                if to:
                    split_lo(*to)

            def x_lo(s, m):
                dve.wait_ge(xg_hi_made, KD * s + m + 1)
                nc.vector.scalar_tensor_tensor(at(xg_lo, m), at(x, m), gain(s, m), at(xg_hi, m), ALU.mult, ALU.subtract
                                               ).then_inc(xg_ready, 1)

            def rms(squares=ps_var):
                made[0] += 1
                dve.wait_ge(var_done, made[0])
                nc.vector.tensor_scalar(var[:, :], squares, EPS, None, ALU.add).then_inc(var_read, 1)
                dve.wait_ge(spread_done, made[0])
                nc.vector.tensor_copy(halves(rstd[:, :]), ps_stat).then_inc(rstd_made, 1)
                dve.wait_ge(rstd_made, made[0])

            def scaled(out, slot):
                return nc.vector.tensor_tensor(halves(out), unit[slot], halves(rstd[:, :]), ALU.mult)

            dve.wait_ge(inputs, N_IN)
            split_lo(phases[0], 0, 0)
            for m in range(KD):
                x_lo(0, m)
            split_lo(phases[0], 0, 1)
            nc.vector.tensor_tensor(lam_prod[0:1, :, :], lam_row[0:1, 0:4:2, :], lam_row[0:1, 1:4:2, :], ALU.mult
                                    ).then_inc(lam_step, 1)
            dve.wait_ge(lam_step, 1)
            nc.vector.tensor_reduce(lam_s[0:1, 0:2], lam_prod[0:1, :, :], AX.X, ALU.add).then_inc(lam_step, 1)
            dve.wait_ge(lam_step, 3)
            nc.vector.tensor_scalar(lam_s[0:1, 4:5], lam_s[0:1, 3:4], lam_s[0:1, 2:3], LAM_INIT, ALU.subtract, ALU.subtract
                                    ).then_inc(lam_step, 1)
            nc.vector.tensor_scalar(sub_g[:, :], col("sub", 0), 1.0 - LAM_INIT, None, ALU.mult)

            def spread_lambda():
                dve.wait_ge(lam_step, 5)
                link(nc.vector.tensor_scalar(neglam[:, :], ps_all[:, 6, 0:1], float(D), None, ALU.mult))
                nc.vector.scalar_tensor_tensor(pairco[:, :], cst[:, C_ODD:C_ODD + 1], neglam[:, :], cst[:, C_EVEN:C_EVEN + 1],
                                               ALU.mult, ALU.add)

            def up(ph):
                def body(g):
                    for q in range(2):
                        n, p = ph.chunk0 + 4 * g + 2 * q, ph.pair0 + 2 * g + q
                        dve.wait_ge(chunk_used, n + 1)
                        scaled(t_gate[:, q, :], 0).then_inc(drained, 1)
                        ahead(ph, g, 2 * q)
                        dve.wait_ge(chunk_used, n + 2)
                        dve.wait_ge(act_scaled, p + 1 - KD * (ph.j > 0))
                        nc.vector.tensor_tensor(halves(t_out[:, q, :]), unit[1], halves(t_gate[:, q, :]), ALU.mult
                                                ).then_inc(drained, 1)
                        ahead(ph, g, 2 * q + 1)
                groups(dve, ph, body, last=True)

            def residual(ph):
                s = SET_AFTER[ph.kind, ph.j]

                def body(g):
                    for c in range(4):
                        last = c % ph.per == ph.per - 1
                        m = (4 * g + c) if ph.per == 1 else 2 * g + c // 2
                        slot = (c if ph.per == 1 else c // 2) % 2
                        dve.wait_ge(chunk_used, ph.chunk0 + 4 * g + c + 1)
                        if last:
                            op, by = {"down": (ALU.mult, 0.5), "o": (ALU.mult, 1.0)}.get(ph.kind) or (ALU.add, col("b_out", m))
                            xm = halves(at(x, m))
                            nc.vector.scalar_tensor_tensor(xm, unit[slot], by, xm, op, ALU.add).then_inc(drained, 1)
                        ahead(ph, g, c)
                        if last and s is not None:
                            x_lo(s, m)
                groups(dve, ph, body, last=True)

            def taps(m, q):
                chains = (conv[:, m, 0:SEQ] if isinstance(m, int) else conv[:, bass.ds(m, 1), 0:SEQ].rearrange("p a t -> p (a t)"),
                          conv_b[:, :])
                for j in range(DVE_TAPS):
                    src = glu[:, q, j:j + SEQ]
                    w = col("dw", KD * j + m)
                    out = chains[j % 2]
                    if j == 0:
                        i = nc.vector.tensor_scalar(out, src, w, col("dw_b", m), ALU.mult, ALU.add)
                    elif j == 1:
                        i = nc.vector.tensor_scalar(out, src, w, None, ALU.mult)
                    else:
                        dve.wait_ge(tapped, DVE_TAPS * m + j - 1)
                        i = nc.vector.scalar_tensor_tensor(out, src, w, out, ALU.mult, ALU.add)
                    i.then_inc(tapped, 1)
                return chains

            def conv_in(ph):
                nc.vector.memset(glu[:, :, 0:CW - 1], 0.0).then_inc(glu_pad, 1)
                dve.wait_ge(glu_pad, 1)

                def body(g):
                    for q in range(2):
                        n, m, p = ph.chunk0 + 4 * g + 2 * q, 2 * g + q, ph.pair0 + 2 * g + q
                        dve.wait_ge(chunk_used, n + 1)
                        scaled(t_gate[:, q, :], 0).then_inc(drained, 1)
                        ahead(ph, g, 2 * q)
                        dve.wait_ge(chunk_used, n + 2)
                        scaled(t_out[:, q, :], 1).then_inc(drained, 1)
                        dve.wait_ge(drained, ph.unit0 + 4 * g + 2 * q + 2)
                        dve.wait_ge(act_done, p + 1)
                        nc.vector.scalar_tensor_tensor(glu[:, q, CW - 1:CW - 1 + T], t_out[:, q, :], col("b_in", m), t_act[:, q, :],
                                                       ALU.add, ALU.mult).then_inc(glu_done, 1)
                        ahead(ph, g, 2 * q + 1)
                        dve.wait_ge(glu_done, m + 1)
                        a, b = taps(m, q)
                        nc.vector.tensor_copy(at(tail, m), glu[:, q, SEQ:CW - 1 + T])
                        win = window[:, m] if isinstance(m, int) else window[:, bass.ds(m, 1)].rearrange("p a j b -> p (a j) b")
                        nc.vector.tensor_copy(win[:, CW - 1, :], glu[:, q, CW - 1 + SEQ:CW - 1 + T]).then_inc(win_done, 2)
                        dve.wait_ge(win_done, 4 * m + 2)
                        w = vec[:, VEC["dw"] + m:VEC["dw"] + m + KD * (CW - 1) + 1:KD] if isinstance(m, int) else \
                            vec[:, bass.ds(VEC["dw"] + m, CW, KD)]
                        nc.vector.tensor_tensor(swin[:, :, :], win, w.unsqueeze(2).broadcast_to([P, CW, NS]), ALU.mult
                                                ).then_inc(win_done, 1)
                        dve.wait_ge(tapped, DVE_TAPS * (m + 1))
                        dve.wait_ge(win_done, 4 * m + 3)
                        nc.vector.tensor_tensor(a, a, b, ALU.add)
                        cs = conv[:, m, SEQ:T] if isinstance(m, int) else conv[:, bass.ds(m, 1), SEQ:T].rearrange("p a t -> p (a t)")
                        nc.vector.tensor_reduce(cs, swin[:, :, :].rearrange("p j b -> p b j"), AX.X, ALU.add).then_inc(win_done, 1)
                        dve.wait_ge(win_done, 4 * m + 4)
                        dve.wait_ge(tap_added, (POOL_TAPS - 1) * (m + 1))
                        nc.vector.tensor_scalar(cs, cs, col("dw_b", m), None, ALU.add)
                        nc.vector.tensor_tensor(a, a, conv_p[:, q, :], ALU.add).then_inc(conv_done, 1)
                dve.wait_ge(in_state, 16)
                groups(dve, ph, body, last=True)
                dve.wait_ge(mean_done, 1)
                for m in range(KD):
                    cm = halves(conv[:, m, :])
                    nc.vector.tensor_tensor(cm, cm, ps_rot, ALU.subtract).then_inc(centred, 1)
                dve.wait_ge(sq_used, KD)
                nc.vector.tensor_copy(halves(acc[:, :]), ps_stat).then_inc(acc_copied, 1)
                rms(ps_all[:, 6, 0:6])

                def lo(m):
                    dve.wait_ge(h_hi_made, ph.h0 + m + 1)
                    nc.vector.tensor_tensor(h_lo[:, MIX + m, :], t_act[:, m % 2, :], h_hi[:, MIX + m, :], ALU.subtract
                                            ).then_inc(h_ready, 1)
                for m in range(KD):
                    nc.vector.tensor_tensor(t_gate[:, m % 2, :], conv[:, m, :], rstd[:, :], ALU.mult).then_inc(ln_scaled, 1)
                    if m:
                        lo(m - 1)
                lo(KD - 1)

            def rotary(ph):
                r0 = 0 if ph.kind == "k" else KD
                cs = cs_k if ph.kind == "k" else cs_q

                def sine(r):
                    dve.wait_ge(rot_done, r + 1)
                    nc.vector.tensor_tensor(halves(t_out[:, r % 2, :]), ps_rot, halves(cs[:, 1, :]), ALU.mult
                                            ).then_inc(sin_done, 1)
                for g in range(ph.groups):
                    for c in range(4):
                        r = r0 + 4 * g + c
                        dve.wait_ge(chunk_used, ph.chunk0 + 4 * g + c + 1)
                        if r >= 2:
                            dve.wait_ge(rope_done, r - 1)
                        scaled(t_gate[:, r % 2, :], c % 2).then_inc(drained, 1)
                        ahead(ph, g, c)
                        if r == r0:
                            dve.wait_ge(in_rope[ph.kind == "q"], 16)
                        else:
                            sine(r - 1)
                sine(r0 + KD - 1)

            def v(ph):
                for g in range(ph.groups):
                    for c in range(4):
                        m = 4 * g + c
                        dve.wait_ge(chunk_used, ph.chunk0 + m + 1)
                        if m < 2:
                            dve.wait_ge(rope_done, KD - 1 + m)
                        else:
                            dve.wait_ge(v_turned, m - 1)
                            dve.wait_ge(vs_copied, m - 1)
                        scaled(t_gate[:, m % 2, :], m % 2).then_inc(drained, 1)
                        ahead(ph, g, c)
                for m in range(KD):
                    x_lo(4, m)
                dve.wait_ge(v_turned, KD)
                dve.wait_ge(vs_copied, KD)

            def attention():
                def maxima(s):
                    keys = (s % 4 + 1) * P
                    dve.wait_ge(scores_done, s + 1)
                    link(nc.vector.tensor_reduce(mx[:, s % 2, :], ps_all[:, 2 * (s % 2):2 * (s % 2) + 2, 0:keys], AX.X, ALU.max))
                    nc.vector.tensor_scalar(nmx[:, s % 2, :], mx[:, s % 2, :], -SCALE, None, ALU.mult).then_inc(max_done, 1)

                def combine(s):
                    e, keys = s % 2, (s % 4 + 1) * P
                    dve.wait_ge(exp_done, s + 1)
                    link(nc.vector.reciprocal(rl[:, e, :], lsum[:, e, :]))
                    link(nc.vector.tensor_tensor(rl2[:, e:e + 1], rl[:, e, 1:2], neglam[:, :], ALU.mult))
                    link(nc.vector.tensor_scalar(pr[:, e, 1, 0:keys], pr[:, e, 1, 0:keys], rl2[:, e:e + 1], None, ALU.mult))
                    if s >= 2:
                        dve.wait_ge(aT_done, s - 1)
                    nc.vector.scalar_tensor_tensor(at_n[:, e, 0:keys], pr[:, e, 0, 0:keys], rl[:, e, 0:1], pr[:, e, 1, 0:keys],
                                                   ALU.mult, ALU.add).then_inc(a_done, 1)

                maxima(0)
                maxima(1)
                for s in range(STEPS + 6):
                    if s < STEPS:
                        combine(s)
                    if s + 2 < STEPS:
                        maxima(s + 2)
                    h, t = divmod(s - 6, 4)
                    if t == 0 and 0 <= h < HEADS:
                        dve.wait_ge(o_stat, h + 1)
                        nc.vector.tensor_scalar(var[:, 0:SEQ // P], ps_all[:, 7, 0:SEQ // P], D / P, EPS, ALU.mult, ALU.add).then_inc(o_var, 1)
                    if t == 1 and 0 <= h < HEADS:
                        dve.wait_ge(o_spread, h + 1)
                        nc.vector.tensor_tensor(sq[:, 1, 0:SEQ], ps_all[:, 7, :], acc[:, 0:SEQ], ALU.mult).then_inc(o_normed, 1)
                    h, t = divmod(s - 9, 4)
                    if t == 0 and 0 <= h < HEADS:
                        dve.wait_ge(o_hi_made, h + 1)
                        nc.vector.scalar_tensor_tensor(h_lo[:, MIX + h, 0:SEQ], sq[:, 1, 0:SEQ], sub_g[:, 0:1], h_hi[:, MIX + h, 0:SEQ],
                                                       ALU.mult, ALU.subtract).then_inc(o_lo_made, 1)
                    if 4 <= s < 4 + NS * NPG:
                        b, g = divmod(s - 4, NPG)
                        dve.wait_ge(kprod_done, s - 3)
                        nc.vector.tensor_reduce(s_dec[:, g, b, :], kprod[:, :].rearrange("p (j d) -> p j d", d=HD), AX.X,
                                                ALU.add).then_inc(kred_done, 1)
                nc.vector.memset(z_dec[:, :, :, :], 0.0).then_inc(d_new, 1)
                dve.wait_ge(d_new, 1)
                for c in range(2):
                    rows = slice(c * HD, (c + 1) * HD)
                    nc.vector.scalar_tensor_tensor(z_dec[rows, :, :, c].rearrange("p b h -> p h b"), qT[rows, :, SEQ:T], float(D),
                                                   kT[rows, :, SEQ:T], ALU.mult, ALU.mult).then_inc(d_new, 1)
                dve.wait_ge(d_scores, 1)
                nc.vector.tensor_reduce(mx_s[:, 0:1], ps_all[:, 0, 0:PAST + 1], AX.X, ALU.max).then_inc(d_max, 1)
                dve.wait_ge(d_max, 1)
                nc.vector.tensor_scalar(mx_s[:, 1:2], mx_s[:, 0:1], -SCALE, None, ALU.mult).then_inc(d_max, 1)
                dve.wait_ge(d_exp, 1)
                link(nc.vector.reciprocal(rl2[:, 0:1], mx_s[:, 2:3]))
                link(nc.vector.tensor_tensor(rl2[:, 1:2], rl2[:, 0:1], pairco[:, :], ALU.mult))
                nc.vector.tensor_scalar(p_dec[:, :], p_dec[:, :], rl2[:, 1:2], None, ALU.mult).then_inc(d_weights, 1)
                dve.wait_ge(d_turned, 1)
                link(nc.vector.tensor_copy(an_dec[:, :, :], ps_all[:, 1, 2 * HD:3 * HD].rearrange("p (b h) -> p b h", b=NS)))
                nc.vector.tensor_copy(at_dec[:, :, :, :].rearrange("p g b h -> p (g b h)"), ps_all[:, 1, 0:2 * HD]).then_inc(d_turned_read, 1)
                nc.vector.tensor_tensor(kprod[:, 0:HD].rearrange("p (h b) -> p h b", h=HEADS), an_dec[:, :, :].rearrange("p b h -> p h b"),
                                        v_s[:, :, :], ALU.mult).then_inc(d_out, 1)
                dve.wait_ge(v_page_used, NS * NPG)
                dve.wait_ge(d_out, 1)
                nc.vector.tensor_tensor(kprod[:, HD:2 * HD], ps_all[:, 2, 0:HD], kprod[:, 0:HD], ALU.add).then_inc(d_out, 1)
                dve.wait_ge(d_stat, 1)
                nc.vector.tensor_scalar(var[0:HD, 0:1], ps_all[0:HD, 3, 0:1], D / P, EPS, ALU.mult, ALU.add).then_inc(d_inv, 1)
                dve.wait_ge(d_spread, 1)
                nc.vector.tensor_tensor(kprod[:, 4 * HD:5 * HD], ps_all[:, 3, 0:HD], kprod[:, HD:2 * HD], ALU.mult).then_inc(d_normed, 1)
                dve.wait_ge(o_hi_made, HEADS + 1)
                nc.vector.scalar_tensor_tensor(h_lo[:, MIX:KF, SEQ:T], kprod[:, 4 * HD:5 * HD].rearrange("p (h b) -> p h b", h=HEADS),
                                               sub_g[:, 0:1], h_hi[:, MIX:KF, SEQ:T], ALU.mult, ALU.subtract).then_inc(o_lo_made, 1)

            for ph in phases:
                if fresh(ph):
                    rms()
                if ph.kind == "up":
                    up(ph)
                    if ph is phases[0]:
                        spread_lambda()
                elif ph.kind == "conv_in":
                    conv_in(ph)
                elif ph.kind in ("k", "q"):
                    rotary(ph)
                    if ph.kind == "q":
                        attention()
                elif ph.kind == "v":
                    v(ph)
                else:
                    residual(ph)
            rms()
            for m in range(KD):
                nc.vector.scalar_tensor_tensor(x[:, m, :], x[:, m, :], col("final", m), rstd[:, :], ALU.mult, ALU.mult
                                               ).then_inc(final_done, 1)

        @block.gpsimd
        def _(pool):
            nc.gpsimd.memset(ones_d[:, :], 1.0 / D).then_inc(const_done, 1)
            nc.gpsimd.memset(minus_half[:, :], -0.5).then_inc(const_done, 1)
            sums, squares = [0], [0]

            def add_tile(m, src):
                if m == 0:
                    i = nc.gpsimd.tensor_copy(acc[:, :], src)
                else:
                    pool.wait_ge(summed, sums[0])
                    i = nc.gpsimd.tensor_tensor(acc[:, :], acc[:, :], src, ALU.add)
                i.then_inc(summed, 1)
                sums[0] += 1

            def add_squares():
                for m in range(KD):
                    squares[0] += 1
                    pool.wait_ge(squared, squares[0])
                    add_tile(m, sq[:, m % 2, :])

            def up(ph):
                def body(g):
                    for q in range(2):
                        p = ph.pair0 + 2 * g + q
                        pool.wait_ge(act_done, p + 1)
                        nc.gpsimd.tensor_tensor(t_gate[:, q, :], t_act[:, q, :], rstd[:, :], ALU.mult).then_inc(act_scaled, 1)
                        pool.wait_ge(h_hi_made, ph.h0 + 2 * g + q + 1)
                        nc.gpsimd.tensor_tensor(at(h_lo, 2 * g + q), t_out[:, q, :], at(h_hi, 2 * g + q), ALU.subtract
                                                ).then_inc(h_ready, 1)
                groups(pool, ph, body)

            def load_for(ph):
                if ph.kind in ("conv_in", "k", "q"):
                    pool.wait_ge(chunk_used, ph.chunk0)
                if ph.kind == "conv_in":
                    pool.dma_start(window[:, :, 0:CW - 1, :], stateT).then_inc(in_state, 16)
                elif ph.kind == "k":
                    pool.dma_start(cs_k[:, :, :], rope_d).then_inc(in_rope[0], 16)
                elif ph.kind == "q":
                    pool.dma_start(cs_q[:, :, :], rope_d).then_inc(in_rope[1], 16)
                    pool.wait_ge(kv_out, N_KV_OUT)
                    pool.dma_start(kT[:, :, :], k_d).then_inc(in_kt, 16)

            def conv_in(ph):
                for m in range(KD):
                    for i in range(1, POOL_TAPS):
                        pool.wait_ge(tap_made, POOL_TAPS * m + i + 1)
                        if i == 1:
                            s = nc.gpsimd.tensor_tensor(conv_p[:, m % 2, :], tap[:, 0, :], tap[:, 1, :], ALU.add)
                        else:
                            pool.wait_ge(tap_added, (POOL_TAPS - 1) * m + i - 1)
                            s = nc.gpsimd.tensor_tensor(conv_p[:, m % 2, :], conv_p[:, m % 2, :], tap[:, i % 3, :], ALU.add)
                        s.then_inc(tap_added, 1)
                squares[0] += KD
                rms()

            def rotary(ph):
                r0, u0 = (0, K0) if ph.kind == "k" else (KD, Q0)
                cs, out = (cs_k, k_new) if ph.kind == "k" else (cs_q, qT)

                def both(r):
                    pool.wait_ge(sin_done, r + 1)
                    pool.wait_ge(cos_done, r + 1)
                    nc.gpsimd.tensor_tensor(out[:, r - r0, :], t_act[:, r % 2, :], t_out[:, r % 2, :], ALU.add
                                            ).then_inc(rope_done, 1)
                pool.wait_ge(in_rope[ph.kind == "q"], 16)
                for r in range(r0, r0 + KD):
                    pool.wait_ge(drained, u0 + r - r0 + 1)
                    nc.gpsimd.tensor_tensor(t_act[:, r % 2, :], t_gate[:, r % 2, :], cs[:, 0, :], ALU.mult).then_inc(cos_done, 1)
                    if r > r0:
                        both(r - 1)
                both(r0 + KD - 1)

            def attention():
                pool.wait_ge(chunk_used, KIND["o"][0].chunk0)
                pool.dma_start(vT[:, :, :], v_d.rearrange("(t p) f -> p t f", p=P)).then_inc(in_vt, 16)

                def head_power(h):
                    pool.wait_ge(o_var, h + 1)
                    power(SEQ // P).then_inc(o_inv, 1)

                for i in range(NS * NPG):
                    b = i // NPG
                    pool.wait_ge(k_page_full[i % len(K_SLOTS)], 16 * (i // len(K_SLOTS) + 1))
                    if i % NPG == 0:
                        pool.wait_ge(qb_full[b % 2], 16 * (b // 2 + 1))
                    if i:
                        pool.wait_ge(kred_done, i)
                    nc.gpsimd.tensor_tensor(kprod[:, :], K_SLOTS[i % len(K_SLOTS)], qb[:, b % 2, :], ALU.mult
                                            ).then_inc(kprod_done, 1)
                    if i % 4 == 2:
                        head_power(i // 4)
                for h in range(NS * NPG // 4, HEADS):
                    head_power(h)
                pool.wait_ge(d_inv, 1)
                power(1, HD).then_inc(d_inv, 1)

            def power(n, rows=P):
                return nc.gpsimd.tensor_tensor(inv[0:rows, 0:n], var[0:rows, 0:n], minus_half[0:rows, 0:n], ALU.pow)

            made = [0]

            def rms():
                made[0] += 1
                pool.wait_ge(var_read, made[0])
                power(len(BLOCKS)).then_inc(inv_made, 1)

            add_squares()
            for ph in phases:
                load_for(ph)
                if fresh(ph):
                    rms()
                if ph.kind == "up":
                    up(ph)
                elif ph.kind == "conv_in":
                    conv_in(ph)
                elif ph.kind in ("k", "q"):
                    rotary(ph)
                    if ph.kind == "q":
                        attention()
                elif ph.kind == "v":
                    for m in range(KD):
                        pool.wait_ge(drained, V0 + m + 1)
                        nc.gpsimd.tensor_copy(v_s[:, m, :], t_gate[:, m % 2, SEQ:T]).then_inc(vs_copied, 1)
                else:
                    add_squares()
            rms()


def kernel(**inputs):
    import concourse.bacc as bacc
    from concourse.bass_utils import run_bass_kernel_spmd

    a = {k: np.ascontiguousarray(v) for k, v in inputs.items()}

    def features(t):
        return np.ascontiguousarray(t.reshape(-1, KD, P).transpose(2, 1, 0))

    f32 = np.float32
    rows = np.concatenate([a[n].reshape(-1, P) for n in (
        "norm_ffn", "norm_mix", "kv_norm", "norm_final", "conv_b_in", "conv_dw", "conv_dw_b", "conv_ln_g", "conv_ln_b",
        "conv_b_out", "subln_g")])
    i = np.arange(P)
    rot = (i[:, None] == (i ^ (HD // 2))[None, :]).astype(f32)
    cst = np.concatenate([np.eye(P, dtype=f32), rot, np.where(i[None, :] > i[:, None], NEG, 0.0).astype(f32),
                          (i[:, None] // 2 == np.arange(HD)[None, :]).astype(f32),
                          (i[:, None] % 2 == 0).astype(f32), (i[:, None] % 2 == 1).astype(f32)], axis=1)
    pos = np.concatenate([np.arange(SEQ), np.full(NS, PAST)]).astype(f32)
    freqs = (f32(10000.0) ** (-np.arange(HD // 2, dtype=f32) * f32(2.0) / f32(HD))).astype(f32)
    ang = freqs[i % (HD // 2)][:, None] * pos[None, :]
    sign = np.where(i % HD < HD // 2, -1.0, 1.0).astype(f32)[:, None]
    rope = np.stack([np.cos(ang), sign * np.sin(ang)], axis=1).astype(f32)

    ins = {
        "xT": features(np.concatenate([a["x_prompt"].reshape(SEQ, D), a["x_sample"].reshape(NS, D)])),
        "vec": np.ascontiguousarray(rows.T),
        "cst": np.ascontiguousarray(cst),
        "rope": np.ascontiguousarray(rope),
        "lam": np.concatenate([a[n] for n in ("lambda_q1", "lambda_k1", "lambda_q2", "lambda_k2")]).reshape(1, 4, HD),
        "stateT": np.ascontiguousarray(a["state_conv"][0].reshape(NS, CW - 1, KD, P).transpose(3, 2, 1, 0)),
        "state": a["state_conv"][0],
        "cache_k": a["cache_k"].reshape(NPOOL, PAGE, D),
        "cache_v": a["cache_v"].reshape(NPOOL, PAGE, D),
        "pages": a["page_table"].reshape(1, NS * NPG),
        "w_in": a["ffn_w_in"], "w_out": a["ffn_w_out"], "c_in": a["conv_w_in"], "c_out": a["conv_w_out"],
        "w_kv": a["w_kv"], "w_q": a["w_q"], "w_o": a["w_o"],
    }
    outs = {"y": (P, KD, T), "conv_tail": (P, KD, CW - 1 + NS), "new_state": (NS, CW - 2, D), "k_new_out": (P, KD, T),
            "v_new_out": (SEQ, D), "v_new_s": (P, KD, NS)}
    nc = bacc.Bacc("TRN2", target_bir_lowering=False, num_devices=1)
    args = [nc.dram_tensor(n, v.shape, mybir.dt.from_np(v.dtype), kind="ExternalInput").ap() for n, v in ins.items()]
    args += [nc.dram_tensor(n, s, F32, kind="ExternalOutput").ap() for n, s in outs.items()]
    trunk(nc, *args)
    r = run_bass_kernel_spmd(nc, [ins], core_ids=[0]).results[0]

    def tokens(t):
        return np.ascontiguousarray(t.transpose(2, 1, 0)).reshape(t.shape[2], -1)

    y, k, v_s, tail = tokens(r["y"]), tokens(r["k_new_out"]), tokens(r["v_new_s"]), tokens(r["conv_tail"])
    heads = (HEADS, 2 * HD)
    new_s = np.concatenate([r["new_state"], tail[CW - 1:].reshape(NS, 1, D)], axis=1)
    return (y[:SEQ].reshape(1, SEQ, D), y[SEQ:].reshape(NS, 1, D), tail[:CW - 1].reshape(1, 1, CW - 1, D),
            k[:SEQ].reshape(1, SEQ, *heads), r["v_new_out"].reshape(1, SEQ, *heads), new_s.reshape(1, NS, CW - 1, D),
            k[SEQ:].reshape(NS, 1, *heads), v_s.reshape(NS, 1, *heads))
```

```python
import math
from contextlib import ExitStack

import numpy as np

import concourse.bass as bass
from concourse import mybir
from concourse.alu_op_type import AluOpType as ALU

F32 = mybir.dt.float32
F32R = mybir.dt.float32r
BF16 = mybir.dt.bfloat16
I32 = mybir.dt.int32
ACT = mybir.ActivationFunctionType
AX = mybir.AxisListType

P = 128
D = 1024
KD = D // P
SEQ = 512
NS = 8
T = SEQ + NS
HALF = T // 2
FF = 2816
KF = FF // P
HEADS = 8
HD = 64
CW = 31
PAST = 256
PAGE = 128
NPG = PAST // PAGE
NPOOL = NS * NPG * 5 // 4
EPS = 1e-6
SCALE = HD ** -0.5
LAM_INIT = 0.8 - 0.6 * math.exp(-0.3 * 1)
KW = KF // 2
MIX = KF - KD
NEG = -1.0e30

VEC = {}
_at = 0
for _name, _n in (("ffn", 4 * KD), ("mix", 2 * KD), ("kv", KD), ("final", KD), ("b_in", 2 * KD),
                  ("dw", CW * KD), ("dw_b", KD), ("ln_g", KD), ("ln_b", KD), ("b_out", KD), ("sub", 1)):
    VEC[_name] = _at
    _at += _n
NVEC = _at
C_ID, C_ROT, C_MASK, C_PAIR, C_EVEN, C_ODD = 0, P, 2 * P, 3 * P, 3 * P + HD, 3 * P + HD + 1
NCST = C_ODD + 1

DVE_TAPS, POOL_TAPS, PE_TAPS = 14, 12, 5
LAST_TAPS = (12, 9, 10)


class Phase:

    def __init__(self, kind, tiles, chunks, per, weights, j=0):
        self.kind, self.tiles, self.chunks, self.per, self.weights, self.j = kind, tiles, chunks, per, weights, j
        self.groups = chunks // 4
        self.chunk0 = self.unit0 = self.pair0 = self.h0 = self.set = self.next = None


def plan(w_in, w_out, c_in, c_out, w_kv, w_q, w_o):
    def pair(w, half):
        v = w.rearrange("(k p) (a m c) -> a p m k c", p=P, a=2, c=P)
        return lambda g, c: v[(c % 2) ^ half, :, 2 * g + c // 2, :, :]

    def down(w):
        v = w.rearrange("(f k p) (m c) -> f p m k c", f=2, p=P, c=P)
        return lambda g, c: v[c % 2, :, 2 * g + c // 2, :, :]

    def square(w):
        v = w.rearrange("(k p) (m c) -> p m k c", p=P, c=P)
        return lambda g, c: v[:, 4 * g + c, :, :]

    def ffn(j):
        return [Phase("up", KD, 2 * KF, 1, pair(w_in[j // 2, j % 2], 0), j),
                Phase("down", KW, 2 * KD, 2, down(w_out[j // 2, j % 2]), j)]

    phases = (ffn(0) + [Phase("conv_in", KD, 2 * KD, 1, pair(c_in[0], 1)), Phase("conv_out", KD, KD, 1, square(c_out[0]))]
              + ffn(1) + [Phase("k", KD, KD, 1, square(w_kv[:, 0:D])), Phase("v", KD, KD, 1, square(w_kv[:, D:2 * D]))]
              + ffn(2) + [Phase("q", KD, KD, 1, square(w_q[0])), Phase("o", KD, KD, 1, square(w_o[0]))] + ffn(3))
    chunk = unit = pairs = h = sets = 0
    for ph in phases:
        ph.chunk0, ph.unit0, ph.pair0, ph.h0 = chunk, unit, pairs, h
        chunk += ph.chunks
        unit += ph.chunks // ph.per
        pairs += ph.chunks // 2 if ph.kind in ("up", "conv_in") else 0
        h += {"up": KF, "conv_in": KD}.get(ph.kind, 0)
        if ph.kind in ("up", "conv_in", "k", "q"):
            ph.set = sets
            sets += 1
        elif ph.kind == "v":
            ph.set = sets - 1
    for a, b in zip(phases, phases[1:]):
        a.next = b
    return phases


def trunk(nc, xT, vec_d, cst_d, rope_d, lam_d, stateT, state, cache_k, cache_v, pages, w_in, w_out, c_in, c_out,
          w_kv, w_q, w_o, y_d, conv_d, new_state_d, k_d, v_d, vs_d):
    q_dram = nc.dram_tensor("q_dram", (NS, D), F32, kind="Internal").ap()
    phases = plan(w_in, w_out, c_in, c_out, w_kv, w_q, w_o)
    KIND = {}
    for ph in phases:
        KIND.setdefault(ph.kind, []).append(ph)
    last_phase = phases[-1]

    with ExitStack() as ctx:
        def sb(name, shape, dt=F32):
            return ctx.enter_context(nc.sbuf_tensor(name, shape, dt))

        def sem(name):
            return ctx.enter_context(nc.semaphore(name))

        cursor = [-(-nc.sbuf_base // 32) * 32]
        top = cursor[0]

        def place(name, shape, dt=F32, at=None):
            size = int(np.prod(shape[1:])) * (2 if dt == BF16 else 4)
            if at is None:
                at = cursor[0]
                cursor[0] += -(-size // 32) * 32
            where[name] = (at, at + -(-size // 32) * 32)
            return nc.alloc_sbuf_tensor_at(name, shape, dt, offset=at)

        where = {}
        xg_hi = place("xg_hi", [P, KD, T], F32R)
        xg_lo = place("xg_lo", [P, KD, T], F32R)
        h_hi = place("h_hi", [P, KF, T], F32R)
        h_lo = place("h_lo", [P, KF, T], F32R)
        x = place("x", [P, KD, T])
        raw = place("raw", [P, 4, KW * P])
        w_hi = place("w_hi", [P, 2, KW * P], F32R)
        w_lo = place("w_lo", [P, 2, KW * P], F32R)
        rstd = place("rstd", [P, T])
        acc = place("acc", [P, T])
        sq = place("sq", [P, 2, T])
        t_gate = place("t_gate", [P, 2, T])
        t_act = place("t_act", [P, 2, T])
        t_out = place("t_out", [P, 2, T])
        vec = place("vec", [P, NVEC])
        cst = place("cst", [P, NCST])
        ones_d = place("ones_d", [P, P])
        ident_b = place("ident_b", [P, P], BF16)
        mask_b = place("mask_b", [P, P], BF16)
        v_s = place("v_s", [P, HEADS, NS])
        neglam = place("neglam", [P, 1])
        pairco = place("pairco", [P, 1])
        sub_g = place("sub_g", [P, 1])
        lam_s = place("lam_s", [1, 8])
        pages_s = place("pages_s", [1, NS * NPG], I32)
        mx = place("mx", [P, 2, 2])
        nmx = place("nmx", [P, 2, 2])
        lsum = place("lsum", [P, 2, 2])
        rl = place("rl", [P, 2, 2])
        rl2 = place("rl2", [P, 2])
        mx_s = place("mx_s", [P, 4])
        var = place("var", [P, 6])
        inv = place("inv", [P, 6])
        minus_half = place("minus_half", [P, 6])
        assert cursor[0] <= nc.sbuf_usable_end, cursor[0]
        sb("fence", [P, (cursor[0] - top) // 4])

        XG, HH, HL = where["xg_hi"][0], where["h_hi"][0], where["h_lo"][0]
        room = MIX * T * 4

        def over(base, size, items):
            made, at = [], base
            for name, shape in items:
                made.append(place(name, shape, at=at))
                at = where[name][1]
            assert at <= base + size, (items, at - base - size)
            return made

        lam_row, lam_prod = over(HH, room, [("lam_row", [1, 4, HD]), ("lam_prod", [1, 2, HD])])
        conv, window, conv_p = over(HL, room, [("conv", [P, KD, T]), ("window", [P, KD, CW, NS]), ("conv_p", [P, 2, SEQ])])
        glu, tap, conv_b, swin, tail, diag = over(HH, room, [
            ("glu", [P, 2, CW - 1 + T]), ("tap", [P, 3, SEQ]), ("conv_b", [P, SEQ]), ("swin", [P, CW, NS]),
            ("tail", [P, KD, CW - 1 + NS]), ("diag", [P, 2, PE_TAPS, P])])
        k_new, = over(HL, room, [("k_new", [P, KD, T])])
        cs_k, v_tok = over(HH, room, [("cs_k", [P, 2, T]), ("v_tok", [P, KD, SEQ])])
        qT, cs_q, pr = over(HL, room, [("qT", [P, KD, T]), ("cs_q", [P, 2, T]), ("pr", [P, 2, 2, SEQ])])
        kT, at_n, aT, s_dec, p_dec, an_dec = over(HH, room, [
            ("kT", [P, KD, T]), ("at_n", [P, 2, SEQ]), ("aT", [P, 2, SEQ]), ("s_dec", [P, NPG, NS, 2 * HEADS]),
            ("p_dec", [P, PAST + 1]), ("an_dec", [P, NS, HEADS])])
        vT, page = over(XG, 2 * KD * T * 4, [("vT", [P, SEQ // P, D]), ("page", [P, 4, D])])
        page_4, = over(where["cs_q"][0], 2 * T * 4, [("page_4", [P, D])])
        tg0 = where["t_gate"][0]
        qb, kprod = over(tg0, 6 * T * 4, [("qb", [P, 2, D]), ("kprod", [P, D])])
        av, = over(XG, SEQ // P * D * 4, [("av", [HD, D])])
        at_dec, own, dec_o, dec_sq, dec_n, z_dec = over(tg0 + D * 4, 2 * D * 4, [("at_dec", [P, NPG, NS, HD + HEADS])] + [
            (n, [P, HD]) for n in ("own", "dec_o", "dec_sq", "dec_n")] + [("z_dec", [P, NS, HEADS, 2])])

        K_SLOTS = [page[:, i, :] for i in range(4)] + [page_4[:, :]]
        V_SLOTS = K_SLOTS + [qb[:, 0, :]]

        ps_all = ctx.enter_context(nc.psum_tensor("ps_all", [P, 8, 512], F32))
        unit = [ps_all[:, 2 * s:2 * s + 2, 0:HALF] for s in range(2)]
        ps_stat = ps_all[:, 4:6, 0:HALF]
        ps_var = ps_all[:, 4, 0:6]
        ps_rot = ps_all[:, 6:8, 0:HALF]

        def halves(ap):
            return ap.rearrange("p (a b) -> p a b", a=2)

        raw_full = [sem(f"raw_full{s}") for s in range(4)]
        hi_made = sem("hi_made")
        weights_ready = sem("weights_ready")
        chunk_used = sem("chunk_used")
        drained = sem("drained")
        act_done = sem("act_done")
        act_scaled = sem("act_scaled")
        h_hi_made = sem("h_hi_made")
        h_ready = sem("h_ready")
        xg_hi_made = sem("xg_hi_made")
        xg_ready = sem("xg_ready")
        squared = sem("squared")
        sq_used = sem("sq_used")
        acc_copied = sem("acc_copied")
        summed = sem("summed")
        mean_done = sem("mean_done")
        var_done = sem("var_done")
        var_read = sem("var_read")
        inv_made = sem("inv_made")
        spread_done = sem("spread_done")
        rstd_made = sem("rstd_made")
        inputs = sem("inputs")
        in_state = sem("in_state")
        in_rope = [sem("in_rope_k"), sem("in_rope_q")]
        const_done = sem("const_done")
        mask_made = sem("mask_made")
        lam_step = sem("lam_step")
        rot_done = sem("rot_done")
        cos_done = sem("cos_done")
        sin_done = sem("sin_done")
        rope_done = sem("rope_done")
        v_turned = sem("v_turned")
        v_copied = sem("v_copied")
        vs_copied = sem("vs_copied")
        kv_out = sem("kv_out")
        out_done = sem("out_done")
        glu_done = sem("glu_done")
        tap_made = sem("tap_made")
        tap_added = sem("tap_added")
        tapped = sem("tapped")
        diag_made = sem("diag_made")
        pe_tapped = sem("pe_tapped")
        joined = sem("joined")
        conv_done = sem("conv_done")
        centred = sem("centred")
        ln_scaled = sem("ln_scaled")
        ln_done = sem("ln_done")
        dve_self = sem("dve_self")
        in_kt, in_vt = sem("in_kt"), sem("in_vt")
        vec_in = sem("vec_in")
        x_in = [sem(f"x_in{i}") for i in range(4)]
        k_page_full = [sem(f"k_page_full{s}") for s in range(5)]
        v_page_full = [sem(f"v_page_full{s}") for s in range(6)]
        q_turned, q_copied, q_stored = sem("q_turned"), sem("q_copied"), sem("q_stored")
        qb_full = [sem(f"qb_full{s}") for s in range(2)]
        v_page_used = sem("v_page_used")
        scores_done = sem("scores_done")
        max_done = sem("max_done")
        exp_done = sem("exp_done")
        a_done = sem("a_done")
        aT_done = sem("aT_done")
        aT_copied = sem("aT_copied")
        o_done = sem("o_done")
        o_squared = sem("o_squared")
        o_stat, o_var, o_inv, o_spread = sem("o_stat"), sem("o_var"), sem("o_inv"), sem("o_spread")
        o_normed = sem("o_normed")
        o_hi_made = sem("o_hi_made")
        o_lo_made = sem("o_lo_made")
        kprod_done = sem("kprod_done")
        kred_done = sem("kred_done")
        d_new, d_scores, d_max, d_exp, d_weights = (sem(n) for n in ("d_new", "d_scores", "d_max", "d_exp", "d_weights"))
        d_turned, d_turned_read, d_out, d_squared, d_stat, d_normed = (
            sem(n) for n in ("d_turned", "d_turned_read", "d_out", "d_squared", "d_stat", "d_normed"))
        d_inv, d_spread = sem("d_inv"), sem("d_spread")
        d_cleared, d_av_copied, d_av_turned = sem("d_cleared"), sem("d_av_copied"), sem("d_av_turned")
        glu_pad = sem("glu_pad")
        win_done = sem("win_done")
        final_done = sem("final_done")

        N_IN = 16 * 3
        N_KV_OUT = 16 * (2 * KD + 1)
        N_OUT = 16 * (KD + 2)
        block = ctx.enter_context(nc.Block())

        def groups(engine, ph, body, first=False, last=False):
            a, b = int(first), ph.groups - int(last)
            if ph.groups <= 2:
                a = b = ph.groups
                for g in range(a):
                    body(g)
                return
            if first:
                body(0)
            with engine.Fori(a, b) as g:
                body(g)
            if last:
                body(ph.groups - 1)

        def wait_then_address(engine, semaphore, value):
            engine.wait_ge(semaphore, value)
            if not isinstance(value, int):
                engine.wait_ge(inputs, N_IN)

        def coming(ph, g, c):
            if c < 2:
                return ph, g, c + 2
            if isinstance(g, int) and g == ph.groups - 1:
                return (ph.next, 0, c - 2) if ph.next else None
            return ph, g + 1, c - 2

        def col(name, i):
            at = VEC[name] + i
            return vec[:, at:at + 1] if isinstance(at, int) else vec[:, bass.ds(at, 1)]

        def at(tensor, m):
            return tensor[:, m, :] if isinstance(m, int) else tensor[:, bass.ds(m, 1), :].rearrange("p a t -> p (a t)")

        def gain(s, k):
            name, i = (("ffn", 0), ("mix", 0), ("ffn", 1), ("kv", 0), ("ffn", 2), ("mix", 1), ("ffn", 3))[s]
            return col(name, KD * i + k)

        SET_AFTER = {("down", 0): 1, ("conv_out", 0): 2, ("down", 1): 3, ("down", 2): 5, ("o", 0): 6, ("down", 3): None}
        SUMS_BEFORE = {("down", 0): KD, ("conv_out", 0): 2 * KD, ("down", 1): 3 * KD, ("down", 2): 4 * KD,
                       ("o", 0): 5 * KD, ("down", 3): 6 * KD}
        MID_HI, MID_GATE, MID_DVE = 4, 7, 7
        Q0 = KIND["q"][0].unit0
        K0 = KIND["k"][0].unit0
        V0 = KIND["v"][0].unit0
        STEPS = HEADS * (SEQ // P)
        SCORES_AT = NS * NPG + 7
        TURN_AT = SCORES_AT + 4

        BLOCKS = tuple(s * HALF + at for s in range(2) for at in (0, P, HALF - P))

        def shares(m):
            return LAST_TAPS if isinstance(m, int) and m == KD - 1 else (DVE_TAPS, POOL_TAPS, PE_TAPS)

        def diagonal(m, i):
            return diag[:, (m + i // PE_TAPS) % 2 if isinstance(m, int) else m, i % PE_TAPS, :]

        def fresh(ph):
            return ph.kind in ("up", "conv_in", "k", "q") and not (ph.kind == "up" and ph.j == 2)

        @block.sync
        def _(sp):
            def load_chunk(ph, g, c):
                n = ph.chunk0 + 4 * g + c
                if not (isinstance(n, int) and n < 4):
                    wait_then_address(sp, weights_ready, n - 3)
                dst = raw[:, c, 0:ph.tiles * P].rearrange("p (k c) -> p k c", c=P)
                sp.dma_start(dst, ph.weights(g, c)).then_inc(raw_full[c], 16)

            def page_of(i, cache):
                pg = sp.value_load(pages_s[0:1, i:i + 1], min_val=0, max_val=NPOOL - 1)
                return cache[bass.ds(pg, 1), :, :].rearrange("a t f -> (a t) f")

            def load_page(i):
                if i >= len(K_SLOTS):
                    sp.wait_ge(kprod_done, i - len(K_SLOTS) + 1)
                s = i % len(K_SLOTS)
                sp.dma_start(K_SLOTS[s], page_of(i, cache_k)).then_inc(k_page_full[s], 16)

            def load_q(b):
                if b >= 2:
                    sp.wait_ge(kprod_done, NPG * (b - 1))
                sp.dma_start(qb[:, b % 2, :], q_dram[b:b + 1, :].broadcast_to([P, D])).then_inc(qb_full[b % 2], 16)

            def load_v_page(i):
                if i == 0:
                    sp.wait_ge(kprod_done, NS * NPG)
                if i >= len(V_SLOTS):
                    sp.wait_ge(v_page_used, i - len(V_SLOTS) + 1)
                s = i % len(V_SLOTS)
                sp.dma_start(V_SLOTS[s], page_of(i, cache_v)).then_inc(v_page_full[s], 16)

            first_chunk = phases[0]
            sp.dma_start(vec[:, :], vec_d).then_inc(vec_in, 16)
            load_chunk(first_chunk, 0, 0)
            for i in range(len(x_in)):
                k = slice(i * KD // len(x_in), (i + 1) * KD // len(x_in))
                sp.dma_start(x[:, k, :], xT[:, k, :]).then_inc(x_in[i], 16)
            load_chunk(first_chunk, 0, 1)
            sp.dma_start(cst[:, :], cst_d).then_inc(inputs, 16)
            sp.dma_start(lam_row[0:1, :, :], lam_d).then_inc(inputs, 16)
            sp.dma_start(pages_s[0:1, :], pages).then_inc(inputs, 16)
            load_chunk(first_chunk, 0, 2)
            load_chunk(first_chunk, 0, 3)
            for ph in phases:
                if ph.kind == "o":
                    for c in range(4):
                        load_chunk(ph, 0, c)
                    sp.wait_ge(chunk_used, ph.chunk0)
                    sp.wait_ge(rope_done, 2 * KD)
                    for i in range(NS * NPG):
                        load_page(i)
                        if i == 1:
                            sp.wait_ge(q_stored, 16)
                        if i % NPG == 1:
                            load_q(i // NPG)
                    for i in range(NS * NPG):
                        load_v_page(i)
                    for c in range(4):
                        load_chunk(ph, 1, c)
                elif ph.kind == "conv_in":
                    for g in range(ph.groups):
                        for c in range(4):
                            load_chunk(ph, g, c)
                else:
                    groups(sp, ph, lambda g: [load_chunk(ph, g, c) for c in range(4)
                                              if not (ph is first_chunk and isinstance(g, int))], first=ph is first_chunk)
            sp.wait_ge(kv_out, N_KV_OUT)
            sp.wait_ge(out_done, N_OUT)

        @block.tensor
        def _(pe):
            def chunk(ph, g, c, between=(), tiles=None, halves=(0, 1)):
                n = ph.chunk0 + 4 * g + c
                u = ph.unit0 + (4 * g + c if ph.per == 1 else 2 * g + c // 2)
                part = c % ph.per
                slot = c % 2 if ph.per == 1 else c // 2
                pe.wait_ge(weights_ready, n + 1)
                if part == 0 and not (isinstance(u, int) and u < 2):
                    pe.wait_ge(drained, u - 1)
                opening = isinstance(g, int) and g == 0 and c < ph.per and ph.kind != "v"
                for k in tiles or range(ph.tiles):
                    if k in between:
                        between[k]()
                    kk = part * ph.tiles + k
                    if ph.kind == "down":
                        hi, lo, need = h_hi[:, kk], h_lo[:, kk], (h_ready, ph.h0 - KF + kk + 1)
                    elif ph.kind == "conv_out":
                        hi, lo, need = h_hi[:, MIX + kk], h_lo[:, MIX + kk], (h_ready, ph.h0 - KD + kk + 1)
                    elif ph.kind == "o":
                        hi, lo, need = h_hi[:, MIX + kk], h_lo[:, MIX + kk], (o_lo_made, HEADS + halves[-1])
                    else:
                        hi, lo, need = xg_hi[:, kk], xg_lo[:, kk], (xg_ready, KD * ph.set + kk + 1)
                    if opening:
                        pe.wait_ge(*need)
                    for i, (w, m) in enumerate(((w_hi, hi), (w_hi, lo), (w_lo, hi))):
                        for s in halves:
                            mm = nc.tensor.matmul(unit[slot][:, s, :], w[:, c % 2, k * P:(k + 1) * P],
                                                  m[:, s * HALF:(s + 1) * HALF], start=kk == 0 and i == 0,
                                                  stop=kk == ph.per * ph.tiles - 1 and i == 2)
                if halves[-1] == 1:
                    mm.then_inc(chunk_used, 1)

            def mean(m, src, out):
                for s in range(2):
                    mm = nc.tensor.matmul(out[:, s, :], ones_d[:, :], src[:, s * HALF:(s + 1) * HALF],
                                          start=m == 0, stop=m == KD - 1)
                return mm

            def tap_products(m):
                v, p, n = shares(m)
                pe.wait_ge(glu_done, m + 1)
                if m >= 2:
                    pe.wait_ge(conv_done, m - 1)
                for i in range(n):
                    if i % PE_TAPS == 0:
                        pe.wait_ge(diag_made, PE_TAPS * m + min(i + PE_TAPS, n))
                    mm = nc.tensor.matmul(ps_all[:, 4 + m % 2, :], diagonal(m, i), glu[:, m % 2, v + p + i:v + p + i + SEQ],
                                          start=i == 0, stop=i == n - 1)
                mm.then_inc(pe_tapped, 1)

            def conv_mean(m):
                pe.wait_ge(conv_done, m + 1)
                return mean(m, conv[:, m, :], ps_rot)

            def layer_norm(made):
                tap_products(KD - 1)
                for m in range(KD - 3, KD):
                    mm = conv_mean(m)
                mm.then_inc(mean_done, 1)
                pe.wait_ge(rstd_made, made)
                for m in range(KD):
                    pe.wait_ge(squared, 2 * KD + m + 1)
                    mean(m, sq[:, m % 2, :], ps_stat).then_inc(sq_used, 1)
                pe.wait_ge(acc_copied, 1)
                for i, b in enumerate(BLOCKS):
                    mm = nc.tensor.matmul(ps_all[:, 6, i:i + 1], acc[:, b:b + P], cst[:, C_ID:C_ID + 1], start=True, stop=True)
                mm.then_inc(var_done, 1)
                spread(made + 1)

            def variance(sums, free):
                if not free:
                    pe.wait_ge(inputs, N_IN)
                    pe.wait_ge(const_done, 2)
                pe.wait_ge(summed, sums)
                if free:
                    pe.wait_ge(*free)
                for i, b in enumerate(BLOCKS):
                    mm = nc.tensor.matmul(ps_var[:, i:i + 1], acc[:, b:b + P], ones_d[:, 0:1], start=True, stop=True)
                mm.then_inc(var_done, 1)

            def spread(made):
                pe.wait_ge(inv_made, made)
                for i, b in enumerate(BLOCKS):
                    half, at_b = divmod(b, HALF)
                    mm = nc.tensor.matmul(ps_stat[:, half, at_b:at_b + P], inv[:, i:i + 1].broadcast_to([P, P]),
                                          cst[:, C_ID:C_ID + P], start=True, stop=True)
                mm.then_inc(spread_done, 1)

            def rotate(r, u):
                pe.wait_ge(drained, u + 1)
                if r >= 1:
                    pe.wait_ge(sin_done, r)
                for s in range(2):
                    mm = nc.tensor.matmul(ps_rot[:, s, :], cst[:, C_ROT:C_ROT + P],
                                          t_gate[:, r % 2, s * HALF:(s + 1) * HALF], start=True, stop=True)
                mm.then_inc(rot_done, 1)

            def turn_v(m):
                pe.wait_ge(drained, V0 + m + 1)
                if m == 0:
                    pe.wait_ge(sin_done, KD)
                else:
                    pe.wait_ge(v_copied, m)
                for t in range(SEQ // P):
                    mm = nc.tensor.transpose(ps_all[:, 6, t * P:(t + 1) * P], t_gate[:, m % 2, t * P:(t + 1) * P],
                                             cst[:, C_ID:C_ID + P])
                mm.then_inc(v_turned, 1)

            def scores(s):
                h, t = divmod(s, SEQ // P)
                keys = (t + 1) * P
                if s >= 2:
                    pe.wait_ge(exp_done, s - 1)
                for c in range(2):
                    rows = slice(c * HD, (c + 1) * HD)
                    nc.tensor.matmul(ps_all[:, 2 * (s % 2) + c, 0:keys], qT[rows, h, t * P:(t + 1) * P],
                                     kT[rows, h, 0:keys], start=True, stop=False)
                for c in range(2):
                    mm = nc.tensor.matmul(ps_all[:, 2 * (s % 2) + c, keys - P:keys], ident_b[:, :], mask_b[:, :],
                                          start=False, stop=True)
                mm.then_inc(scores_done, 1)

            def turn_a(s):
                pe.wait_ge(a_done, s + 1)
                if s >= 2:
                    pe.wait_ge(aT_copied, s - 1)
                for k in range(s % (SEQ // P) + 1):
                    mm = nc.tensor.transpose(ps_all[:, 4 + s % 2, k * P:(k + 1) * P],
                                             at_n[:, s % 2, k * P:(k + 1) * P], cst[:, C_ID:C_ID + P])
                mm.then_inc(aT_done, 1)

            def values(s):
                h, t = divmod(s, SEQ // P)
                pe.wait_ge(aT_copied, s + 1)
                if t == 0 and h:
                    pe.wait_ge(o_squared, h)
                for k in range(t + 1):
                    mm = nc.tensor.matmul(ps_all[:, 6, t * P:(t + 1) * P], vT[:, k, h * P:(h + 1) * P],
                                          aT[:, s % 2, k * P:(k + 1) * P], start=k == 0, stop=k == t)
                if t == SEQ // P - 1:
                    mm.then_inc(o_done, 1)

            def head_stat(h):
                pe.wait_ge(o_squared, h + 1)
                if h:
                    pe.wait_ge(o_normed, h)
                for t in range(SEQ // P):
                    mm = nc.tensor.matmul(ps_all[:, 7, t:t + 1], sq[:, 0, t * P:(t + 1) * P], ones_d[:, 0:1], start=True, stop=True)
                mm.then_inc(o_stat, 1)

            def head_spread(h):
                pe.wait_ge(o_inv, h + 1)
                for t in range(SEQ // P):
                    mm = nc.tensor.matmul(ps_all[:, 7, t * P:(t + 1) * P], inv[:, t:t + 1].broadcast_to([P, P]),
                                          cst[:, C_ID:C_ID + P], start=True, stop=True)
                mm.then_inc(o_spread, 1)

            def turn_q():
                for h in range(HEADS):
                    mm = nc.tensor.transpose(ps_all[0:NS, 4 + h // 4, h % 4 * P:(h % 4 + 1) * P], qT[:, h, SEQ:T],
                                             cst[:, C_ID:C_ID + P])
                mm.then_inc(q_turned, 1)

            def sample_scores():
                pe.wait_ge(o_normed, SCORES_AT // 4)
                pe.wait_ge(kred_done, NS * NPG)
                pe.wait_ge(d_new, 3)
                for g in range(NPG):
                    nc.tensor.transpose(ps_all[:, 7, g * P:(g + 1) * P], s_dec[:, g].rearrange("p b j -> p (b j)"),
                                        cst[:, C_ID:C_ID + P])
                nc.tensor.matmul(ps_all[:, 7, PAST:PAST + 1], z_dec[:, :, :, :].rearrange("p b h c -> p (b h c)"),
                                 ones_d[:, 0:1], start=True, stop=True).then_inc(d_scores, 1)

            def turn_samples():
                pe.wait_ge(o_normed, TURN_AT // 4)
                pe.wait_ge(d_weights, 1)
                for g in range(NPG):
                    nc.tensor.matmul(ps_all[:, 7, g * HD:(g + 1) * HD], p_dec[:, g * P:(g + 1) * P],
                                     cst[:, C_PAIR:C_PAIR + HD], start=True, stop=True)
                nc.tensor.matmul(ps_all[:, 7, 2 * HD:3 * HD], p_dec[:, PAST:PAST + 1].broadcast_to([P, P]),
                                 cst[:, C_PAIR:C_PAIR + HD], start=True, stop=True).then_inc(d_turned, 1)

            def sample_values(i):
                b, g = divmod(i, NPG)
                weights = at_dec[:, g].rearrange("p b c -> p (b c)")[:, b * HD:(b + 1) * HD]
                pe.wait_ge(v_page_full[i % len(V_SLOTS)], 16 * (i // len(V_SLOTS) + 1))
                for c in range(2):
                    mm = nc.tensor.matmul(ps_all[0:HD, 2 + c, :], weights, V_SLOTS[i % len(V_SLOTS)][:, c * SEQ:(c + 1) * SEQ],
                                          start=i == 0, stop=i == NS * NPG - 1)
                mm.then_inc(v_page_used, 1)

            def attention():
                pe.wait_ge(rope_done, 2 * KD)
                turn_q()
                pe.wait_ge(drained, Q0 + KD)
                pe.wait_ge(in_kt, 16)
                pe.wait_ge(mask_made, 2)
                scores(0)
                scores(1)
                pe.wait_ge(q_copied, 1)
                for s in range(STEPS + 3):
                    if s + 2 < STEPS:
                        scores(s + 2)
                    if s < STEPS:
                        turn_a(s)
                    if 1 <= s <= STEPS:
                        if s == 1:
                            pe.wait_ge(in_vt, 16)
                        values(s - 1)
                    h, t = divmod(s - 5, 4)
                    if t == 0 and 0 <= h < HEADS:
                        if s == SCORES_AT + 2:
                            pe.wait_ge(d_exp, 1)
                        if s == TURN_AT + 2:
                            pe.wait_ge(d_turned_read, 1)
                        head_stat(h)
                    if t == 1 and 0 <= h < HEADS:
                        head_spread(h)
                    if s == SCORES_AT:
                        sample_scores()
                    if s == TURN_AT:
                        turn_samples()
                    if s >= STEPS:
                        for i in range(*((0, 6), (6, 10), (10, NS * NPG))[s - STEPS]):
                            sample_values(i)
                pe.wait_ge(d_av_copied, 2)
                for h in range(HEADS):
                    mm = nc.tensor.matmul(ps_all[:, 6, h * NS:(h + 1) * NS], av[:, h * P:(h + 1) * P],
                                          cst[0:HD, C_ID + h:C_ID + HD:HEADS], start=True, stop=True)
                mm.then_inc(d_av_turned, 1)
                pe.wait_ge(d_squared, 1)
                nc.tensor.matmul(ps_all[0:HD, 4, 0:1], dec_sq[:, :], ones_d[:, 0:1], start=True, stop=True
                                 ).then_inc(d_stat, 1)
                o = KIND["o"][0]
                chunk(o, 0, 0, tiles=range(KD // 2), halves=(0,))
                pe.wait_ge(d_inv, 2)
                nc.tensor.matmul(ps_all[:, 4, 0:HD], inv[0:HD, 0:1].broadcast_to([HD, P]), cst[0:HD, C_ID:C_ID + HD],
                                 start=True, stop=True).then_inc(d_spread, 1)
                chunk(o, 0, 0, tiles=range(KD // 2, KD), halves=(0,))
                chunk(o, 0, 1, halves=(0,))

            sums = 0
            made = 0
            for ph in phases:
                if fresh(ph):
                    sums += KD

                def body(g):
                    for c in range(4):
                        opening = isinstance(g, int) and g == 0
                        if ph is phases[0] and opening and c == 1:
                            chunk(ph, g, c, {3: lambda: variance(sums, None)})
                            spread(made + 1)
                        elif ph.kind == "o" and opening and c < 2:
                            chunk(ph, g, c, halves=(1,))
                        else:
                            chunk(ph, g, c, {2: lambda: spread(made + 1)} if opening and c == 1 and fresh(ph) else ())
                        r = 4 * g + c - 1
                        if opening and c == 0:
                            if fresh(ph) and ph is not phases[0]:
                                variance(sums, (rstd_made, made) if made else None)
                        elif ph.kind == "k":
                            rotate(r, K0 + r)
                        elif ph.kind == "q":
                            rotate(KD + r, Q0 + r)
                        elif ph.kind == "v" and r >= 0:
                            turn_v(r)
                        if ph.kind == "conv_in" and c % 2:
                            m = 2 * g + c // 2
                            if m >= 1:
                                tap_products(m - 1)
                            if m >= 3:
                                conv_mean(m - 3)
                if ph.kind == "conv_in":
                    for g in range(ph.groups):
                        body(g)
                else:
                    groups(pe, ph, body, first=True)
                made += fresh(ph)
                if ph is phases[0]:
                    pe.wait_ge(lam_step, 4)
                    nc.tensor.matmul(ps_all[:, 6, 0:1], ones_d[0:1, :], lam_s[0:1, 4:5], start=True, stop=True
                                     ).then_inc(lam_step, 1)
                if ph.kind == "k":
                    rotate(KD - 1, K0 + KD - 1)
                elif ph.kind == "v":
                    turn_v(KD - 1)
                elif ph.kind == "q":
                    rotate(2 * KD - 1, Q0 + KD - 1)
                    attention()
                elif ph.kind == "conv_in":
                    layer_norm(made)
                    made += 1
            variance(sums + KD, (rstd_made, made))
            spread(made + 1)

        @block.scalar
        def _(act):
            def round_hi(ph, g, c):
                n = ph.chunk0 + 4 * g + c
                act.wait_ge(raw_full[c], 16 * (ph.chunk0 // 4 + g + 1))
                if not (isinstance(n, int) and n < 2):
                    act.wait_ge(chunk_used, n - 1)
                w = ph.tiles * P
                nc.scalar.activation(w_hi[:, c % 2, 0:w], raw[:, c, 0:w], ACT.Copy).then_inc(hi_made, 1)

            def ahead(ph, g, c):
                to = coming(ph, g, c)
                if to:
                    round_hi(*to)

            def x_hi(s, m):
                nc.scalar.activation(xg_hi[:, m, :], x[:, m, :], ACT.Copy, scale=gain(s, m)).then_inc(xg_hi_made, 1)

            act.wait_ge(vec_in, 16)
            round_hi(phases[0], 0, 0)
            for m in range(KD):
                if m % 2 == 0:
                    act.wait_ge(x_in[m // 2], 16)
                x_hi(0, m)
            round_hi(phases[0], 0, 1)
            nc.scalar.activation(acc[:, :], x[:, 0, :], ACT.Square).then_inc(squared, 1)
            for m in range(1, KD):
                if m >= 3:
                    act.wait_ge(summed, m - 1)
                nc.scalar.activation(sq[:, m % 2, :], x[:, m, :], ACT.Square).then_inc(squared, 1)
            act.wait_ge(inputs, N_IN)
            nc.scalar.activation(ident_b[:, :], cst[:, C_ID:C_ID + P], ACT.Copy).then_inc(mask_made, 1)
            nc.scalar.activation(mask_b[:, :], cst[:, C_MASK:C_MASK + P], ACT.Copy).then_inc(mask_made, 1)
            act.wait_ge(lam_step, 2)
            nc.scalar.activation(lam_s[0:1, 2:4], lam_s[0:1, 0:2], ACT.Exp).then_inc(lam_step, 1)
            act.dma_start(new_state_d, state[:, 1:CW - 1, :]).then_inc(out_done, 16)

            def up(ph):
                def body(g):
                    for q in range(2):
                        u, p = ph.unit0 + 4 * g + 2 * q, ph.pair0 + 2 * g + q
                        ahead(ph, g, 2 * q)
                        act.wait_ge(drained, u + 1)
                        nc.scalar.activation(t_act[:, q, :], t_gate[:, q, :], ACT.Silu).then_inc(act_done, 1)
                        ahead(ph, g, 2 * q + 1)
                        wait_then_address(act, drained, u + 2)
                        if isinstance(g, int) and g == 0 and q == 0 and ph.j in (1, 2):
                            if ph.j == 1:
                                act.wait_ge(out_done, 16 * 2)
                            else:
                                act.wait_ge(kv_out, N_KV_OUT)
                        nc.scalar.activation(at(h_hi, 2 * g + q), t_out[:, q, :], ACT.Copy).then_inc(h_hi_made, 1)
                groups(act, ph, body, first=True, last=True)

            def residual(ph):
                key = (ph.kind, ph.j)
                sums = SUMS_BEFORE[key]

                def body(g):
                    for c in range(4):
                        ahead(ph, g, c)
                        if c % ph.per == ph.per - 1:
                            m = (4 * g + c) if ph.per == 1 else 2 * g + c // 2
                            act.wait_ge(summed, sums + m - 1)
                            wait_then_address(act, drained, ph.unit0 + m + 1)
                            if SET_AFTER[key] is not None:
                                nc.scalar.activation(at(xg_hi, m), at(x, m), ACT.Copy, scale=gain(SET_AFTER[key], m)
                                                     ).then_inc(xg_hi_made, 1)
                            slot = (c if ph.per == 1 else c // 2) % 2
                            nc.scalar.activation(sq[:, slot, :], at(x, m), ACT.Square).then_inc(squared, 1)
                groups(act, ph, body, last=True)

            def conv_in(ph):
                def sigmoid(g, q):
                    wait_then_address(act, drained, ph.unit0 + 4 * g + 2 * q + 1)
                    nc.scalar.activation(t_act[:, q, :], t_gate[:, q, :], ACT.Sigmoid, bias=col("b_in", KD + 2 * g + q)
                                         ).then_inc(act_done, 1)

                def diagonals(m, slot, first, count):
                    v, p, _ = shares(m)
                    for i in range(first, first + count):
                        nc.scalar.activation(diagonal(slot, i), cst[:, C_ID:C_ID + P], ACT.Copy,
                                             scale=col("dw", KD * (v + p + i) + m)).then_inc(diag_made, 1)

                def body(g):
                    for q in range(2):
                        m = 2 * g + q
                        following = None if isinstance(m, int) and m == KD - 1 else (g + q, 1 - q)
                        v, count, n = shares(m)
                        act.wait_ge(glu_done, m + 1)
                        for i in range(count):
                            if following and i == MID_HI:
                                ahead(ph, following[0], 2 * following[1])
                            if following and i == MID_GATE:
                                sigmoid(*following)
                                ahead(ph, following[0], 2 * following[1] + 1)
                                if not (isinstance(m, int) and m == 0):
                                    wait_then_address(act, pe_tapped, m)
                                diagonals(m + 1, 1 - q, 0, PE_TAPS)
                            if n > PE_TAPS and i == 3:
                                act.wait_ge(pe_tapped, m)
                                diagonals(m, q, PE_TAPS, n - PE_TAPS)
                            j = v + i
                            if i >= 3:
                                wait_then_address(act, tap_added, (POOL_TAPS - 1) * m + max(i - 3, 1))
                            elif not (isinstance(m, int) and m == 0):
                                last = POOL_TAPS - 1 - (POOL_TAPS - 1 - i) % 3
                                wait_then_address(act, tap_added, (POOL_TAPS - 1) * (m - 1) + last)
                            nc.scalar.activation(tap[:, i % 3, :], glu[:, q, j:j + SEQ], ACT.Copy,
                                                 scale=col("dw", KD * j + m)).then_inc(tap_made, 1)
                ahead(ph, 0, 0)
                sigmoid(0, 0)
                ahead(ph, 0, 1)
                diagonals(0, 0, 0, PE_TAPS)
                groups(act, ph, body, first=True, last=True)
                act.wait_ge(summed, 2 * KD)
                for m in range(KD):
                    act.wait_ge(centred, m + 1)
                    if m >= 2:
                        act.wait_ge(sq_used, m - 1)
                    nc.scalar.activation(sq[:, m % 2, :], conv[:, m, :], ACT.Square).then_inc(squared, 1)
                act.dma_start(conv_d, tail[:, :, :]).then_inc(out_done, 16)
                for m in range(KD):
                    act.wait_ge(ln_scaled, m + 1)
                    nc.scalar.activation(t_act[:, m % 2, :], t_gate[:, m % 2, :], ACT.Silu, scale=col("ln_g", m),
                                         bias=col("ln_b", m)).then_inc(ln_done, 1)
                    act.wait_ge(ln_done, m + 1)
                    nc.scalar.activation(h_hi[:, MIX + m, :], t_act[:, m % 2, :], ACT.Copy).then_inc(h_hi_made, 1)

            def rotary(ph):
                for g in range(ph.groups):
                    for c in range(4):
                        ahead(ph, g, c)
                        m = 4 * g + c - 1
                        if ph.kind == "k" and m >= 1:
                            act.wait_ge(rope_done, m)
                            act.dma_start(k_d[:, m - 1, :], k_new[:, m - 1, :]).then_inc(kv_out, 16)
                if ph.kind == "k":
                    for m in (KD - 2, KD - 1):
                        act.wait_ge(rope_done, m + 1)
                        act.dma_start(k_d[:, m, :], k_new[:, m, :]).then_inc(kv_out, 16)

            def store_v(m):
                act.wait_ge(v_turned, m + 1)
                nc.scalar.activation(v_tok[:, m, :], ps_all[:, 6, :], ACT.Copy).then_inc(v_copied, 1)
                act.wait_ge(v_copied, m + 1)
                act.dma_start(v_d[:, m * P:(m + 1) * P].rearrange("(t p) c -> p t c", p=P),
                              v_tok[:, m, :].rearrange("p (t c) -> p t c", c=P)).then_inc(kv_out, 16)

            def v(ph):
                for g in range(ph.groups):
                    for c in range(4):
                        ahead(ph, g, c)
                        if 4 * g + c >= 1:
                            store_v(4 * g + c - 1)
                act.wait_ge(chunk_used, ph.chunk0 + ph.chunks)
                for m in range(KD):
                    x_hi(4, m)
                store_v(KD - 1)
                act.wait_ge(vs_copied, KD)
                act.dma_start(vs_d, v_s[:, :, :]).then_inc(kv_out, 16)

            def attention():
                def exps(s):
                    keys = (s % 4 + 1) * P
                    act.wait_ge(max_done, s + 1)
                    if s >= 2:
                        act.wait_ge(a_done, s - 1)
                    for c in range(2):
                        e = nc.scalar.activation(pr[:, s % 2, c, 0:keys], ps_all[:, 2 * (s % 2) + c, 0:keys], ACT.Exp,
                                                 scale=SCALE, bias=nmx[:, s % 2, c:c + 1],
                                                 accum_out=lsum[:, s % 2, c:c + 1])
                    e.then_inc(exp_done, 1)

                act.wait_ge(q_turned, 1)
                nc.scalar.activation(kprod[0:NS, :].rearrange("p (a c) -> p a c", a=2), ps_all[0:NS, 4:6, :], ACT.Copy
                                     ).then_inc(q_copied, 1)
                act.wait_ge(q_copied, 1)
                act.dma_start(q_dram, kprod[0:NS, :]).then_inc(q_stored, 16)
                exps(0)
                for s in range(STEPS + 5):
                    if s + 1 < STEPS:
                        exps(s + 1)
                    if s < STEPS:
                        keys = (s % 4 + 1) * P
                        act.wait_ge(aT_done, s + 1)
                        nc.scalar.activation(aT[:, s % 2, 0:keys], ps_all[:, 4 + s % 2, 0:keys], ACT.Copy
                                             ).then_inc(aT_copied, 1)
                    if s == SCORES_AT + 1:
                        act.wait_ge(d_max, 2)
                        nc.scalar.activation(p_dec[:, :], ps_all[:, 7, 0:PAST + 1], ACT.Exp, scale=SCALE, bias=mx_s[:, 1:2],
                                             accum_out=mx_s[:, 2:3]).then_inc(d_exp, 1)
                    h, t = divmod(s - 8, 4)
                    if t == 0 and 0 <= h < HEADS:
                        act.wait_ge(o_normed, h + 1)
                        nc.scalar.activation(h_hi[:, MIX + h, 0:SEQ], sq[:, 1, 0:SEQ], ACT.Copy, scale=sub_g[:, 0:1]
                                             ).then_inc(o_hi_made, 1)
                    h, t = divmod(s - 4, 4)
                    if t == 0 and 0 <= h < HEADS:
                        act.wait_ge(o_done, h + 1)
                        nc.scalar.activation(acc[:, 0:SEQ], ps_all[:, 6, :], ACT.Copy)
                        nc.scalar.activation(sq[:, 0, 0:SEQ], ps_all[:, 6, :], ACT.Square).then_inc(o_squared, 1)
                act.wait_ge(v_page_used, NS * NPG)
                nc.scalar.activation(av[:, SEQ:D], ps_all[0:HD, 3, :], ACT.Copy).then_inc(d_av_copied, 1)
                act.wait_ge(d_out, 2)
                nc.scalar.activation(dec_sq[:, :], dec_o[:, :], ACT.Square).then_inc(d_squared, 1)
                act.wait_ge(d_normed, 1)
                nc.scalar.activation(h_hi[:, MIX:KF, SEQ:T], dec_n[:, :].rearrange("p (h b) -> p h b", h=HEADS),
                                     ACT.Copy, scale=sub_g[:, 0:1]).then_inc(o_hi_made, 1)

            for ph in phases:
                if ph.kind == "up":
                    up(ph)
                elif ph.kind == "conv_in":
                    conv_in(ph)
                elif ph.kind in ("k", "q"):
                    rotary(ph)
                    if ph.kind == "q":
                        attention()
                elif ph.kind == "v":
                    v(ph)
                else:
                    residual(ph)
            for m in range(KD):
                act.wait_ge(final_done, m + 1)
                act.dma_start(y_d[:, m, :], x[:, m, :]).then_inc(out_done, 16)

        @block.vector
        def _(dve):
            links = [0]

            def link(instruction):
                links[0] += 1
                instruction.then_inc(dve_self, 1)
                dve.wait_ge(dve_self, links[0])

            made = [0]

            def split_lo(ph, g, c):
                n = ph.chunk0 + 4 * g + c
                dve.wait_ge(hi_made, n + 1)
                w = ph.tiles * P
                nc.vector.tensor_tensor(w_lo[:, c % 2, 0:w], raw[:, c, 0:w], w_hi[:, c % 2, 0:w], ALU.subtract
                                        ).then_inc(weights_ready, 1)

            def ahead(ph, g, c):
                to = coming(ph, g, c)
                if to:
                    split_lo(*to)

            def x_lo(s, m):
                dve.wait_ge(xg_hi_made, KD * s + m + 1)
                nc.vector.scalar_tensor_tensor(at(xg_lo, m), at(x, m), gain(s, m), at(xg_hi, m), ALU.mult, ALU.subtract
                                               ).then_inc(xg_ready, 1)

            def rms(squares=ps_var):
                made[0] += 1
                dve.wait_ge(var_done, made[0])
                nc.vector.tensor_scalar(var[:, :], squares, EPS, None, ALU.add).then_inc(var_read, 1)
                dve.wait_ge(spread_done, made[0])
                nc.vector.tensor_copy(halves(rstd[:, :]), ps_stat).then_inc(rstd_made, 1)
                dve.wait_ge(rstd_made, made[0])

            def scaled(out, slot):
                return nc.vector.tensor_tensor(halves(out), unit[slot], halves(rstd[:, :]), ALU.mult)

            dve.wait_ge(vec_in, 16)
            split_lo(phases[0], 0, 0)
            for m in range(KD):
                x_lo(0, m)
            split_lo(phases[0], 0, 1)
            for m in range(1, KD):
                dve.wait_ge(squared, m + 1)
                if m >= 2:
                    dve.wait_ge(summed, m)
                nc.vector.tensor_tensor(acc[:, :], acc[:, :], sq[:, m % 2, :], ALU.add).then_inc(summed, 2 if m == 1 else 1)
            dve.wait_ge(inputs, N_IN)
            nc.vector.tensor_tensor(lam_prod[0:1, :, :], lam_row[0:1, 0:4:2, :], lam_row[0:1, 1:4:2, :], ALU.mult
                                    ).then_inc(lam_step, 1)
            dve.wait_ge(lam_step, 1)
            nc.vector.tensor_reduce(lam_s[0:1, 0:2], lam_prod[0:1, :, :], AX.X, ALU.add).then_inc(lam_step, 1)
            dve.wait_ge(lam_step, 3)
            nc.vector.tensor_scalar(lam_s[0:1, 4:5], lam_s[0:1, 3:4], lam_s[0:1, 2:3], LAM_INIT, ALU.subtract, ALU.subtract
                                    ).then_inc(lam_step, 1)
            nc.vector.tensor_scalar(sub_g[:, :], col("sub", 0), 1.0 - LAM_INIT, None, ALU.mult)

            def spread_lambda():
                dve.wait_ge(lam_step, 5)
                link(nc.vector.tensor_scalar(neglam[:, :], ps_all[:, 6, 0:1], float(D), None, ALU.mult))
                nc.vector.scalar_tensor_tensor(pairco[:, :], cst[:, C_ODD:C_ODD + 1], neglam[:, :], cst[:, C_EVEN:C_EVEN + 1],
                                               ALU.mult, ALU.add)

            def up(ph):
                def body(g):
                    for q in range(2):
                        n, p = ph.chunk0 + 4 * g + 2 * q, ph.pair0 + 2 * g + q
                        dve.wait_ge(chunk_used, n + 1)
                        scaled(t_gate[:, q, :], 0).then_inc(drained, 1)
                        ahead(ph, g, 2 * q)
                        dve.wait_ge(chunk_used, n + 2)
                        dve.wait_ge(act_scaled, p + 1 - KD * (ph.j > 0))
                        nc.vector.tensor_tensor(halves(t_out[:, q, :]), unit[1], halves(t_gate[:, q, :]), ALU.mult
                                                ).then_inc(drained, 1)
                        ahead(ph, g, 2 * q + 1)
                groups(dve, ph, body, last=True)

            def residual(ph):
                s = SET_AFTER[ph.kind, ph.j]

                def body(g):
                    for c in range(4):
                        last = c % ph.per == ph.per - 1
                        m = (4 * g + c) if ph.per == 1 else 2 * g + c // 2
                        slot = (c if ph.per == 1 else c // 2) % 2
                        dve.wait_ge(chunk_used, ph.chunk0 + 4 * g + c + 1)
                        if last:
                            op, by = {"down": (ALU.mult, 0.5), "o": (ALU.mult, 1.0)}.get(ph.kind) or (ALU.add, col("b_out", m))
                            xm = halves(at(x, m))
                            nc.vector.scalar_tensor_tensor(xm, unit[slot], by, xm, op, ALU.add).then_inc(drained, 1)
                        ahead(ph, g, c)
                        if last and s is not None:
                            x_lo(s, m)
                groups(dve, ph, body, last=True)

            def taps(m, q, between):
                chains = (conv[:, m, 0:SEQ] if isinstance(m, int) else conv[:, bass.ds(m, 1), 0:SEQ].rearrange("p a t -> p (a t)"),
                          conv_b[:, :])
                for j in range(shares(m)[0]):
                    if j == MID_DVE:
                        between()
                    src = glu[:, q, j:j + SEQ]
                    w = col("dw", KD * j + m)
                    out = chains[j % 2]
                    if j == 0:
                        i = nc.vector.tensor_scalar(out, src, w, col("dw_b", m), ALU.mult, ALU.add)
                    elif j == 1:
                        i = nc.vector.tensor_scalar(out, src, w, None, ALU.mult)
                    else:
                        dve.wait_ge(tapped, DVE_TAPS * m + j - 1)
                        i = nc.vector.scalar_tensor_tensor(out, src, w, out, ALU.mult, ALU.add)
                    i.then_inc(tapped, 1)
                return chains

            def finish(m, q):
                a = conv[:, m, 0:SEQ] if isinstance(m, int) else conv[:, bass.ds(m, 1), 0:SEQ].rearrange("p a t -> p (a t)")
                dve.wait_ge(pe_tapped, m + 1)
                nc.vector.tensor_tensor(a, a, ps_all[:, 4 + q, :], ALU.add).then_inc(joined, 1)
                dve.wait_ge(joined, m + 1)
                dve.wait_ge(tap_added, (POOL_TAPS - 1) * m + shares(m)[1] - 1)
                nc.vector.tensor_tensor(a, a, conv_p[:, q, :], ALU.add).then_inc(conv_done, 1)

            def conv_in(ph):
                nc.vector.memset(glu[:, :, 0:CW - 1], 0.0).then_inc(glu_pad, 1)
                dve.wait_ge(glu_pad, 1)

                def gate(g, q):
                    dve.wait_ge(chunk_used, ph.chunk0 + 4 * g + 2 * q + 1)
                    scaled(t_gate[:, q, :], 0).then_inc(drained, 1)
                    ahead(ph, g, 2 * q)

                def body(g):
                    for q in range(2):
                        n, m, p = ph.chunk0 + 4 * g + 2 * q, 2 * g + q, ph.pair0 + 2 * g + q
                        following = None if isinstance(m, int) and m == KD - 1 else (g + q, 1 - q)
                        dve.wait_ge(chunk_used, n + 2)
                        scaled(t_out[:, q, :], 1).then_inc(drained, 1)
                        dve.wait_ge(drained, ph.unit0 + 4 * g + 2 * q + 2)
                        dve.wait_ge(act_done, p + 1)
                        nc.vector.scalar_tensor_tensor(glu[:, q, CW - 1:CW - 1 + T], t_out[:, q, :], col("b_in", m), t_act[:, q, :],
                                                       ALU.add, ALU.mult).then_inc(glu_done, 1)
                        ahead(ph, g, 2 * q + 1)
                        dve.wait_ge(glu_done, m + 1)
                        a, b = taps(m, q, lambda: following and gate(*following))
                        nc.vector.tensor_copy(at(tail, m), glu[:, q, SEQ:CW - 1 + T])
                        win = window[:, m] if isinstance(m, int) else window[:, bass.ds(m, 1)].rearrange("p a j b -> p (a j) b")
                        nc.vector.tensor_copy(win[:, CW - 1, :], glu[:, q, CW - 1 + SEQ:CW - 1 + T]).then_inc(win_done, 2)
                        dve.wait_ge(win_done, 4 * m + 2)
                        w = vec[:, VEC["dw"] + m:VEC["dw"] + m + KD * (CW - 1) + 1:KD] if isinstance(m, int) else \
                            vec[:, bass.ds(VEC["dw"] + m, CW, KD)]
                        nc.vector.tensor_tensor(swin[:, :, :], win, w.unsqueeze(2).broadcast_to([P, CW, NS]), ALU.mult
                                                ).then_inc(win_done, 1)
                        dve.wait_ge(tapped, DVE_TAPS * m + shares(m)[0])
                        dve.wait_ge(win_done, 4 * m + 3)
                        nc.vector.tensor_tensor(a, a, b, ALU.add)
                        cs = conv[:, m, SEQ:T] if isinstance(m, int) else conv[:, bass.ds(m, 1), SEQ:T].rearrange("p a t -> p (a t)")
                        nc.vector.tensor_reduce(cs, swin[:, :, :].rearrange("p j b -> p b j"), AX.X, ALU.add).then_inc(win_done, 1)
                        dve.wait_ge(win_done, 4 * m + 4)
                        nc.vector.tensor_scalar(cs, cs, col("dw_b", m), None, ALU.add)
                        if not (isinstance(m, int) and m == 0):
                            finish(m - 1, 1 - q)
                dve.wait_ge(in_state, 16)
                gate(0, 0)
                groups(dve, ph, body, first=True, last=True)
                finish(KD - 1, (KD - 1) % 2)
                dve.wait_ge(mean_done, 1)
                for m in range(KD):
                    cm = halves(conv[:, m, :])
                    nc.vector.tensor_tensor(cm, cm, ps_rot, ALU.subtract).then_inc(centred, 1)
                dve.wait_ge(sq_used, KD)
                nc.vector.tensor_copy(halves(acc[:, :]), ps_stat).then_inc(acc_copied, 1)
                rms(ps_all[:, 6, 0:6])

                def lo(m):
                    dve.wait_ge(h_hi_made, ph.h0 + m + 1)
                    nc.vector.tensor_tensor(h_lo[:, MIX + m, :], t_act[:, m % 2, :], h_hi[:, MIX + m, :], ALU.subtract
                                            ).then_inc(h_ready, 1)
                for m in range(KD):
                    nc.vector.tensor_tensor(t_gate[:, m % 2, :], conv[:, m, :], rstd[:, :], ALU.mult).then_inc(ln_scaled, 1)
                    if m:
                        lo(m - 1)
                lo(KD - 1)

            def rotary(ph):
                r0 = 0 if ph.kind == "k" else KD
                cs = cs_k if ph.kind == "k" else cs_q

                def sine(r):
                    dve.wait_ge(rot_done, r + 1)
                    nc.vector.tensor_tensor(halves(t_out[:, r % 2, :]), ps_rot, halves(cs[:, 1, :]), ALU.mult
                                            ).then_inc(sin_done, 1)
                for g in range(ph.groups):
                    for c in range(4):
                        r = r0 + 4 * g + c
                        dve.wait_ge(chunk_used, ph.chunk0 + 4 * g + c + 1)
                        if r >= 2:
                            dve.wait_ge(rope_done, r - 1)
                        scaled(t_gate[:, r % 2, :], c % 2).then_inc(drained, 1)
                        ahead(ph, g, c)
                        if r == r0:
                            dve.wait_ge(in_rope[ph.kind == "q"], 16)
                        else:
                            sine(r - 1)
                sine(r0 + KD - 1)

            def v(ph):
                for g in range(ph.groups):
                    for c in range(4):
                        m = 4 * g + c
                        dve.wait_ge(chunk_used, ph.chunk0 + m + 1)
                        if m < 2:
                            dve.wait_ge(rope_done, KD - 1 + m)
                        else:
                            dve.wait_ge(v_turned, m - 1)
                            dve.wait_ge(vs_copied, m - 1)
                        scaled(t_gate[:, m % 2, :], m % 2).then_inc(drained, 1)
                        ahead(ph, g, c)
                for m in range(KD):
                    x_lo(4, m)
                dve.wait_ge(v_turned, KD)
                dve.wait_ge(vs_copied, KD)

            def attention():
                def maxima(s):
                    keys = (s % 4 + 1) * P
                    dve.wait_ge(scores_done, s + 1)
                    link(nc.vector.tensor_reduce(mx[:, s % 2, :], ps_all[:, 2 * (s % 2):2 * (s % 2) + 2, 0:keys], AX.X, ALU.max))
                    nc.vector.tensor_scalar(nmx[:, s % 2, :], mx[:, s % 2, :], -SCALE, None, ALU.mult).then_inc(max_done, 1)

                def combine(s):
                    e, keys = s % 2, (s % 4 + 1) * P
                    dve.wait_ge(exp_done, s + 1)
                    link(nc.vector.reciprocal(rl[:, e, :], lsum[:, e, :]))
                    link(nc.vector.tensor_tensor(rl2[:, e:e + 1], rl[:, e, 1:2], neglam[:, :], ALU.mult))
                    link(nc.vector.tensor_scalar(pr[:, e, 1, 0:keys], pr[:, e, 1, 0:keys], rl2[:, e:e + 1], None, ALU.mult))
                    if s >= 2:
                        dve.wait_ge(aT_done, s - 1)
                    nc.vector.scalar_tensor_tensor(at_n[:, e, 0:keys], pr[:, e, 0, 0:keys], rl[:, e, 0:1], pr[:, e, 1, 0:keys],
                                                   ALU.mult, ALU.add).then_inc(a_done, 1)

                def own_scores():
                    nc.vector.memset(z_dec[:, :, :, :], 0.0).then_inc(d_new, 1)
                    dve.wait_ge(d_new, 1)
                    for c in range(2):
                        rows = slice(c * HD, (c + 1) * HD)
                        nc.vector.scalar_tensor_tensor(z_dec[rows, :, :, c].rearrange("p b h -> p h b"), qT[rows, :, SEQ:T], float(D),
                                                       kT[rows, :, SEQ:T], ALU.mult, ALU.mult).then_inc(d_new, 1)

                def sample_maxima():
                    dve.wait_ge(d_scores, 1)
                    nc.vector.tensor_reduce(mx_s[:, 0:1], ps_all[:, 7, 0:PAST + 1], AX.X, ALU.max).then_inc(d_max, 1)
                    dve.wait_ge(d_max, 1)
                    nc.vector.tensor_scalar(mx_s[:, 1:2], mx_s[:, 0:1], -SCALE, None, ALU.mult).then_inc(d_max, 1)

                def sample_weights():
                    dve.wait_ge(d_exp, 1)
                    link(nc.vector.reciprocal(mx_s[:, 3:4], mx_s[:, 2:3]))
                    link(nc.vector.tensor_tensor(mx_s[:, 0:1], mx_s[:, 3:4], pairco[:, :], ALU.mult))
                    nc.vector.tensor_scalar(p_dec[:, :], p_dec[:, :], mx_s[:, 0:1], None, ALU.mult).then_inc(d_weights, 1)

                def take_weights():
                    dve.wait_ge(d_turned, 1)
                    dve.wait_ge(d_cleared, 1)
                    link(nc.vector.tensor_copy(an_dec[:, :, :], ps_all[:, 7, 2 * HD:3 * HD].rearrange("p (b h) -> p b h", b=NS)))
                    nc.vector.tensor_copy(at_dec[:, :, :, 0:HEADS], ps_all[:, 7, 0:2 * HD].rearrange("p (g b h) -> p g b h", g=NPG, b=NS)
                                          ).then_inc(d_turned_read, 1)
                    nc.vector.tensor_tensor(own[:, :].rearrange("p (h b) -> p h b", h=HEADS), an_dec[:, :, :].rearrange("p b h -> p h b"),
                                            v_s[:, :, :], ALU.mult).then_inc(d_out, 1)

                maxima(0)
                maxima(1)
                for s in range(STEPS + 6):
                    if s < STEPS:
                        combine(s)
                    if s + 2 < STEPS:
                        maxima(s + 2)
                    h, t = divmod(s - 6, 4)
                    if t == 0 and 0 <= h < HEADS:
                        dve.wait_ge(o_stat, h + 1)
                        nc.vector.tensor_scalar(var[:, 0:SEQ // P], ps_all[:, 7, 0:SEQ // P], D / P, EPS, ALU.mult, ALU.add).then_inc(o_var, 1)
                    if t == 1 and 0 <= h < HEADS:
                        dve.wait_ge(o_spread, h + 1)
                        nc.vector.tensor_tensor(sq[:, 1, 0:SEQ], ps_all[:, 7, :], acc[:, 0:SEQ], ALU.mult).then_inc(o_normed, 1)
                    h, t = divmod(s - 9, 4)
                    if t == 0 and 0 <= h < HEADS:
                        dve.wait_ge(o_hi_made, h + 1)
                        nc.vector.scalar_tensor_tensor(h_lo[:, MIX + h, 0:SEQ], sq[:, 1, 0:SEQ], sub_g[:, 0:1], h_hi[:, MIX + h, 0:SEQ],
                                                       ALU.mult, ALU.subtract).then_inc(o_lo_made, 1)
                    if s == 4 + NS * NPG:
                        own_scores()
                    if s == SCORES_AT + 1:
                        sample_maxima()
                    if s == SCORES_AT + 2:
                        sample_weights()
                    if s == TURN_AT + 1:
                        take_weights()
                    if 4 <= s < 4 + NS * NPG:
                        b, g = divmod(s - 4, NPG)
                        dve.wait_ge(kprod_done, s - 3)
                        nc.vector.tensor_reduce(s_dec[:, g, b, :], kprod[:, :].rearrange("p (j d) -> p j d", d=HD), AX.X,
                                                ALU.add).then_inc(kred_done, 1)
                dve.wait_ge(v_page_used, NS * NPG)
                nc.vector.tensor_copy(av[:, 0:SEQ], ps_all[0:HD, 2, :]).then_inc(d_av_copied, 1)
                dve.wait_ge(d_av_turned, 1)
                dve.wait_ge(d_out, 1)
                nc.vector.tensor_tensor(dec_o[:, :], ps_all[:, 6, 0:HD], own[:, :], ALU.add).then_inc(d_out, 1)
                dve.wait_ge(d_stat, 1)
                nc.vector.tensor_scalar(var[0:HD, 0:1], ps_all[0:HD, 4, 0:1], D / P, EPS, ALU.mult, ALU.add).then_inc(d_inv, 1)
                dve.wait_ge(d_spread, 1)
                nc.vector.tensor_tensor(dec_n[:, :], ps_all[:, 4, 0:HD], dec_o[:, :], ALU.mult).then_inc(d_normed, 1)
                dve.wait_ge(o_hi_made, HEADS + 1)
                nc.vector.scalar_tensor_tensor(h_lo[:, MIX:KF, SEQ:T], dec_n[:, :].rearrange("p (h b) -> p h b", h=HEADS),
                                               sub_g[:, 0:1], h_hi[:, MIX:KF, SEQ:T], ALU.mult, ALU.subtract).then_inc(o_lo_made, 1)

            for ph in phases:
                if fresh(ph):
                    rms()
                if ph.kind == "up":
                    up(ph)
                    if ph is phases[0]:
                        spread_lambda()
                elif ph.kind == "conv_in":
                    conv_in(ph)
                elif ph.kind in ("k", "q"):
                    rotary(ph)
                    if ph.kind == "q":
                        attention()
                elif ph.kind == "v":
                    v(ph)
                else:
                    residual(ph)
            rms()
            for m in range(KD):
                nc.vector.scalar_tensor_tensor(x[:, m, :], x[:, m, :], col("final", m), rstd[:, :], ALU.mult, ALU.mult
                                               ).then_inc(final_done, 1)

        @block.gpsimd
        def _(pool):
            nc.gpsimd.memset(ones_d[:, :], 1.0 / D).then_inc(const_done, 1)
            nc.gpsimd.memset(minus_half[:, :], -0.5).then_inc(const_done, 1)
            sums, squares = [KD], [KD]

            def add_tile(m, src):
                if m == 0:
                    i = nc.gpsimd.tensor_copy(acc[:, :], src)
                else:
                    pool.wait_ge(summed, sums[0])
                    i = nc.gpsimd.tensor_tensor(acc[:, :], acc[:, :], src, ALU.add)
                i.then_inc(summed, 1)
                sums[0] += 1

            def add_squares():
                for m in range(KD):
                    squares[0] += 1
                    pool.wait_ge(squared, squares[0])
                    add_tile(m, sq[:, m % 2, :])

            def up(ph):
                def body(g):
                    for q in range(2):
                        p = ph.pair0 + 2 * g + q
                        pool.wait_ge(act_done, p + 1)
                        nc.gpsimd.tensor_tensor(t_gate[:, q, :], t_act[:, q, :], rstd[:, :], ALU.mult).then_inc(act_scaled, 1)
                        pool.wait_ge(h_hi_made, ph.h0 + 2 * g + q + 1)
                        nc.gpsimd.tensor_tensor(at(h_lo, 2 * g + q), t_out[:, q, :], at(h_hi, 2 * g + q), ALU.subtract
                                                ).then_inc(h_ready, 1)
                groups(pool, ph, body)

            def load_for(ph):
                if ph.kind in ("conv_in", "k", "q"):
                    pool.wait_ge(chunk_used, ph.chunk0)
                if ph.kind == "conv_in":
                    pool.dma_start(window[:, :, 0:CW - 1, :], stateT).then_inc(in_state, 16)
                elif ph.kind == "k":
                    pool.dma_start(cs_k[:, :, :], rope_d).then_inc(in_rope[0], 16)
                elif ph.kind == "q":
                    pool.dma_start(cs_q[:, :, :], rope_d).then_inc(in_rope[1], 16)
                    pool.wait_ge(kv_out, N_KV_OUT)
                    pool.dma_start(kT[:, :, :], k_d).then_inc(in_kt, 16)

            def conv_in(ph):
                for m in range(KD):
                    if m >= 2:
                        pool.wait_ge(conv_done, m - 1)
                    for i in range(1, shares(m)[1]):
                        pool.wait_ge(tap_made, POOL_TAPS * m + i + 1)
                        if i == 1:
                            s = nc.gpsimd.tensor_tensor(conv_p[:, m % 2, :], tap[:, 0, :], tap[:, 1, :], ALU.add)
                        else:
                            pool.wait_ge(tap_added, (POOL_TAPS - 1) * m + i - 1)
                            s = nc.gpsimd.tensor_tensor(conv_p[:, m % 2, :], conv_p[:, m % 2, :], tap[:, i % 3, :], ALU.add)
                        s.then_inc(tap_added, 1)
                squares[0] += KD
                rms()

            def rotary(ph):
                r0, u0 = (0, K0) if ph.kind == "k" else (KD, Q0)
                cs, out = (cs_k, k_new) if ph.kind == "k" else (cs_q, qT)

                def both(r):
                    pool.wait_ge(sin_done, r + 1)
                    pool.wait_ge(cos_done, r + 1)
                    nc.gpsimd.tensor_tensor(out[:, r - r0, :], t_act[:, r % 2, :], t_out[:, r % 2, :], ALU.add
                                            ).then_inc(rope_done, 1)
                pool.wait_ge(in_rope[ph.kind == "q"], 16)
                for r in range(r0, r0 + KD):
                    pool.wait_ge(drained, u0 + r - r0 + 1)
                    nc.gpsimd.tensor_tensor(t_act[:, r % 2, :], t_gate[:, r % 2, :], cs[:, 0, :], ALU.mult).then_inc(cos_done, 1)
                    if r > r0:
                        both(r - 1)
                both(r0 + KD - 1)

            def attention():
                pool.wait_ge(chunk_used, KIND["o"][0].chunk0)
                pool.dma_start(vT[:, :, :], v_d.rearrange("(t p) f -> p t f", p=P)).then_inc(in_vt, 16)

                def head_power(h):
                    pool.wait_ge(o_var, h + 1)
                    power(SEQ // P).then_inc(o_inv, 1)

                for i in range(NS * NPG):
                    b = i // NPG
                    pool.wait_ge(k_page_full[i % len(K_SLOTS)], 16 * (i // len(K_SLOTS) + 1))
                    if i % NPG == 0:
                        pool.wait_ge(qb_full[b % 2], 16 * (b // 2 + 1))
                    if i:
                        pool.wait_ge(kred_done, i)
                    nc.gpsimd.tensor_tensor(kprod[:, :], K_SLOTS[i % len(K_SLOTS)], qb[:, b % 2, :], ALU.mult
                                            ).then_inc(kprod_done, 1)
                    if i % 4 == 2:
                        head_power(i // 4)
                pool.wait_ge(kred_done, NS * NPG)
                nc.gpsimd.memset(at_dec[:, :, :, :], 0.0).then_inc(d_cleared, 1)
                for h in range(NS * NPG // 4, HEADS):
                    head_power(h)
                pool.wait_ge(d_inv, 1)
                power(1, HD).then_inc(d_inv, 1)

            def power(n, rows=P):
                return nc.gpsimd.tensor_tensor(inv[0:rows, 0:n], var[0:rows, 0:n], minus_half[0:rows, 0:n], ALU.pow)

            made = [0]

            def rms():
                made[0] += 1
                pool.wait_ge(var_read, made[0])
                power(len(BLOCKS)).then_inc(inv_made, 1)

            for ph in phases:
                load_for(ph)
                if fresh(ph):
                    rms()
                if ph.kind == "up":
                    up(ph)
                elif ph.kind == "conv_in":
                    conv_in(ph)
                elif ph.kind in ("k", "q"):
                    rotary(ph)
                    if ph.kind == "q":
                        attention()
                elif ph.kind == "v":
                    for m in range(KD):
                        pool.wait_ge(drained, V0 + m + 1)
                        nc.gpsimd.tensor_copy(v_s[:, m, :], t_gate[:, m % 2, SEQ:T]).then_inc(vs_copied, 1)
                else:
                    add_squares()
            rms()


def kernel(**inputs):
    import concourse.bacc as bacc
    from concourse.bass_utils import run_bass_kernel_spmd

    a = {k: np.ascontiguousarray(v) for k, v in inputs.items()}

    def features(t):
        return np.ascontiguousarray(t.reshape(-1, KD, P).transpose(2, 1, 0))

    f32 = np.float32
    rows = np.concatenate([a[n].reshape(-1, P) for n in (
        "norm_ffn", "norm_mix", "kv_norm", "norm_final", "conv_b_in", "conv_dw", "conv_dw_b", "conv_ln_g", "conv_ln_b",
        "conv_b_out", "subln_g")])
    i = np.arange(P)
    rot = (i[:, None] == (i ^ (HD // 2))[None, :]).astype(f32)
    cst = np.concatenate([np.eye(P, dtype=f32), rot, np.where(i[None, :] > i[:, None], NEG, 0.0).astype(f32),
                          (i[:, None] // 2 == np.arange(HD)[None, :]).astype(f32),
                          (i[:, None] % 2 == 0).astype(f32), (i[:, None] % 2 == 1).astype(f32)], axis=1)
    pos = np.concatenate([np.arange(SEQ), np.full(NS, PAST)]).astype(f32)
    freqs = (f32(10000.0) ** (-np.arange(HD // 2, dtype=f32) * f32(2.0) / f32(HD))).astype(f32)
    ang = freqs[i % (HD // 2)][:, None] * pos[None, :]
    sign = np.where(i % HD < HD // 2, -1.0, 1.0).astype(f32)[:, None]
    rope = np.stack([np.cos(ang), sign * np.sin(ang)], axis=1).astype(f32)

    ins = {
        "xT": features(np.concatenate([a["x_prompt"].reshape(SEQ, D), a["x_sample"].reshape(NS, D)])),
        "vec": np.ascontiguousarray(rows.T),
        "cst": np.ascontiguousarray(cst),
        "rope": np.ascontiguousarray(rope),
        "lam": np.concatenate([a[n] for n in ("lambda_q1", "lambda_k1", "lambda_q2", "lambda_k2")]).reshape(1, 4, HD),
        "stateT": np.ascontiguousarray(a["state_conv"][0].reshape(NS, CW - 1, KD, P).transpose(3, 2, 1, 0)),
        "state": a["state_conv"][0],
        "cache_k": a["cache_k"].reshape(NPOOL, PAGE, D),
        "cache_v": a["cache_v"].reshape(NPOOL, PAGE, D),
        "pages": a["page_table"].reshape(1, NS * NPG),
        "w_in": a["ffn_w_in"], "w_out": a["ffn_w_out"], "c_in": a["conv_w_in"], "c_out": a["conv_w_out"],
        "w_kv": a["w_kv"], "w_q": a["w_q"], "w_o": a["w_o"],
    }
    outs = {"y": (P, KD, T), "conv_tail": (P, KD, CW - 1 + NS), "new_state": (NS, CW - 2, D), "k_new_out": (P, KD, T),
            "v_new_out": (SEQ, D), "v_new_s": (P, KD, NS)}
    nc = bacc.Bacc("TRN2", target_bir_lowering=False, num_devices=1)
    args = [nc.dram_tensor(n, v.shape, mybir.dt.from_np(v.dtype), kind="ExternalInput").ap() for n, v in ins.items()]
    args += [nc.dram_tensor(n, s, F32, kind="ExternalOutput").ap() for n, s in outs.items()]
    trunk(nc, *args)
    r = run_bass_kernel_spmd(nc, [ins], core_ids=[0]).results[0]

    def tokens(t):
        return np.ascontiguousarray(t.transpose(2, 1, 0)).reshape(t.shape[2], -1)

    y, k, v_s, tail = tokens(r["y"]), tokens(r["k_new_out"]), tokens(r["v_new_s"]), tokens(r["conv_tail"])
    heads = (HEADS, 2 * HD)
    new_s = np.concatenate([r["new_state"], tail[CW - 1:].reshape(NS, 1, D)], axis=1)
    return (y[:SEQ].reshape(1, SEQ, D), y[SEQ:].reshape(NS, 1, D), tail[:CW - 1].reshape(1, 1, CW - 1, D),
            k[:SEQ].reshape(1, SEQ, *heads), r["v_new_out"].reshape(1, SEQ, *heads), new_s.reshape(1, NS, CW - 1, D),
            k[SEQ:].reshape(NS, 1, *heads), v_s.reshape(NS, 1, *heads))
```
